# Optimizing a Trainium2 kernel written in Bass

```python
import jax, jax.numpy as jnp
from jax import lax
import numpy as np
import math

D_MODEL = 1024
BATCH = 1
SEQ = 256
DEPTH = 2

MEM_LEN = 256
HEAD_DIM = 64
LRU_WIDTH = 256
LRU_BLOCKS = 4
LRU_BLOCK = LRU_WIDTH // LRU_BLOCKS
CONV_WIDTH = 4
LRU_C = 8.0
FOX_HEADS = 8
FOX_WIDTH = FOX_HEADS * HEAD_DIM
RET_HEADS = 4
RET_WIDTH = RET_HEADS * HEAD_DIM
MIX_WIDTH = LRU_WIDTH + FOX_WIDTH + RET_WIDTH
SPLIT_SIZES = (LRU_WIDTH, LRU_WIDTH, FOX_WIDTH, FOX_WIDTH, FOX_WIDTH, FOX_HEADS, RET_WIDTH, RET_WIDTH, RET_WIDTH, RET_WIDTH)
IN_WIDTH = sum(SPLIT_SIZES)
CROSS_HEADS = 4
CROSS_HEAD_DIM = D_MODEL // CROSS_HEADS
D_FF = ((8 * D_MODEL + 3 * 256 - 1) // (3 * 256)) * 256
Q_BLOCK = 128
RET_CHUNK = 128
ROPE_THETA = 10000.0
EPS = 1e-6


def rms_norm(x, g):
    xf = x.astype(jnp.float32)
    y = xf * lax.rsqrt(jnp.mean(xf * xf, axis=-1, keepdims=True) + EPS)
    return (y * g.astype(jnp.float32)).astype(x.dtype)

def causal_depthwise_conv(x, w, b):
    c = x.shape[-1]
    xp = jnp.pad(x, ((0, 0), (CONV_WIDTH - 1, 0), (0, 0)))
    out = lax.conv_general_dilated(xp, w.astype(x.dtype)[:, None, :], window_strides=(1,), padding='VALID', dimension_numbers=('NWC', 'WIO', 'NWC'), feature_group_count=c)
    return out + b.astype(x.dtype)

def rg_lru(x, w_r, b_r, w_i, b_i, lam):
    bsz, s, _ = x.shape
    xb = x.reshape(bsz, s, LRU_BLOCKS, LRU_BLOCK)
    r = jax.nn.sigmoid((jnp.einsum('bsni,nij->bsnj', xb, w_r).reshape(bsz, s, LRU_WIDTH) + b_r).astype(jnp.float32))
    i = jax.nn.sigmoid((jnp.einsum('bsni,nij->bsnj', xb, w_i).reshape(bsz, s, LRU_WIDTH) + b_i).astype(jnp.float32))
    log_a = -LRU_C * r * jax.nn.softplus(-lam.astype(jnp.float32))
    a = jnp.exp(log_a)
    u = jnp.sqrt(-jnp.expm1(2.0 * log_a)) * (i * x.astype(jnp.float32))

    def combine(left, right):
        a1, b1 = left
        a2, b2 = right
        return a1 * a2, a2 * b1 + b2

    _, h = lax.associative_scan(combine, (a, u), axis=1)
    return h.astype(x.dtype)

def forgetting_attention(q, k, v, f_logit, b_f):
    bsz, s, _ = q.shape
    q = q.reshape(bsz, s, FOX_HEADS, HEAD_DIM).transpose(0, 2, 1, 3)
    k = k.reshape(bsz, s, FOX_HEADS, HEAD_DIM).transpose(0, 2, 1, 3)
    v = v.reshape(bsz, s, FOX_HEADS, HEAD_DIM).transpose(0, 2, 1, 3)
    log_f = jax.nn.log_sigmoid((f_logit + b_f).astype(jnp.float32))
    c = jnp.cumsum(log_f, axis=1).transpose(0, 2, 1)
    key_pos = jnp.arange(s)
    scale = HEAD_DIM ** -0.5

    def block(bi):
        start = bi * Q_BLOCK
        qb = lax.dynamic_slice_in_dim(q, start, Q_BLOCK, axis=2)
        cb = lax.dynamic_slice_in_dim(c, start, Q_BLOCK, axis=2)
        logits = jnp.einsum('bhqd,bhkd->bhqk', qb, k).astype(jnp.float32) * scale + cb[..., None] - c[:, :, None, :]
        q_pos = start + jnp.arange(Q_BLOCK)
        mask = key_pos[None, :] <= q_pos[:, None]
        p = jax.nn.softmax(jnp.where(mask, logits, -jnp.inf), axis=-1)
        return jnp.einsum('bhqk,bhkd->bhqd', p.astype(v.dtype), v)

    out = lax.map(block, jnp.arange(s // Q_BLOCK))
    return out.transpose(1, 0, 3, 2, 4).reshape(bsz, s, FOX_WIDTH)

def rotary(x, positions):
    half = x.shape[-1] // 2
    inv_freq = ROPE_THETA ** (-jnp.arange(half, dtype=jnp.float32) / half)
    ang = positions.astype(jnp.float32)[..., None] * inv_freq
    cos = jnp.cos(ang)[:, :, None, :]
    sin = jnp.sin(ang)[:, :, None, :]
    xf = x.astype(jnp.float32)
    x1, x2 = xf[..., :half], xf[..., half:]
    return jnp.concatenate([x1 * cos - x2 * sin, x1 * sin + x2 * cos], axis=-1)

def retention(q, k, v, g, positions):
    bsz, s, _ = q.shape
    n_chunks = s // RET_CHUNK
    shp = (bsz, n_chunks, RET_CHUNK, RET_HEADS, HEAD_DIM)
    qc = rotary(q.reshape(bsz, s, RET_HEADS, HEAD_DIM), positions).reshape(shp)
    kc = (rotary(k.reshape(bsz, s, RET_HEADS, HEAD_DIM), positions) * HEAD_DIM ** -0.5).reshape(shp)
    vc = v.astype(jnp.float32).reshape(shp)
    log_gamma = jnp.log1p(-jnp.exp2(-5.0 - jnp.arange(RET_HEADS, dtype=jnp.float32)))
    idx = jnp.arange(RET_CHUNK, dtype=jnp.float32)
    diff = idx[:, None] - idx[None, :]
    decay = jnp.where(diff >= 0, jnp.exp(log_gamma[:, None, None] * jnp.maximum(diff, 0.0)), 0.0)
    scores = jnp.einsum('bnihd,bnjhd->bnhij', qc, kc) * decay[None, None]
    y_inner = jnp.einsum('bnhij,bnjhd->bnihd', scores, vc)
    k_w = jnp.exp(log_gamma[None, :] * (RET_CHUNK - 1.0 - idx)[:, None])
    u = jnp.einsum('bnjhd,bnjhe,jh->bnhde', kc, vc, k_w)
    chunk_decay = jnp.exp(log_gamma * RET_CHUNK)[None, :, None, None]

    def step(state, u_n):
        return chunk_decay * state + u_n, state

    init = jnp.zeros((bsz, RET_HEADS, HEAD_DIM, HEAD_DIM), jnp.float32)
    _, prev_states = lax.scan(step, init, u.transpose(1, 0, 2, 3, 4))
    q_w = jnp.exp(log_gamma[None, :] * (idx + 1.0)[:, None])
    y_cross = jnp.einsum('bnihd,nbhde,ih->bnihe', qc, prev_states, q_w)
    y = (y_inner + y_cross).reshape(bsz, s, RET_HEADS, HEAD_DIM)
    mu = jnp.mean(y, axis=-1, keepdims=True)
    var = jnp.mean(jnp.square(y - mu), axis=-1, keepdims=True)
    y = ((y - mu) * lax.rsqrt(var + EPS)).reshape(bsz, s, RET_WIDTH)
    return (jax.nn.silu(g.astype(jnp.float32)) * y).astype(g.dtype)

def parallel_mixer(h, positions, w_in, conv_w, conv_b, w_rg, b_rg, w_ig, b_ig, lru_lambda, fox_b_f, w_out):
    proj = h @ w_in
    lx, ly, fq, fk, fv, ff, rq, rk, rv, rg = jnp.split(proj, np.cumsum(SPLIT_SIZES)[:-1].tolist(), axis=-1)
    lru_out = rg_lru(causal_depthwise_conv(lx, conv_w, conv_b), w_rg, b_rg, w_ig, b_ig, lru_lambda) * jax.nn.gelu(ly)
    fox_out = forgetting_attention(fq, fk, fv, ff, fox_b_f)
    ret_out = retention(rq, rk, rv, rg, positions)
    return jnp.concatenate([lru_out, fox_out.astype(h.dtype), ret_out], axis=-1) @ w_out

def memory_cross_attention(h, mem_n, w_q, w_k, w_v, w_o):
    bsz, s, _ = h.shape
    m = mem_n.shape[1]
    q = (h @ w_q).reshape(bsz, s, CROSS_HEADS, CROSS_HEAD_DIM)
    k = (mem_n @ w_k).reshape(bsz, m, CROSS_HEADS, CROSS_HEAD_DIM)
    v = (mem_n @ w_v).reshape(bsz, m, CROSS_HEADS, CROSS_HEAD_DIM)
    logits = jnp.einsum('bshd,bmhd->bhsm', q, k).astype(jnp.float32) * CROSS_HEAD_DIM ** -0.5
    p = jax.nn.softmax(logits, axis=-1)
    o = jnp.einsum('bhsm,bmhd->bshd', p.astype(v.dtype), v).reshape(bsz, s, D_MODEL)
    return o @ w_o

def swiglu(h, w_gate, w_up, w_down):
    return (jax.nn.silu(h @ w_gate) * (h @ w_up)) @ w_down

def first_inputs(seed: int = 0) -> dict:
    key = jax.random.key(seed)
    ks = jax.random.split(key, 32)

    def nrm(k, shape, scale):
        return scale * jax.random.normal(k, shape, jnp.float32)

    def gain(k, shape):
        return 1.0 + 0.02 * jax.random.normal(k, shape, jnp.float32)

    u = jax.random.uniform(ks[12], (DEPTH, LRU_WIDTH), jnp.float32, 0.9, 0.999)
    a_base = u ** (1.0 / LRU_C)
    lru_lambda = jnp.log(a_base) - jnp.log1p(-a_base)
    return {
        'x': nrm(ks[0], (BATCH, SEQ, D_MODEL), 1.0),
        'mem': nrm(ks[1], (BATCH, MEM_LEN, D_MODEL), 1.0),
        'positions': jnp.tile(jnp.arange(SEQ, dtype=jnp.int32)[None, :], (BATCH, 1)),
        'pre_mix_g': gain(ks[2], (DEPTH, D_MODEL)),
        'post_mix_g': gain(ks[3], (DEPTH, D_MODEL)),
        'w_in': nrm(ks[4], (DEPTH, D_MODEL, IN_WIDTH), D_MODEL ** -0.5),
        'conv_w': nrm(ks[5], (DEPTH, CONV_WIDTH, LRU_WIDTH), CONV_WIDTH ** -0.5),
        'conv_b': nrm(ks[6], (DEPTH, LRU_WIDTH), 0.01),
        'w_rg': nrm(ks[7], (DEPTH, LRU_BLOCKS, LRU_BLOCK, LRU_BLOCK), LRU_BLOCK ** -0.5),
        'b_rg': nrm(ks[8], (DEPTH, LRU_WIDTH), 0.01),
        'w_ig': nrm(ks[9], (DEPTH, LRU_BLOCKS, LRU_BLOCK, LRU_BLOCK), LRU_BLOCK ** -0.5),
        'b_ig': nrm(ks[10], (DEPTH, LRU_WIDTH), 0.01),
        'lru_lambda': lru_lambda,
        'fox_b_f': 2.0 + nrm(ks[11], (DEPTH, FOX_HEADS), 0.5),
        'w_out': nrm(ks[13], (DEPTH, MIX_WIDTH, D_MODEL), MIX_WIDTH ** -0.5),
        'pre_cross_g': gain(ks[14], (DEPTH, D_MODEL)),
        'post_cross_g': gain(ks[15], (DEPTH, D_MODEL)),
        'mem_norm_g': gain(ks[16], (D_MODEL,)),
        'w_cq': nrm(ks[17], (DEPTH, D_MODEL, D_MODEL), D_MODEL ** -0.5),
        'w_ck': nrm(ks[18], (DEPTH, D_MODEL, D_MODEL), D_MODEL ** -0.5),
        'w_cv': nrm(ks[19], (DEPTH, D_MODEL, D_MODEL), D_MODEL ** -0.5),
        'w_co': nrm(ks[20], (DEPTH, D_MODEL, D_MODEL), D_MODEL ** -0.5),
        'pre_ffn_g': gain(ks[21], (DEPTH, D_MODEL)),
        'post_ffn_g': gain(ks[22], (DEPTH, D_MODEL)),
        'w_gate': nrm(ks[23], (DEPTH, D_MODEL, D_FF), D_MODEL ** -0.5),
        'w_up': nrm(ks[24], (DEPTH, D_MODEL, D_FF), D_MODEL ** -0.5),
        'w_down': nrm(ks[25], (DEPTH, D_FF, D_MODEL), D_FF ** -0.5),
    }

def first_block(x, mem, positions, pre_mix_g, post_mix_g, w_in, conv_w, conv_b, w_rg, b_rg, w_ig, b_ig, lru_lambda, fox_b_f, w_out, pre_cross_g, post_cross_g, mem_norm_g, w_cq, w_ck, w_cv, w_co, pre_ffn_g, post_ffn_g, w_gate, w_up, w_down):
    mem_n = rms_norm(mem, mem_norm_g)
    for l in range(DEPTH):
        h = rms_norm(x, pre_mix_g[l])
        mix = parallel_mixer(h, positions, w_in[l], conv_w[l], conv_b[l], w_rg[l], b_rg[l], w_ig[l], b_ig[l], lru_lambda[l], fox_b_f[l], w_out[l])
        x = x + rms_norm(mix, post_mix_g[l])
        h = rms_norm(x, pre_cross_g[l])
        x = x + rms_norm(memory_cross_attention(h, mem_n, w_cq[l], w_ck[l], w_cv[l], w_co[l]), post_cross_g[l])
        h = rms_norm(x, pre_ffn_g[l])
        x = x + rms_norm(swiglu(h, w_gate[l], w_up[l], w_down[l]), post_ffn_g[l])
    return x


NSA_HEADS = 8
NSA_KV_HEADS = 2
CMP_LEN = 32
CMP_STRIDE = 16
CMP_HIDDEN = 256
SLC_LEN = 64
SLC_TOPN = 16
NSA_WINDOW = 512
FORCE_SCORE = 1e4
SB_HEADS = 4
SWA_HEADS = 4
SWA_KV_HEADS = 2
SWA_WINDOW = 128
NUM_BUCKETS = 32
MAX_DISTANCE = 128
N_BIAS_HEADS = NSA_HEADS + SWA_HEADS
D_FF_2 = 2816
NORM_EPS = 1e-6
NEG_INF = -1e30
N_BRANCHES = 3

SPLIT_SIZES_2 = (
    NSA_HEADS * HEAD_DIM,
    NSA_KV_HEADS * HEAD_DIM, NSA_KV_HEADS * HEAD_DIM,
    NSA_KV_HEADS * HEAD_DIM, NSA_KV_HEADS * HEAD_DIM,
    NSA_KV_HEADS * HEAD_DIM, NSA_KV_HEADS * HEAD_DIM,
    3 * NSA_HEADS,
    SB_HEADS * HEAD_DIM, SB_HEADS * HEAD_DIM, SB_HEADS * HEAD_DIM,
    SWA_HEADS * HEAD_DIM, SWA_KV_HEADS * HEAD_DIM, SWA_KV_HEADS * HEAD_DIM,
    N_BRANCHES * D_MODEL,
)
D_IN = sum(SPLIT_SIZES_2)
SPLIT_POINTS = tuple(int(p) for p in np.cumsum(SPLIT_SIZES_2)[:-1])


def rms_norm_2(x, w):
    xf = x.astype(jnp.float32)
    y = xf * lax.rsqrt(jnp.mean(xf * xf, axis=-1, keepdims=True) + NORM_EPS)
    return (y * w.astype(jnp.float32)).astype(x.dtype)

def swiglu_2(x, w_gate, w_up, w_down):
    return (jax.nn.silu(x @ w_gate) * (x @ w_up)) @ w_down

def t5_bucket(dist):
    max_exact = NUM_BUCKETS // 2
    d = jnp.maximum(dist, 0)
    df = jnp.maximum(d, 1).astype(jnp.float32)
    large = max_exact + (jnp.log(df / max_exact) / math.log(MAX_DISTANCE / max_exact)
                         * (NUM_BUCKETS - max_exact)).astype(jnp.int32)
    large = jnp.minimum(large, NUM_BUCKETS - 1)
    return jnp.where(d < max_exact, d, large)

def masked_softmax(logits, mask):
    p = jax.nn.softmax(jnp.where(mask, logits, NEG_INF), axis=-1)
    return p * mask

def nsa_attention(q, k_cmp, v_cmp, k_slc, v_slc, k_win, v_win, gate_logits,
                  q_norm, k_norm, cmp_pos, cmp_k_w1, cmp_k_w2, cmp_v_w1, cmp_v_w2, bias_table):
    B, S = q.shape[0], q.shape[1]
    G, R, Dh = NSA_KV_HEADS, NSA_HEADS // NSA_KV_HEADS, HEAD_DIM
    scale = Dh ** -0.5
    qg = rms_norm_2(q, q_norm).reshape(B, S, G, R, Dh).transpose(0, 2, 3, 1, 4)
    gates = jax.nn.sigmoid(gate_logits.astype(jnp.float32)).reshape(B, S, 3, G, R)

    n_cmp = (S - CMP_LEN) // CMP_STRIDE + 1
    cmp_idx = np.arange(n_cmp)[:, None] * CMP_STRIDE + np.arange(CMP_LEN)[None, :]
    cmp_end = jnp.asarray(cmp_idx[:, -1], jnp.int32)

    def compress(t, w1, w2):
        blocks = t[:, cmp_idx] + cmp_pos[:, None, :]
        blocks = blocks.transpose(0, 3, 1, 2, 4).reshape(B, G, n_cmp, CMP_LEN * Dh)
        return jax.nn.silu(blocks @ w1) @ w2

    kc = rms_norm_2(compress(k_cmp, cmp_k_w1, cmp_k_w2), k_norm)
    vc = compress(v_cmp, cmp_v_w1, cmp_v_w2)

    n_slc = S // SLC_LEN
    slc_start = np.arange(n_slc) * SLC_LEN
    overlap = jnp.asarray((cmp_idx[:, :1] < slc_start[None, :] + SLC_LEN)
                          & (cmp_idx[:, -1:] >= slc_start[None, :]), jnp.float32)
    top_n = min(SLC_TOPN, n_slc)
    ks = rms_norm_2(k_slc, k_norm).transpose(0, 2, 1, 3).reshape(B, G, n_slc, SLC_LEN, Dh)
    vs = v_slc.transpose(0, 2, 1, 3).reshape(B, G, n_slc, SLC_LEN, Dh)

    pad = ((0, 0), (0, 0), (NSA_WINDOW, 0), (0, 0))
    kw = jnp.pad(rms_norm_2(k_win, k_norm).transpose(0, 2, 1, 3), pad)
    vw = jnp.pad(v_win.transpose(0, 2, 1, 3), pad)

    head_bias = bias_table[:, :NSA_HEADS].T.reshape(G, R, NUM_BUCKETS).astype(jnp.float32)
    b_idx = jnp.arange(B)[:, None, None, None]
    g_idx = jnp.arange(G)[None, :, None, None]
    g5 = jnp.arange(G)[None, :, None, None, None]
    r5 = jnp.arange(R)[None, None, :, None, None]
    slc_ids = jnp.arange(n_slc)[None, :]

    def block(i):
        q0 = i * Q_BLOCK
        t = q0 + jnp.arange(Q_BLOCK)
        qb = lax.dynamic_slice_in_dim(qg, q0, Q_BLOCK, axis=3)

        dist_c = t[:, None] - cmp_end[None, :]
        s_c = (jnp.einsum('bgrqd,bgnd->bgrqn', qb, kc).astype(jnp.float32) * scale
               + head_bias[:, :, t5_bucket(dist_c)])
        p_c = masked_softmax(s_c, dist_c >= 0)
        o_c = jnp.einsum('bgrqn,bgnd->bgrqd', p_c.astype(vc.dtype), vc)

        imp = jnp.einsum('bgrqn,nj->bgqj', p_c, overlap)
        cur = (t // SLC_LEN)[:, None]
        forced = (slc_ids == 0) | (slc_ids == cur) | (slc_ids == cur - 1)
        score = jnp.where(forced, FORCE_SCORE, jnp.where(slc_ids <= cur, imp, -1.0))
        _, sel = lax.top_k(score, top_n)
        kg = ks[b_idx, g_idx, sel].reshape(B, G, Q_BLOCK, top_n * SLC_LEN, Dh)
        vg = vs[b_idx, g_idx, sel].reshape(B, G, Q_BLOCK, top_n * SLC_LEN, Dh)
        pos = (sel[..., None] * SLC_LEN + jnp.arange(SLC_LEN)).reshape(B, G, Q_BLOCK, top_n * SLC_LEN)
        dist_s = t[None, None, :, None] - pos
        s_s = (jnp.einsum('bgrqd,bgqkd->bgrqk', qb, kg).astype(jnp.float32) * scale
               + head_bias[g5, r5, t5_bucket(dist_s)[:, :, None]])
        p_s = masked_softmax(s_s, (dist_s >= 0)[:, :, None])
        o_s = jnp.einsum('bgrqk,bgqkd->bgrqd', p_s.astype(vg.dtype), vg)

        kb = lax.dynamic_slice_in_dim(kw, q0, Q_BLOCK + NSA_WINDOW, axis=2)
        vb = lax.dynamic_slice_in_dim(vw, q0, Q_BLOCK + NSA_WINDOW, axis=2)
        key_pos = q0 - NSA_WINDOW + jnp.arange(Q_BLOCK + NSA_WINDOW)
        dist_w = t[:, None] - key_pos[None, :]
        mask_w = (dist_w >= 0) & (dist_w < NSA_WINDOW) & (key_pos[None, :] >= 0)
        s_w = (jnp.einsum('bgrqd,bgkd->bgrqk', qb, kb).astype(jnp.float32) * scale
               + head_bias[:, :, t5_bucket(dist_w)])
        p_w = masked_softmax(s_w, mask_w)
        o_w = jnp.einsum('bgrqk,bgkd->bgrqd', p_w.astype(vb.dtype), vb)

        g = lax.dynamic_slice_in_dim(gates, q0, Q_BLOCK, axis=1).transpose(2, 0, 3, 4, 1)[..., None]
        return (g[0] * o_c + g[1] * o_s + g[2] * o_w).astype(q.dtype)

    o = lax.map(block, jnp.arange(S // Q_BLOCK))
    return o.transpose(1, 0, 4, 2, 3, 5).reshape(B, S, NSA_HEADS * Dh)

def stick_breaking_attention(q, k, v):
    B, S = q.shape[0], q.shape[1]
    scale = HEAD_DIM ** -0.5
    qh = q.transpose(0, 2, 1, 3)
    kh = k.transpose(0, 2, 1, 3)
    vh = v.transpose(0, 2, 1, 3)
    key_pos = jnp.arange(S)

    def block(i):
        q0 = i * Q_BLOCK
        t = q0 + jnp.arange(Q_BLOCK)
        qb = lax.dynamic_slice_in_dim(qh, q0, Q_BLOCK, axis=2)
        z = jnp.einsum('bhqd,bhkd->bhqk', qb, kh).astype(jnp.float32) * scale
        mask = key_pos[None, :] < t[:, None]
        log_fail = jnp.where(mask, jax.nn.log_sigmoid(-z), 0.0)
        after = lax.cumsum(log_fail, axis=3, reverse=True) - log_fail
        w = jnp.where(mask, jnp.exp(jax.nn.log_sigmoid(z) + after), 0.0)
        return jnp.einsum('bhqk,bhkd->bhqd', w.astype(vh.dtype), vh)

    o = lax.map(block, jnp.arange(S // Q_BLOCK))
    return o.transpose(1, 0, 3, 2, 4).reshape(B, S, SB_HEADS * HEAD_DIM)

def swa_sink_attention(q, k, v, q_norm, k_norm, sinks, bias_table):
    B, S = q.shape[0], q.shape[1]
    G, R, Dh = SWA_KV_HEADS, SWA_HEADS // SWA_KV_HEADS, HEAD_DIM
    scale = Dh ** -0.5
    qg = rms_norm_2(q, q_norm).reshape(B, S, G, R, Dh).transpose(0, 2, 3, 1, 4)
    pad = ((0, 0), (0, 0), (SWA_WINDOW, 0), (0, 0))
    kp = jnp.pad(rms_norm_2(k, k_norm).transpose(0, 2, 1, 3), pad)
    vp = jnp.pad(v.transpose(0, 2, 1, 3), pad)
    head_bias = bias_table[:, NSA_HEADS:].T.reshape(G, R, NUM_BUCKETS).astype(jnp.float32)
    sink = sinks.astype(jnp.float32).reshape(1, G, R, 1, 1)

    def block(i):
        q0 = i * Q_BLOCK
        t = q0 + jnp.arange(Q_BLOCK)
        qb = lax.dynamic_slice_in_dim(qg, q0, Q_BLOCK, axis=3)
        kb = lax.dynamic_slice_in_dim(kp, q0, Q_BLOCK + SWA_WINDOW, axis=2)
        vb = lax.dynamic_slice_in_dim(vp, q0, Q_BLOCK + SWA_WINDOW, axis=2)
        key_pos = q0 - SWA_WINDOW + jnp.arange(Q_BLOCK + SWA_WINDOW)
        dist = t[:, None] - key_pos[None, :]
        mask = (dist >= 0) & (dist < SWA_WINDOW) & (key_pos[None, :] >= 0)
        s = (jnp.einsum('bgrqd,bgkd->bgrqk', qb, kb).astype(jnp.float32) * scale
             + head_bias[:, :, t5_bucket(dist)])
        s = jnp.where(mask, s, NEG_INF)
        m = jnp.maximum(jnp.max(s, axis=-1, keepdims=True), sink)
        e = jnp.exp(s - m)
        p = e / (jnp.sum(e, axis=-1, keepdims=True) + jnp.exp(sink - m))
        return jnp.einsum('bgrqk,bgkd->bgrqd', p.astype(vb.dtype), vb)

    o = lax.map(block, jnp.arange(S // Q_BLOCK))
    return o.transpose(1, 0, 4, 2, 3, 5).reshape(B, S, SWA_HEADS * Dh)

def second_inputs(seed: int = 0) -> dict:
    key = jax.random.key(seed)
    ks = jax.random.split(key, 32)
    L, D, F = DEPTH, D_MODEL, D_FF_2

    def w(k, shape, fan_in):
        return jax.random.normal(k, shape, jnp.float32) * fan_in ** -0.5

    def gain(k, shape):
        return 1.0 + 0.02 * jax.random.normal(k, shape, jnp.float32)

    return {
        "x": jax.random.normal(ks[0], (BATCH, SEQ, D), jnp.float32),
        "rel_bias": 0.5 * jax.random.normal(ks[1], (NUM_BUCKETS, N_BIAS_HEADS), jnp.float32),
        "ffn1_norm": gain(ks[2], (L, D)),
        "ffn1_w_gate": w(ks[3], (L, D, F), D),
        "ffn1_w_up": w(ks[4], (L, D, F), D),
        "ffn1_w_down": w(ks[5], (L, F, D), F),
        "mix_norm": gain(ks[6], (L, D)),
        "w_in": w(ks[7], (L, D, D_IN), D),
        "nsa_q_norm": gain(ks[8], (L, HEAD_DIM)),
        "nsa_k_norm": gain(ks[9], (L, HEAD_DIM)),
        "nsa_cmp_pos": 0.5 * jax.random.normal(ks[10], (L, CMP_LEN, HEAD_DIM), jnp.float32),
        "nsa_cmp_k_w1": w(ks[11], (L, CMP_LEN * HEAD_DIM, CMP_HIDDEN), CMP_LEN * HEAD_DIM),
        "nsa_cmp_k_w2": w(ks[12], (L, CMP_HIDDEN, HEAD_DIM), CMP_HIDDEN),
        "nsa_cmp_v_w1": w(ks[13], (L, CMP_LEN * HEAD_DIM, CMP_HIDDEN), CMP_LEN * HEAD_DIM),
        "nsa_cmp_v_w2": w(ks[14], (L, CMP_HIDDEN, HEAD_DIM), CMP_HIDDEN),
        "swa_q_norm": gain(ks[15], (L, HEAD_DIM)),
        "swa_k_norm": gain(ks[16], (L, HEAD_DIM)),
        "swa_sinks": jax.random.normal(ks[17], (L, SWA_HEADS), jnp.float32),
        "w_up_nsa": w(ks[18], (L, NSA_HEADS * HEAD_DIM, D), NSA_HEADS * HEAD_DIM),
        "w_up_sb": w(ks[19], (L, SB_HEADS * HEAD_DIM, D), SB_HEADS * HEAD_DIM),
        "w_up_swa": w(ks[20], (L, SWA_HEADS * HEAD_DIM, D), SWA_HEADS * HEAD_DIM),
        "w_out": w(ks[21], (L, D, D), D),
        "ffn2_norm": gain(ks[22], (L, D)),
        "ffn2_w_gate": w(ks[23], (L, D, F), D),
        "ffn2_w_up": w(ks[24], (L, D, F), D),
        "ffn2_w_down": w(ks[25], (L, F, D), F),
    }

def second_block(x, rel_bias, ffn1_norm, ffn1_w_gate, ffn1_w_up, ffn1_w_down, mix_norm, w_in,
              nsa_q_norm, nsa_k_norm, nsa_cmp_pos, nsa_cmp_k_w1, nsa_cmp_k_w2, nsa_cmp_v_w1,
              nsa_cmp_v_w2, swa_q_norm, swa_k_norm, swa_sinks, w_up_nsa, w_up_sb, w_up_swa, w_out,
              ffn2_norm, ffn2_w_gate, ffn2_w_up, ffn2_w_down):
    B, S = x.shape[0], x.shape[1]

    def heads(t, n):
        return t.reshape(B, S, n, HEAD_DIM)

    for l in range(DEPTH):
        h = rms_norm_2(x, ffn1_norm[l])
        x = x + 0.5 * swiglu_2(h, ffn1_w_gate[l], ffn1_w_up[l], ffn1_w_down[l])

        h = rms_norm_2(x, mix_norm[l])
        (nq, nkc, nvc, nks, nvs, nkw, nvw, ngate, sq, sk, sv, wq, wk, wv, bgate) = jnp.split(
            h @ w_in[l], SPLIT_POINTS, axis=-1)
        y_nsa = nsa_attention(heads(nq, NSA_HEADS), heads(nkc, NSA_KV_HEADS), heads(nvc, NSA_KV_HEADS),
                              heads(nks, NSA_KV_HEADS), heads(nvs, NSA_KV_HEADS),
                              heads(nkw, NSA_KV_HEADS), heads(nvw, NSA_KV_HEADS), ngate,
                              nsa_q_norm[l], nsa_k_norm[l], nsa_cmp_pos[l], nsa_cmp_k_w1[l],
                              nsa_cmp_k_w2[l], nsa_cmp_v_w1[l], nsa_cmp_v_w2[l], rel_bias)
        y_sb = stick_breaking_attention(heads(sq, SB_HEADS), heads(sk, SB_HEADS), heads(sv, SB_HEADS))
        y_swa = swa_sink_attention(heads(wq, SWA_HEADS), heads(wk, SWA_KV_HEADS), heads(wv, SWA_KV_HEADS),
                                   swa_q_norm[l], swa_k_norm[l], swa_sinks[l], rel_bias)

        g = jax.nn.sigmoid(bgate.astype(jnp.float32)).reshape(B, S, N_BRANCHES, D_MODEL).astype(x.dtype)
        merged = (g[:, :, 0] * (y_nsa @ w_up_nsa[l]) + g[:, :, 1] * (y_sb @ w_up_sb[l])
                  + g[:, :, 2] * (y_swa @ w_up_swa[l]))
        x = x + merged @ w_out[l]

        h = rms_norm_2(x, ffn2_norm[l])
        x = x + 0.5 * swiglu_2(h, ffn2_w_gate[l], ffn2_w_up[l], ffn2_w_down[l])
    return x


def setup_inputs(seed=0):
    out = dict(first_inputs(seed))
    for name, value in second_inputs(seed + 1).items():
        if name != "x":
            out[name + "_2"] = value
    return out


def reference(
    x, mem, positions, pre_mix_g, post_mix_g, w_in, conv_w, conv_b, w_rg, b_rg, w_ig, b_ig,
    lru_lambda, fox_b_f, w_out, pre_cross_g, post_cross_g, mem_norm_g, w_cq, w_ck, w_cv, w_co,
    pre_ffn_g, post_ffn_g, w_gate, w_up, w_down, rel_bias_2, ffn1_norm_2, ffn1_w_gate_2,
    ffn1_w_up_2, ffn1_w_down_2, mix_norm_2, w_in_2, nsa_q_norm_2, nsa_k_norm_2, nsa_cmp_pos_2,
    nsa_cmp_k_w1_2, nsa_cmp_k_w2_2, nsa_cmp_v_w1_2, nsa_cmp_v_w2_2, swa_q_norm_2, swa_k_norm_2,
    swa_sinks_2, w_up_nsa_2, w_up_sb_2, w_up_swa_2, w_out_2, ffn2_norm_2, ffn2_w_gate_2,
    ffn2_w_up_2, ffn2_w_down_2,
):
    x = first_block(
        x, mem, positions, pre_mix_g, post_mix_g, w_in, conv_w, conv_b, w_rg, b_rg, w_ig, b_ig,
        lru_lambda, fox_b_f, w_out, pre_cross_g, post_cross_g, mem_norm_g, w_cq, w_ck, w_cv,
        w_co, pre_ffn_g, post_ffn_g, w_gate, w_up, w_down,
    )
    return second_block(
        x, rel_bias_2, ffn1_norm_2, ffn1_w_gate_2, ffn1_w_up_2, ffn1_w_down_2, mix_norm_2,
        w_in_2, nsa_q_norm_2, nsa_k_norm_2, nsa_cmp_pos_2, nsa_cmp_k_w1_2, nsa_cmp_k_w2_2,
        nsa_cmp_v_w1_2, nsa_cmp_v_w2_2, swa_q_norm_2, swa_k_norm_2, swa_sinks_2, w_up_nsa_2,
        w_up_sb_2, w_up_swa_2, w_out_2, ffn2_norm_2, ffn2_w_gate_2, ffn2_w_up_2, ffn2_w_down_2,
    )


_drawn_inputs = setup_inputs


def setup_inputs(seed=0):
    import zlib

    import numpy as np

    out = dict(_drawn_inputs(seed))
    spreads = {}
    factors = {'post_mix_g': 2.709,
     'b_rg': 8.0,
     'b_ig': 8.0,
     'pre_cross_g': 3.152,
     'post_cross_g': 2.76,
     'pre_ffn_g': 2.673,
     'post_ffn_g': 3.909,
     'ffn1_norm_2': 8.0,
     'mix_norm_2': 8.0,
     'nsa_q_norm_2': 8.0,
     'nsa_k_norm_2': 8.0,
     'nsa_cmp_k_w1_2': 2.901,
     'nsa_cmp_k_w2_2': 2.865,
     'swa_q_norm_2': 8.0,
     'swa_k_norm_2': 8.0,
     'swa_sinks_2': 42.338,
     'ffn2_norm_2': 8.0}
    for name, (base, spread) in spreads.items():
        noise = np.random.default_rng([zlib.crc32(name.encode()), seed]).standard_normal(out[name].shape)
        drawn = base * np.exp(spread * noise) if base else spread * noise
        out[name] = __import__('jax').numpy.asarray(drawn.astype(out[name].dtype))
    for name, factor in factors.items():
        out[name] = (out[name] * factor).astype(out[name].dtype)
    return out
```

```python
from contextlib import ExitStack, contextmanager

import numpy as np

import concourse.bass as bass
from concourse import mybir

F32 = mybir.dt.float32
F32R = mybir.dt.float32r
I32 = mybir.dt.int32
ACT = mybir.ActivationFunctionType
ALU = mybir.AluOpType
AX = mybir.AxisListType

P = 128
D = 1024
KT = D // P
S = 256
ST = S // P
DEPTH = 2
HD = 64
EPS = 1e-6
FF = 2816
FT = FF // P
BIG = -8e30
LOWEST = -3e38
COLS = 256
SLOT = KT * COLS
N_CMP = (S - 32) // 16 + 1
N_CMP0 = (P - 32) // 16 + 1
VEC = 3 * P

B1_SLOTS = 13 + 4 + 4 + 4 + 4 + 4 + 2 * (FF // COLS) + FT // 2
B2_SLOTS = 2 * (2 * (FF // COLS) + FT // 2) + 10 + 12 + 4 + 4 + 4
N_SLOTS = DEPTH * (B1_SLOTS + B2_SLOTS)


def columns(**widths):
    at, out = 0, {}
    for name, w in widths.items():
        out[name] = slice(at, at + w)
        at += w
    return out, at


SM1, SM1_W = columns(pre_mix=KT, post_mix=KT, pre_cross=KT, post_cross=KT, pre_ffn=KT, post_ffn=KT,
                     conv_w=8, conv_b=2, b_rg=2, b_ig=2, lam=2, fox_b=1, w_rg=256, w_ig=256)
SM2, SM2_W = columns(ffn1=KT, mix=KT, ffn2=KT, nsa_q=1, nsa_k=1, swa_q=1, swa_k=1, sinks=4,
                     cmp_pos=16, w2k=128, w2v=128, w_gate=KT * 24)
CON, CON_W = columns(ident=P, blk=P, tri=P, rot=P, causal=S, strict=P, decay=4 * S, strict_add=P, inv_freq=1,
                     late=1, mem_g=KT)
EARLY, EARLY_W = columns(onehot=VEC, nsel=8 * P)


class Counter:

    def __init__(self, loops, name, step=1):
        self.loops, self.name, self.step = loops, name, step
        self.sem = loops.nc.alloc_semaphore(name)
        self.done = 0
        loops.counters.append(self)

    def did(self, instruction):
        instruction.then_inc(self.sem, self.step)
        self.done += self.step
        return self.at(self.done)

    def at(self, value):
        return Mark(self, value, tuple(self.loops.open))

    def now(self):
        return self.at(self.done)


class Mark:

    def __init__(self, counter, value, loops):
        self.counter, self.value, self.loops = counter, value, loops

    def number(self):
        out = self.value
        for loop in self.loops:
            per = loop.adds(self.counter.name)
            if per:
                out = loop.i * per + out
        return out


class Loop:
    def __init__(self, key, known):
        self.key, self.i = key, None
        self.known = known.setdefault(key, {})
        self.found, self.start, self.kept = {}, {}, {}

    def adds(self, name):
        return self.known.get(name, 0)

    def keep(self, label, mark):
        self.found["keep " + label] = mark.value - self.start[mark.counter.name]
        self.kept[label] = mark.counter

    def last(self, label, counter):
        off = self.known.get("keep " + label, 0)
        return counter.at(self.start[counter.name] + off - self.adds(counter.name))


class Loops:

    def __init__(self, nc, known, final):
        self.nc, self.known, self.final = nc, known, final
        self.counters, self.open, self.engines, self.n = [], [], [], 0

    @contextmanager
    def run(self, rounds, engines=mybir.ALL_ENGINES):
        loop = Loop(self.n, self.known)
        self.n += 1
        for c in self.counters:
            loop.start[c.name] = c.done
        for e in self.engines:
            e.passed.clear()
            e.settle()
        with self.nc.Fori(0, rounds, engines=engines) as i:
            loop.i = i
            self.open.append(loop)
            yield loop
            self.open.pop()
        for e in self.engines:
            e.passed.clear()
        for c in self.counters:
            add = c.done - loop.start.get(c.name, 0)
            loop.found[c.name] = add
            c.done = loop.start.get(c.name, 0) + rounds * add
        if self.final:
            assert loop.found == loop.known, f"loop {loop.key} adds otherwise than counted"
        else:
            loop.known.update(loop.found)


class Engine:

    def __init__(self, loops, eng, name):
        self.eng, self.counter, self.passed = eng, Counter(loops, "steps_" + name), {}
        self.settled = loops.nc.alloc_semaphore("settled_" + name)
        loops.engines.append(self)

    def wait(self, *marks):
        for m in marks:
            if m is None:
                continue
            if isinstance(m, (list, tuple)):
                self.wait(*m)
                continue
            key = (m.counter.name, m.loops)
            if m.value <= self.passed.get(key, 0):
                continue
            self.passed[key] = m.value
            self.eng.wait_ge(m.counter.sem, m.number())

    def did(self, instruction):
        return self.counter.did(instruction)

    def settle(self):
        self.eng.sem_inc(self.settled)

    def now(self):
        return self.counter.now()


def build(nc, A, known, final):
    L = Loops(nc, known, final)
    pe, act, dve, pool = (Engine(L, e, n) for e, n in (
        (nc.tensor, "pe"), (nc.scalar, "act"), (nc.vector, "dve"), (nc.gpsimd, "pool")))
    T, AC, V, G = nc.tensor, nc.scalar, nc.vector, nc.gpsimd

    def sb(name, shape, dt=F32):
        return nc.alloc_sbuf_tensor(name, shape, dt)[tuple(slice(None) for _ in shape)]

    def sb_at(name, shape, dt, offset):
        return nc.alloc_sbuf_tensor_at(name, shape, dt, offset=offset)[tuple(slice(None) for _ in shape)]

    base = (nc.sbuf_base + 31) // 32 * 32
    shared = 13 * 2048 + 24 * 1024 + 16384
    nc.alloc_sbuf_tensor("shared", [P, shared // 4 + 16], F32)
    proj = sb_at("proj", [P, 13, 2, COLS], F32, base)
    gates = sb_at("gates", [P, 24, S], F32, base + 13 * 2048)
    hid_hi = sb_at("hid_hi", [P, FT, S], F32R, base)
    hid_lo = sb_at("hid_lo", [P, FT, S], F32R, base + FT * 1024)
    lru_at = [base + 13 * 2048 + n * 2048 for n in range(8)]
    xc, lru_r, lru_i, lru_a, lru_t, lru_u, lru_h, lru_g = (
        sb_at(f"lru{n}", [P, 2, S], F32, at) for n, at in enumerate(lru_at))
    mem_hi = sb_at("mem_hi", [P, KT, S], F32R, base + 13 * 2048 + 24 * 1024)
    mem_lo = sb_at("mem_lo", [P, KT, S], F32R, base + 13 * 2048 + 24 * 1024 + 8192)
    table = sb_at("table", [P, 12, S], F32, base + 13 * 2048 + 24 * 1024)

    raw = [sb(f"raw{r}", [P, KT, COLS]) for r in range(2)]
    w_hi = [sb(f"w_hi{r}", [P, KT, COLS], F32R) for r in range(2)]
    w_lo = [sb(f"w_lo{r}", [P, KT, COLS], F32R) for r in range(2)]
    x = sb("x", [P, KT, S])
    xn = sb("xn", [P, KT, S])
    xn_hi, xn_lo = sb("xn_hi", [P, KT, S], F32R), sb("xn_lo", [P, KT, S], F32R)
    y_hi, y_lo = sb("y_hi", [P, KT, S], F32R), sb("y_lo", [P, KT, S], F32R)
    sq = sb("sq", [P, KT, S])
    con = sb("con", [P, CON_W])
    ones = sb("ones", [P, P])
    ones_row = sb("ones_row", [8, S])
    small = sb("small", [P, max(SM1_W, SM2_W)])
    root, rinv = sb("root", [P, 2, S]), sb("rinv", [P, 2, S])
    act_t = sb("act_t", [P, 2, S])
    logit = [sb(f"logit{i}", [P, 2, 512]) for i in range(2)]
    probT = [sb(f"probT{i}", [P, 2, 512]) for i in range(2)]
    stat = sb("stat", [P, 8, 32])
    f8 = act_t[0:8]
    tbl34 = sb("tbl34", [34, 12])
    avg = sb("avg", [P, P])
    eps_t = sb("eps_t", [P, 2])
    rows_8 = sb_at("rows_8", [8, 8 * P], F32, base + 45056)
    cos, sin = (sb_at(n, [P, S], F32, base + 45056 + 4096 + at) for n, at in (("cos", 0), ("sin", 1024)))
    onehot = sb_at("onehot", [34, VEC], F32, lru_at[3])
    c_late, c_early = xn, sq.rearrange("p a s -> p (a s)")[:, 0:8 * P].rearrange("p (h s) -> p h s", h=8)

    bank = [nc.alloc_psum_tensor(f"bank{i}", [P, 512], F32)[:, :] for i in range(8)]
    two = lambda b: b.rearrange("p (a s) -> p a s", a=2)
    dense = [two(bank[0]), two(bank[1])]
    acc = [two(bank[i]) for i in range(2, 6)]
    misc = [two(bank[6]), two(bank[7])]

    def c(name):
        return con[:, CON[name]]

    loaded = [Counter(L, f"loaded{r}", 16) for r in range(2)]
    used = Counter(L, "slots_used")
    hi_done, lo_done = Counter(L, "slots_hi"), Counter(L, "slots_lo")
    stream = A["stream"]

    def load(n, r):
        nc.sync.dma_start(raw[r], stream[bass.ds(n, 1)].rearrange("o p (k c) -> (o p) k c", k=KT)
                          ).then_inc(loaded[r].sem, 16)

    load(0, 0)
    load(1, 1)
    with nc.Fori(1, N_SLOTS // 2, engines=[mybir.EngineType.SP]) as i:
        for r in range(2):
            nc.sync.wait_ge(lo_done.sem, i * 2 + (r - 1))
            load(i * 2 + r, r)

    def split():
        m = hi_done.done
        r = m % 2
        loaded[r].done += 16
        free = used.at(m - 1) if m >= 2 else None
        act.wait(loaded[r].now(), free)
        hi = hi_done.did(AC.activation(w_hi[r], raw[r], ACT.Copy))
        dve.wait(loaded[r].now(), hi, free)
        lo_done.did(V.tensor_tensor(w_lo[r], raw[r], w_hi[r].bitcast(F32), ALU.subtract))

    def take(ahead=True):
        n = used.done
        if hi_done.done == n:
            split()
        if ahead:
            split()
        pe.wait(hi_done.at(n + 1), lo_done.at(n + 1))
        return n % 2

    def products(out, lhs, rhs, first, last, **kw):
        trio = [(lhs[0], rhs[0]), (lhs[0], rhs[1]), (lhs[1], rhs[0])]
        for j, (a, b) in enumerate(trio):
            m = T.matmul(out, a, b, start=first and j == 0, stop=last and j == 2, **kw)
        return m

    def columns_T(out, ct, r, hi, lo, kts=range(KT)):
        for n, k in enumerate(kts):
            w = [t[r][:, k, ct * P:(ct + 1) * P] for t in (w_hi, w_lo)]
            m = products(out, w, [hi[:, k, :], lo[:, k, :]], n == 0, n == len(kts) - 1)
        return m

    def rows(out, rt, r, hi, lo, cols=slice(0, COLS)):
        for k in range(KT):
            a = [t[:, k, rt * P:(rt + 1) * P] for t in (hi, lo)]
            m = products(out, a, [w_hi[r][:, k, cols], w_lo[r][:, k, cols]], k == 0, k == KT - 1)
        return m

    def slot_T(out, hi, lo, ahead=True):
        r = take(ahead)
        for ct in range(2):
            m = columns_T(out[:, ct, :], ct, r, hi, lo)
        return used.did(m)

    def slot_rows(out, hi, lo, ahead=True):
        r = take(ahead)
        for rt in range(ST):
            m = rows(out[:, rt, :], rt, r, hi, lo)
        return used.did(m)

    got_con, got_x, got_small = Counter(L, "got_con", 16), Counter(L, "got_x", 16), Counter(L, "got_small", 16)
    got_con.did(G.dma_start(rows_8, A["early"][0:8, EARLY["nsel"]]))
    got_con.did(G.dma_start(onehot, A["early"][0:34, EARLY["onehot"]]))
    con_in = got_con.did(G.dma_start(con, A["con"]))
    x_in = got_x.did(G.dma_start(x, A["x"]))
    got_mem = Counter(L, "got_mem", 16)
    mem_in = got_mem.did(G.dma_start(xn, A["mem"]))
    got_pos = Counter(L, "got_pos", 16)
    pos_raw = stat.rearrange("p a b -> p (a b)").bitcast(I32)
    pos_in = got_pos.did(G.dma_start(pos_raw, A["positions"]))
    got_bias = Counter(L, "got_bias", 16)
    bias_in = got_bias.did(G.dma_start(tbl34, A["rel_bias"]))
    ones_set = pool.did(G.memset(ones, 1.0))
    avg_set = pool.did(G.memset(avg, 1.0 / D))
    row_set = pool.did(G.memset(ones_row, 1.0))

    bcast = sb_at("bcast", [34, 12, P], F32, lru_at[0])
    dve.wait(bias_in, ones_set)
    for h in range(12):
        m = dve.did(V.tensor_scalar(bcast[:, h, :], ones[0:34, :], tbl34[:, h:h + 1], 8.0, ALU.mult, ALU.mult))
    pe.wait(con_in, m)
    wrote_vec = Counter(L, "wrote_vec", 16)
    vec_sb = sb_at("vec_sb", [P, 12, VEC], F32, base)
    vec_out = {}
    for h in range(12):
        pe.wait(vec_out.get(h - 2))
        m = pe.did(T.matmul(bank[h % 2][:, 0:VEC], bcast[:, h, :], onehot, start=True, stop=True))
        dve.wait(m)
        vec_out[h] = dve.did(V.tensor_copy(vec_sb[:, h, :], bank[h % 2][:, 0:VEC]))
    pool.wait(vec_out[11])
    skew_out = wrote_vec.did(G.dma_start(A["skew"].rearrange("(p h v) -> p h v", h=12, v=VEC), vec_sb))

    def mean_square(src_of, n_src, out, after, also=None):
        sums = None
        for b in range(n_src):
            act.wait(after[b])
            s = act.did(AC.activation(sq[:, 2 * b:2 * b + 2, :], src_of(b), ACT.Square))
            pe.wait(s)
            for k in (2 * b, 2 * b + 1):
                sums = T.matmul(out, avg, sq[:, k, :], start=k == 0, stop=k == KT - 1)
        return pe.did(sums)

    def inverse_root(src, w, ready):
        act.wait(ready)
        m = act.did(AC.activation(root_f[:, 0:w], src, ACT.Sqrt, bias=eps))
        dve.wait(m)
        return dve.did(V.reciprocal(rinv_f[:, 0:w], root_f[:, 0:w]))

    root_f = root.rearrange("p a s -> p (a s)")
    rinv_f = rinv.rearrange("p a s -> p (a s)")
    pool.did(G.memset(eps_t[:, 0:1], EPS))
    eps_set = pool.did(G.memset(eps_t[:, 1:2], 1.0))
    eps, one = eps_t[:, 0:1], eps_t[:, 1:2]

    def norm_in(src, gain, hi, lo, src_ready, free):
        ms = mean_square(lambda b: src[:, 2 * b:2 * b + 2, :], 4, misc[0][:, 0, :], [src_ready] * 4)
        r = inverse_root(misc[0][:, 0, :], S, ms)
        dve.wait(free, r)
        act.wait(free)
        marks = []
        for b in range(4):
            for k in (2 * b, 2 * b + 1):
                n = dve.did(V.scalar_tensor_tensor(xn[:, k, :], src[:, k, :], gain[:, k:k + 1], rinv[:, 0, :],
                                                   ALU.mult, ALU.mult))
            pair = slice(2 * b, 2 * b + 2)
            act.wait(n)
            h = act.did(AC.activation(hi[:, pair, :], xn[:, pair, :], ACT.Copy))
            dve.wait(h)
            marks.append(dve.did(V.tensor_tensor(lo[:, pair, :], xn[:, pair, :], hi[:, pair, :].bitcast(F32),
                                                 ALU.subtract)))
        return marks[-1]

    def norm_add(gain, ready):
        ms = mean_square(lambda b: acc[b], 4, misc[0][:, 0, :], ready)
        r = inverse_root(misc[0][:, 0, :], S, ms)
        dve.wait(r)
        for k in range(KT):
            n = dve.did(V.scalar_tensor_tensor(sq[:, k, :], acc[k // 2][:, k % 2, :], gain[:, k:k + 1],
                                               rinv[:, 0, :], ALU.mult, ALU.mult))
        dve.wait(n)
        return dve.did(V.tensor_tensor(x, x, sq, ALU.add))

    def split_out(hi, lo, psum, ready):
        act.wait(ready)
        h = act.did(AC.activation(hi, psum, ACT.Copy))
        dve.wait(h)
        return dve.did(V.tensor_tensor(lo, psum, hi.bitcast(F32), ALU.subtract))

    def ffn(hi, lo, ready, last_ahead):
        pe.wait(ready)
        act.wait(pe.now(), dve.now(), act.now())
        dve.wait(pe.now(), act.now())
        pe.wait(act.now(), dve.now())
        with L.run(FF // COLS) as loop:
            j = loop.i
            pe.wait(loop.last("silu", act.counter))
            up_free = loop.last("up", dve.counter)
            gate = slot_T(dense[0], hi, lo)
            act.wait(gate, up_free)
            silu = act.did(AC.activation(act_t, dense[0], ACT.Silu))
            loop.keep("silu", silu)
            pe.wait(up_free)
            up = slot_T(dense[1], hi, lo)
            dve.wait(up, silu)
            h = dve.did(V.tensor_tensor(act_t, act_t, dense[1], ALU.mult))
            act.wait(h)
            hh = act.did(AC.activation(hid_hi[:, bass.ds(j * 2, 2), :], act_t, ACT.Copy))
            dve.wait(hh)
            low = dve.did(V.tensor_tensor(hid_lo[:, bass.ds(j * 2, 2), :], act_t,
                                          hid_hi[:, bass.ds(j * 2, 2), :].bitcast(F32), ALU.subtract))
            loop.keep("up", low)
        pe.wait(dve.now(), act.now())

        def down(j, start, ahead=True):
            r = take(ahead)
            for k in range(2):
                for ct in range(KT):
                    blk = k * KT + ct
                    w = [t[r].rearrange("p k c -> p (k c)")[:, blk * P:(blk + 1) * P] for t in (w_hi, w_lo)]
                    h = [t[:, bass.ds(j * 2 + k, 1), :].rearrange("p o s -> p (o s)") for t in (hid_hi, hid_lo)]
                    m = products(acc[ct // 2][:, ct % 2, :], w, h, start and k == 0 and ct % 2 == 0, True,
                                 skip_group_check=True)
            return used.did(m)

        n = FT // 2
        down(0, True)
        with L.run((n - 3) // 2) as loop:
            down(loop.i * 2 + 1, False)
            down(loop.i * 2 + 2, False)
        down(n - 2, False)
        return [down(n - 1, False, last_ahead)] * 4

    def out_projection(hi, lo, ready, first_free):
        pe.wait(ready, first_free)
        return [slot_T(acc[b], hi, lo) for b in range(4)]

    mem_g = c("mem_g")
    act.wait(mem_in, eps_set, con_in)
    dve.wait(con_in)
    pe.wait(avg_set)
    ms = mean_square(lambda b: xn[:, 2 * b:2 * b + 2, :], 4, misc[0][:, 0, :], [mem_in] * 4)
    r = inverse_root(misc[0][:, 0, :], S, ms)
    dve.wait(r, mem_in)
    for b in range(4):
        for k in (2 * b, 2 * b + 1):
            n = dve.did(V.scalar_tensor_tensor(xn[:, k, :], xn[:, k, :], mem_g[:, k:k + 1], rinv[:, 0, :],
                                               ALU.mult, ALU.mult))
        pair = slice(2 * b, 2 * b + 2)
        act.wait(n)
        h = act.did(AC.activation(mem_hi[:, pair, :], xn[:, pair, :], ACT.Copy))
        dve.wait(h)
        mem_ready = dve.did(V.tensor_tensor(mem_lo[:, pair, :], xn[:, pair, :], mem_hi[:, pair, :].bitcast(F32),
                                            ALU.subtract))

    TWO_PI = 2 * np.pi
    C1 = 6.28125
    C2 = float((np.array([TWO_PI - C1], np.float32).view(np.uint32) & np.uint32(0xfffff000)).view(np.float32)[0])
    C3 = float(TWO_PI - C1 - C2)
    MAGIC = 1.5 * 2.0 ** 23
    posf, ang, turn, red = (logit[1][:, n // 2, (n % 2) * S:(n % 2 + 1) * S] for n in range(4))
    dve.wait(pos_in)
    p0 = dve.did(V.tensor_copy(posf, pos_raw))
    dve.wait(p0)
    p0 = dve.did(V.tensor_scalar(ang, posf, c("inv_freq"), None, ALU.mult))
    dve.wait(p0)
    for out, quarter in ((sin, 0.0), (cos, 0.25)):
        m = dve.did(V.tensor_scalar(turn, ang, 1.0 / TWO_PI, quarter, ALU.mult, ALU.add))
        for k in (MAGIC, -MAGIC):
            dve.wait(m)
            m = dve.did(V.tensor_scalar(turn, turn, k, None, ALU.add))
        dve.wait(m)
        m = dve.did(V.scalar_tensor_tensor(red, turn, -C1, ang, ALU.mult, ALU.add))
        for k in (C2, C3):
            dve.wait(m)
            m = dve.did(V.scalar_tensor_tensor(red, turn, -k, red, ALU.mult, ALU.add))
        dve.wait(m)
        m = dve.did(V.tensor_scalar(red, red, quarter * TWO_PI, float(np.float32(3.1415925)), ALU.add, ALU.min))
        dve.wait(m)
        m = dve.did(V.tensor_scalar(red, red, -float(np.float32(3.1415925)), None, ALU.max))
        act.wait(m)
        trig = act.did(AC.activation(out, red, ACT.Sin))
        dve.wait(trig)


    def causal_values(out, v_of, pT, first=True, last=True):
        T.matmul(out, v_of(0), pT[:, 0:S], start=first, stop=False, skip_group_check=True)
        return T.matmul(out[:, P:S], v_of(1), pT[:, S:S + P], start=False, stop=last, skip_group_check=True)

    def slot_of(t, n):
        return t[:, bass.ds(n, 1), :, :].rearrange("p o a s -> p (o a) s")

    def head_rows(h):
        return slice((h % 2) * HD, (h % 2 + 1) * HD)

    act.wait(skew_out)
    with L.run(DEPTH) as layer:
        l = layer.i
        sm = lambda name: small[:, SM1[name]]
        pool.wait(pe.now(), act.now(), dve.now())
        small_in = got_small.did(G.dma_start(small[:, 0:SM1_W], A["small1"][bass.ds(l, 1)].rearrange("o p c -> (o p) c")))
        for e in (dve, act, pe):
            e.wait(small_in, pe.now(), act.now(), dve.now(), pool.now())
        split()
        ready = norm_in(x, sm("pre_mix"), xn_hi, xn_lo, x_in, None)

        pe.wait(ready)
        with L.run(4) as loop:
            for r in range(2):
                pe.wait(loop.last(f"out{r}", act.counter))
                got = slot_T(dense[r], xn_hi, xn_lo)
                act.wait(got)
                loop.keep(f"out{r}", act.did(AC.activation(slot_of(proj, loop.i * 2 + r), dense[r], ACT.Copy)))
        pe.wait(act.now())
        got = slot_T(dense[0], xn_hi, xn_lo)
        act.wait(got)
        ly_done = act.did(AC.activation(proj[:, 8, :, :], dense[0], ACT.Copy))
        r = take()
        forget = used.did(columns_T(dense[1][:, 0, :], 0, r, xn_hi, xn_lo))
        pe.wait(ly_done)
        got = slot_rows(dense[0], xn_hi, xn_lo)
        act.wait(got)
        v0_done = act.did(AC.activation(proj[:, 10, :, :], dense[0], ACT.Copy))

        dve.wait(forget)
        z = dve.did(V.tensor_scalar(f8[:, 0, :], dense[1][0:8, 0, :], small[0:8, SM1["fox_b"]], 0.0, ALU.add, ALU.min))
        act.wait(forget, z)
        a = act.did(AC.activation(f8[:, 1, :], dense[1][0:8, 0, :], ACT.Abs, bias=small[0:8, SM1["fox_b"]]))
        act.wait(a)
        a = act.did(AC.activation(f8[:, 1, :], f8[:, 1, :], ACT.Exp, scale=-1.0))
        act.wait(a)
        a = act.did(AC.activation(f8[:, 1, :], f8[:, 1, :], ACT.Ln, bias=one[0:8]))
        dve.wait(z, a)
        m = dve.did(V.tensor_tensor(f8[:, 0, :], f8[:, 0, :], f8[:, 1, :], ALU.subtract))
        dve.wait(m)
        m = dve.did(V.tensor_tensor_scan(f8[:, 1, :], ones_row, f8[:, 0, :], 0.0, ALU.mult, ALU.add))
        dve.wait(m)
        c_ready = dve.did(V.tensor_scalar(f8[:, 1, :], f8[:, 1, :], 8.0, None, ALU.mult))

        pe.wait(c_ready)
        got = slot_rows(dense[1], xn_hi, xn_lo)
        act.wait(got)
        v1_done = act.did(AC.activation(proj[:, 11, :, :], dense[1], ACT.Copy))
        pe.wait(v0_done)
        got = slot_rows(dense[0], xn_hi, xn_lo)
        act.wait(got)
        rv_done = act.did(AC.activation(proj[:, 12, :, :], dense[0], ACT.Copy))
        pe.wait(v1_done, rv_done)

        lx, ly = proj[:, 7, :, :], proj[:, 8, :, :]
        dve.wait(ly_done)
        for ct in range(2):
            w = lambda n: small[:, SM1["conv_w"].start + 2 * n + ct:SM1["conv_w"].start + 2 * n + ct + 1]
            m = dve.did(V.tensor_scalar(xc[:, ct, :], lx[:, ct, :], w(3), sm("conv_b")[:, ct:ct + 1], ALU.mult, ALU.add))
            for n in (2, 1, 0):
                back = 3 - n
                dve.wait(m)
                m = dve.did(V.scalar_tensor_tensor(xc[:, ct, back:S], lx[:, ct, 0:S - back], w(n), xc[:, ct, back:S],
                                                   ALU.mult, ALU.add))
        xc_done = m
        pe.wait(xc_done)
        for dst, name in ((misc[0], "w_rg"), (misc[1], "w_ig")):
            for ct in range(2):
                m = T.matmul(dst[:, ct, :], sm(name)[:, ct * P:(ct + 1) * P], xc[:, ct, :], start=True, stop=True)
        gated = pe.did(m)
        act.wait(gated)
        for dst, src, b in ((lru_r, misc[0], "b_rg"), (lru_i, misc[1], "b_ig")):
            for ct in range(2):
                m = act.did(AC.activation(dst[:, ct, :], src[:, ct, :], ACT.Sigmoid, bias=sm(b)[:, ct:ct + 1]))
        st = lambda n, w=2: stat[:, n, 0:w]
        a = act.did(AC.activation(st(0), sm("lam"), ACT.Abs))
        act.wait(a)
        a = act.did(AC.activation(st(0), st(0), ACT.Exp, scale=-1.0))
        act.wait(a)
        a = act.did(AC.activation(st(0), st(0), ACT.Ln, bias=one))
        sp0 = dve.did(V.tensor_scalar(st(1), sm("lam"), -1.0, 0.0, ALU.mult, ALU.max))
        dve.wait(sp0, a)
        sp0 = dve.did(V.tensor_tensor(st(1), st(1), st(0), ALU.add))
        dve.wait(sp0)
        dve.did(V.tensor_scalar(st(2), st(1), -8.0, None, ALU.mult))
        sp = dve.did(V.tensor_scalar(st(3), st(1), 8.0, None, ALU.mult))
        act.wait(m, sp)
        for ct in range(2):
            ea = act.did(AC.activation(lru_a[:, ct, :], lru_r[:, ct, :], ACT.Exp, scale=stat[:, 2, ct:ct + 1]))
            act.wait(ea)
            th = act.did(AC.activation(lru_t[:, ct, :], lru_r[:, ct, :], ACT.Tanh, scale=stat[:, 3, ct:ct + 1]))
        dve.wait(th)
        m = dve.did(V.tensor_tensor(lru_u, lru_a, lru_a, ALU.mult))
        dve.wait(m)
        m = dve.did(V.scalar_tensor_tensor(lru_u, lru_u, 1.0, lru_t, ALU.add, ALU.mult))
        act.wait(m)
        m = act.did(AC.activation(lru_u, lru_u, ACT.Sqrt))
        g = act.did(AC.activation(lru_g, ly, ACT.Gelu_apprx_tanh))
        m2 = dve.did(V.tensor_tensor(lru_i, lru_i, xc, ALU.mult))
        dve.wait(m, m2)
        m = dve.did(V.tensor_tensor(lru_u, lru_u, lru_i, ALU.mult))
        dve.wait(m)
        for ct in range(2):
            m = dve.did(V.tensor_tensor_scan(lru_h[:, ct, :], lru_a[:, ct, :], lru_u[:, ct, :], 0.0, ALU.mult, ALU.add))
        dve.wait(m, g)
        m = dve.did(V.tensor_tensor(lru_h, lru_h, lru_g, ALU.mult))
        split_out(y_hi[:, 0:2, :], y_lo[:, 0:2, :], lru_h, m)

        pe.wait(c_ready)
        read = {}
        for h in range(8):
            pe.wait(read.get(h - 2))
            nsel = rows_8[:, h * P:(h + 1) * P]
            m = pe.did(T.matmul(acc[2 + h % 2][:, 0, :], nsel, f8[:, 1, :], start=True, stop=True))
            dve.wait(m)
            dve.did(V.tensor_tensor(c_late[:, h, :], acc[2 + h % 2][:, 0, :], c("causal"), ALU.add))
            read[h] = dve.did(V.tensor_tensor(c_early[:, h, :], acc[2 + h % 2][:, 0, 0:P],
                                              c("causal")[:, P:S], ALU.add))

        def fox_scores(h):
            q, k = proj[head_rows(h), h // 4, (h // 2) % 2, :], proj[head_rows(h), 2 + h // 4, (h // 2) % 2, :]
            out = acc[h % 2].rearrange("p a s -> p (a s)")
            pe.wait(scored.get(h - 2))
            for rt, cols, nk in ((1, slice(0, S), S), (0, slice(S, S + P), P)):
                m = T.matmul(out[:, cols], q[:, rt * P:(rt + 1) * P], k[:, 0:nk], start=True, stop=True)
            return pe.did(m)

        def fox_softmax(h, ready):
            src = acc[h % 2].rearrange("p a s -> p (a s)")
            lg = logit[h % 2][:, 0, :]
            s4 = stat[:, 0:4, 16 + 2 * (h % 2):18 + 2 * (h % 2)]
            dve.wait(ready, transposed.get(h - 2))
            dve.settle()
            dve.did(V.tensor_tensor_reduce(lg[:, 0:S], src[:, 0:S], c_late[:, h, :], 1.0, LOWEST, ALU.add, ALU.max, s4[:, 0, 0:1]))
            m = dve.did(V.tensor_tensor_reduce(lg[:, S:S + P], src[:, S:S + P], c_early[:, h, :], 1.0, LOWEST,
                                               ALU.add, ALU.max, s4[:, 0, 1:2]))
            scored[h] = m
            dve.wait(m)
            m = dve.did(V.tensor_scalar(s4[:, 1, :], s4[:, 0, :], -0.125, None, ALU.mult))
            act.wait(m)
            act.did(AC.activation(lg[:, 0:S], lg[:, 0:S], ACT.Exp, bias=s4[:, 1, 0:1], scale=0.125,
                                  accum_out=s4[:, 2, 0:1]))
            m = act.did(AC.activation(lg[:, S:S + P], lg[:, S:S + P], ACT.Exp, bias=s4[:, 1, 1:2], scale=0.125,
                                      accum_out=s4[:, 2, 1:2]))
            dve.wait(m)
            m = dve.did(V.reciprocal(s4[:, 3, :], s4[:, 2, :]))
            dve.wait(m)
            dve.did(V.tensor_scalar(lg[:, 0:S], lg[:, 0:S], s4[:, 3, 0:1], None, ALU.mult))
            return dve.did(V.tensor_scalar(lg[:, S:S + P], lg[:, S:S + P], s4[:, 3, 1:2], None, ALU.mult))

        def causal_transpose(n, lg, dst_bank, dst, ready, free):
            pe.wait(ready, free)
            for to, frm in ((0, S), (1, 0), (2, P)):
                m = T.transpose(dst_bank[:, to * P:(to + 1) * P], lg[:, frm:frm + P], c("ident"))
            m = pe.did(m)
            transposed[n] = m
            act.wait(m, free)
            return act.did(AC.activation(dst[:, 0:384], dst_bank[:, 0:384], ACT.Copy))

        scored, transposed, valued, ysplit, probs, pTs = {}, {}, {}, {}, {}, {}
        for n in range(8 + 2):
            if n < 8:
                s = fox_scores(n)
                probs[n] = fox_softmax(n, s)
            if 1 <= n < 9:
                h = n - 1
                pTs[h] = causal_transpose(h, logit[h % 2][:, 0, :], bank[4 + h % 2], probT[h % 2][:, 0, :],
                                          probs[h], valued.get(h - 2))
            if n >= 2:
                h = n - 2
                o = misc[(h // 2) % 2][:, 0, :]
                pe.wait(pTs[h], ysplit.get(h // 2 - 2))
                v = lambda kt: proj[:, 10 + h // 4, kt, (h % 4) * HD:(h % 4 + 1) * HD]
                valued[h] = pe.did(causal_values(o[head_rows(h), :], v, probT[h % 2][:, 0, :]))
                if h % 2:
                    ysplit[h // 2] = split_out(y_hi[:, 2 + h // 2, :], y_lo[:, 2 + h // 2, :], o, valued[h])
        fox_done = ysplit[3]

        rq, rk, rg = proj[:, 4, :, :], proj[:, 5, :, :], proj[:, 6, :, :]
        pe.wait(fox_done)
        rot_done = []
        for n, src in enumerate((rq, rk)):
            m = pe.did(T.matmul(misc[n].rearrange("p a s -> p (a s)"), c("rot"), src.rearrange("p a s -> p (a s)"),
                                start=True, stop=True))
            dve.wait(m)
            dst = (lru_a, lru_t)[n]
            other = (lru_u, lru_h)[n]
            dve.wait(act.now())
            a1 = dve.did(V.tensor_tensor(dst, src, cos.unsqueeze(1).broadcast_to([P, 2, S]), ALU.mult))
            a2 = dve.did(V.tensor_tensor(other, misc[n], sin.unsqueeze(1).broadcast_to([P, 2, S]), ALU.mult))
            dve.wait(a2)
            rot_done.append(dve.did(V.tensor_tensor(dst, dst, other, ALU.add)))
        pe.wait(rot_done[1])
        read = {}
        for h in range(4):
            q, k = lru_a[head_rows(h), h // 2, :], lru_t[head_rows(h), h // 2, :]
            b = acc[h % 2].rearrange("p a s -> p (a s)")
            pe.wait(read.get(h - 2))
            T.matmul(b[:, 0:S], k[:, 0:P], q[:, :], start=True, stop=True)
            m = pe.did(T.matmul(b[:, S:S + P], k[:, P:S], q[:, P:S], start=True, stop=True))
            dve.wait(m, read.get(("v", h - 2)))
            dec = con[:, CON["decay"].start + h * S:CON["decay"].start + (h + 1) * S]
            dve.did(V.tensor_tensor(probT[h % 2][:, 0, 0:S], b[:, 0:S], dec, ALU.mult))
            read[h] = dve.did(V.tensor_tensor(probT[h % 2][:, 0, S:S + P], b[:, S:S + P], dec[:, 0:P], ALU.mult))
            pe.wait(read[h])
            v = lambda kt: proj[:, 12, kt, h * HD:(h + 1) * HD]
            read[("v", h)] = pe.did(causal_values(acc[2 + h // 2][head_rows(h), 0, :], v, probT[h % 2][:, 0, :]))
        yr = lru_u
        act.wait(read[("v", 3)])
        for t in range(2):
            m = act.did(AC.activation(yr[:, t, :], acc[2 + t][:, 0, :], ACT.Copy))
        pe.wait(m)
        mean = pe.did(T.matmul(bank[6], c("blk"), yr.rearrange("p a s -> p (a s)"), start=True, stop=True))
        dve.wait(mean)
        m = dve.did(V.tensor_tensor(yr, yr, misc[0], ALU.subtract))
        act.wait(m)
        m = act.did(AC.activation(lru_h, yr, ACT.Square))
        pe.wait(m)
        var = pe.did(T.matmul(bank[7], c("blk"), lru_h.rearrange("p a s -> p (a s)"), start=True, stop=True))
        r = inverse_root(bank[7], 512, var)
        sg = act.did(AC.activation(lru_g, rg, ACT.Silu))
        dve.wait(r)
        m = dve.did(V.tensor_tensor(yr, yr, rinv, ALU.mult))
        dve.wait(m, sg)
        m = dve.did(V.tensor_tensor(yr, yr, lru_g, ALU.mult))
        ret_done = split_out(y_hi[:, 6:8, :], y_lo[:, 6:8, :], yr, m)

        got = out_projection(y_hi, y_lo, ret_done, None)
        x_ready = norm_add(sm("post_mix"), got)

        ready = norm_in(x, sm("pre_cross"), xn_hi, xn_lo, x_ready, None)
        pe.wait(ready, mem_ready)
        for form, first, hi, lo in ((slot_T, 0, xn_hi, xn_lo), (slot_T, 4, mem_hi, mem_lo), (slot_rows, 8, mem_hi, mem_lo)):
            with L.run(2) as loop:
                for r in range(2):
                    pe.wait(loop.last(f"out{r}", act.counter))
                    got = form(dense[r], hi, lo)
                    act.wait(got)
                    loop.keep(f"out{r}", act.did(AC.activation(slot_of(proj, loop.i * 2 + (r + first)),
                                                               dense[r], ACT.Copy)))
            pe.wait(act.now())
        scored, transposed, valued, ysplit, probs, pTs = {}, {}, {}, {}, {}, {}
        for n in range(4 + 2):
            if n < 4:
                h = n
                pe.wait(scored.get(h - 2))
                for rt in range(2):
                    for dt in range(2):
                        m = T.matmul(acc[h % 2][:, rt, :], proj[:, h, dt, rt * P:(rt + 1) * P], proj[:, 4 + h, dt, :],
                                     start=dt == 0, stop=dt == 1)
                m = pe.did(m)
                s4 = stat[:, 0:4, 16 + 2 * (h % 2):18 + 2 * (h % 2)]
                dve.wait(m, scored.get(h - 2))
                m = dve.did(V.tensor_reduce(s4[:, 0, :], acc[h % 2], AX.X, ALU.max))
                dve.wait(m)
                m = dve.did(V.tensor_scalar(s4[:, 1, :], s4[:, 0, :], -0.0625, None, ALU.mult))
                act.wait(m, transposed.get(h - 2))
                for rt in range(2):
                    m = act.did(AC.activation(logit[h % 2][:, 0, rt * S:(rt + 1) * S], acc[h % 2][:, rt, :], ACT.Exp,
                                              bias=s4[:, 1, rt:rt + 1], scale=0.0625, accum_out=s4[:, 2, rt:rt + 1]))
                scored[h] = m
                dve.wait(m)
                m = dve.did(V.reciprocal(s4[:, 3, :], s4[:, 2, :]))
                dve.wait(m)
                for rt in range(2):
                    probs[h] = dve.did(V.tensor_scalar(logit[h % 2][:, 0, rt * S:(rt + 1) * S],
                                                       logit[h % 2][:, 0, rt * S:(rt + 1) * S],
                                                       s4[:, 3, rt:rt + 1], None, ALU.mult))
            if 1 <= n < 5:
                h = n - 1
                pe.wait(probs[h], pTs.get(h - 1))
                for kt in range(2):
                    for rt in range(2):
                        m = T.transpose(bank[4 + h % 2][:, kt * S + rt * P:kt * S + (rt + 1) * P],
                                        logit[h % 2][:, 0, rt * S + kt * P:rt * S + (kt + 1) * P], c("ident"))
                transposed[h] = pe.did(m)
                act.wait(transposed[h], valued.get(h - 2))
                pTs[h] = act.did(AC.activation(probT[h % 2][:, 0, :], bank[4 + h % 2], ACT.Copy))
            if n >= 2:
                h = n - 2
                pe.wait(pTs[h], ysplit.get(h - 2))
                for dt in range(2):
                    for kt in range(2):
                        m = T.matmul(misc[h % 2][:, dt, :], proj[:, 8 + h, kt, dt * P:(dt + 1) * P],
                                     probT[h % 2][:, 0, kt * S:(kt + 1) * S], start=kt == 0, stop=kt == 1)
                valued[h] = pe.did(m)
                ysplit[h] = split_out(y_hi[:, 2 * h:2 * h + 2, :], y_lo[:, 2 * h:2 * h + 2, :], misc[h % 2], valued[h])
        got = out_projection(y_hi, y_lo, ysplit[3], None)
        x_ready = norm_add(sm("post_cross"), got)

        ready = norm_in(x, sm("pre_ffn"), xn_hi, xn_lo, x_ready, None)
        got = ffn(xn_hi, xn_lo, ready, False)
        x_ready = norm_add(sm("post_ffn"), got)

    got_table = Counter(L, "got_table", 16)
    pool.wait(skew_out, pe.now())
    by_row = A["skew"][P - 1:P - 1 + P * (12 * VEC - 1)].rearrange("(p v) -> p v", v=12 * VEC - 1)
    got_table.did(G.dma_start(table[:, 0:11, :], by_row[:, 0:11 * VEC].rearrange("p (h v) -> p h v", v=VEC)[:, :, 0:S]))
    table_in = got_table.did(G.dma_start(table[:, 11, :], by_row[:, 11 * VEC:11 * VEC + S]))

    got_y2 = x_ready
    with L.run(DEPTH) as layer:
        l = layer.i
        sm = lambda name: small[:, SM2[name]]
        pool.wait(pe.now(), act.now(), dve.now())
        small_in = got_small.did(G.dma_start(small[:, 0:SM2_W], A["small2"][bass.ds(l, 1)].rearrange("o p c -> (o p) c")))
        for e in (dve, act, pe):
            e.wait(small_in, pe.now(), act.now(), dve.now(), pool.now(), table_in)
        split()

        def half_ffn(gain, x_ready, last_ahead):
            ready = norm_in(x, gain, xn_hi, xn_lo, x_ready, None)
            got = ffn(xn_hi, xn_lo, ready, last_ahead)
            dve.wait(got)
            for b in range(4):
                m = dve.did(V.scalar_tensor_tensor(x[:, 2 * b:2 * b + 2, :], acc[b], 0.5, x[:, 2 * b:2 * b + 2, :],
                                                   ALU.mult, ALU.add))
            return m

        x_ready = half_ffn(sm("ffn1"), None, True)
        ready = norm_in(x, sm("mix"), xn_hi, xn_lo, x_ready, pe.now())

        pe.wait(ready, act.now(), dve.now())
        act.wait(pe.now(), dve.now())
        with L.run(3) as loop:
            for r in range(2):
                pe.wait(loop.last(f"out{r}", act.counter))
                got = slot_T(dense[r], xn_hi, xn_lo)
                act.wait(got)
                loop.keep(f"out{r}", act.did(AC.activation(slot_of(proj, loop.i * 2 + r), dense[r], ACT.Copy)))
        pe.wait(act.now())
        got = slot_T(dense[0], xn_hi, xn_lo)
        act.wait(got)
        m = act.did(AC.activation(proj[:, 6, :, :], dense[0], ACT.Copy))
        r = take()
        columns_T(dense[1][:, 0, :], 0, r, xn_hi, xn_lo)
        for rt in range(2):
            mm = rows(dense[1][:, 1, rt * P:(rt + 1) * P], rt, r, xn_hi, xn_lo, slice(P, 2 * P))
        got = used.did(mm)
        act.wait(got)
        m7 = act.did(AC.activation(proj[:, 7, :, :], dense[1], ACT.Copy))
        pe.wait(m)
        got = slot_rows(dense[0], xn_hi, xn_lo)
        act.wait(got)
        m = act.did(AC.activation(proj[:, 8, :, :], dense[0], ACT.Copy))
        pe.wait(m7)
        got = slot_rows(dense[1], xn_hi, xn_lo)
        act.wait(got)
        m9 = act.did(AC.activation(proj[:, 9, :, :], dense[1], ACT.Copy))

        gate24 = stat[:, 4:6, 0:24]
        wg = sm("w_gate").rearrange("p (k n) -> p k n", k=KT)
        for rt in range(2):
            for k in range(KT):
                mm = T.matmul(misc[1][:, 0, rt * 24:(rt + 1) * 24], xn[:, k, rt * P:(rt + 1) * P], wg[:, k, :],
                              start=k == 0, stop=k == KT - 1)
        m = pe.did(mm)
        act.wait(m)
        gate_ready = act.did(AC.activation(gate24, misc[1][:, 0, 0:48].rearrange("p (r n) -> p r n", r=2), ACT.Sigmoid))

        pe.wait(m9)
        with L.run(6) as loop:
            for r in range(2):
                pe.wait(loop.last(f"out{r}", act.counter))
                got = slot_T(dense[r], xn_hi, xn_lo)
                act.wait(got)
                loop.keep(f"out{r}", act.did(AC.activation(gates[:, bass.ds(loop.i * 4 + r * 2, 2), :], dense[r], ACT.Sigmoid)))

        def head_norm(tiles, gain, ready):
            n = tiles.shape[1]
            act.wait(ready)
            m = act.did(AC.activation(sq[:, 0:n, :], tiles, ACT.Square))
            pe.wait(m, dve.now())
            m = pe.did(T.matmul(bank[6][:, 0:n * S], c("blk"), sq[:, 0:n, :].rearrange("p a s -> p (a s)"),
                                start=True, stop=True))
            r = inverse_root(bank[6][:, 0:n * S], n * S, m)
            dve.wait(r)
            return dve.did(V.scalar_tensor_tensor(tiles, tiles, gain, rinv[:, 0:n, :], ALU.mult, ALU.mult))

        m = act.now()
        m = head_norm(proj[:, 0, :, :], sm("nsa_q"), m)
        m = head_norm(proj[:, 1, :, :], sm("nsa_q"), m)
        m = head_norm(proj[:, 3, :, :], sm("nsa_k"), m)
        m = head_norm(proj[:, 6, :, :], sm("swa_q"), m)
        m = head_norm(proj[:, 7, 0:1, :], sm("swa_k"), m)

        cmp_w = 2 * N_CMP
        blocks = sq.rearrange("p a s -> p (a s)")[:, 0:16 * cmp_w].rearrange("p (t n) -> p t n", n=cmp_w)
        b_hi = y_hi.rearrange("p a s -> p (a s)")[:, 0:16 * cmp_w].rearrange("p (t n) -> p t n", n=cmp_w)
        b_lo = y_lo.rearrange("p a s -> p (a s)")[:, 0:16 * cmp_w].rearrange("p (t n) -> p t n", n=cmp_w)
        hid = rinv_f[:, 0:2 * cmp_w].rearrange("p (t n) -> p t n", n=cmp_w)
        kc = root_f[:, 0:N_CMP]
        vc = root_f[0:N_CMP, 128:128 + 2 * HD]
        for which in range(2):
            src = proj[:, 2, which, :]
            dve.wait(pe.now(), act.now(), dve.now())
            for g in range(2):
                for par in range(2):
                    rs, ps_ = slice(par * HD, (par + 1) * HD), slice(g * HD, (g + 1) * HD)
                    by_two = src[ps_, :].rearrange("p (n t q) -> p t n q", t=8, q=2)
                    pos = small[rs, SM2["cmp_pos"]].unsqueeze(2).broadcast_to([HD, 16, N_CMP])
                    for u in range(2):
                        m = dve.did(V.tensor_copy(blocks[rs, 8 * u:8 * u + 8, g * N_CMP:(g + 1) * N_CMP],
                                                  by_two[:, :, u:u + N_CMP, par]))
                    dve.wait(m)
                    m = dve.did(V.tensor_tensor(blocks[rs, :, g * N_CMP:(g + 1) * N_CMP],
                                                blocks[rs, :, g * N_CMP:(g + 1) * N_CMP], pos, ALU.add))
            m = split_out(b_hi, b_lo, blocks, m)
            pe.wait(m)
            for half in range(2):
                r = take()
                for ct in range(2):
                    for k in range(KT):
                        w = [t[r][:, k, ct * P:(ct + 1) * P] for t in (w_hi, w_lo)]
                        b = [t[:, half * KT + k, :] for t in (b_hi, b_lo)]
                        mm = products(misc[ct][:, 0, 0:cmp_w], w, b, half == 0 and k == 0, half == 1 and k == KT - 1,
                                      skip_group_check=True)
                m = used.did(mm)
            act.wait(m)
            for ct in range(2):
                m = act.did(AC.activation(hid[:, ct, :], misc[ct][:, 0, 0:cmp_w], ACT.Silu))
            pe.wait(m)
            w2 = small[:, SM2["w2v" if which else "w2k"]].rearrange("p (t d) -> p t d", t=2)
            for g in range(2):
                for t in range(2):
                    h = hid[:, t, g * N_CMP:(g + 1) * N_CMP]
                    if which == 0:
                        mm = T.matmul(acc[g][g * HD:(g + 1) * HD, 0, 0:N_CMP], w2[:, t, :], h, start=t == 0, stop=t == 1)
                    else:
                        mm = T.matmul(acc[2][0:N_CMP, 0, g * HD:(g + 1) * HD], h, w2[:, t, :], start=t == 0, stop=t == 1)
            m = pe.did(mm)
            act.wait(m)
            if which == 0:
                for g in range(2):
                    pr = slice(g * HD, (g + 1) * HD)
                    m = act.did(AC.activation(kc[pr, :], acc[g][pr, 0, 0:N_CMP], ACT.Copy))
                act.wait(m)
                m = act.did(AC.activation(hid[:, 0, 0:N_CMP], kc, ACT.Square))
                pe.wait(m)
                m = pe.did(T.matmul(bank[6][:, 0:N_CMP], c("blk"), hid[:, 0, 0:N_CMP], start=True, stop=True))
                act.wait(m)
                m = act.did(AC.activation(hid[:, 0, 0:N_CMP], bank[6][:, 0:N_CMP], ACT.Sqrt, bias=eps))
                dve.wait(m)
                m = dve.did(V.reciprocal(hid[:, 0, 0:N_CMP], hid[:, 0, 0:N_CMP]))
                dve.wait(m)
                m = dve.did(V.scalar_tensor_tensor(kc, kc, sm("nsa_k"), hid[:, 0, 0:N_CMP], ALU.mult, ALU.mult))
            else:
                m = act.did(AC.activation(vc, acc[2][0:N_CMP, 0, 0:P], ACT.Copy))

        CL, CE = slice(384, 384 + N_CMP), slice(384 + N_CMP, 384 + N_CMP + N_CMP0)
        scored, transposed, valued, ysplit, probs, pTs = {}, {}, {}, {}, {}, {}
        for e in (pe, act, dve):
            e.wait(pe.now(), act.now(), dve.now())

        def nsa_scores(h):
            g, t = h // 4, h % 4
            pr = slice(g * HD, (g + 1) * HD)
            q = proj[pr, t // 2, t % 2, :]
            pe.wait(scored.get(h - 1))
            for b in range(2):
                k, out = proj[pr, 3, b, :], bank[2 + b]
                T.matmul(out[:, 0:S], q[:, P:S], k, start=True, stop=True)
                mm = T.matmul(out[:, S:S + P], q[:, 0:P], k[:, 0:P], start=True, stop=True)
                if b == 0:
                    T.matmul(out[:, CL], q[:, P:S], kc[pr, :], start=True, stop=True)
                    mm = T.matmul(out[:, CE], q[:, 0:P], kc[pr, 0:N_CMP0], start=True, stop=True)
            return pe.did(mm)

        spans = [(0, slice(0, S), slice(0, S), 1, 1), (1, slice(0, S), slice(0, S), 1, 2), (0, CL, slice(31, S, 16), 1, 0),
                 (0, slice(S, S + P), slice(P, S), 0, 1), (1, slice(S, S + P), slice(P, S), 0, 2),
                 (0, CE, slice(P + 31, S, 16), 0, 0)]

        def nsa_softmax(h, ready):
            lg = logit[h % 2]
            s6 = stat[:, 0:4, 8 * (h % 2):8 * (h % 2) + 6]
            dve.wait(ready, transposed.get(h - 2))
            dve.settle()
            for n, (b, cols, tc, rt, br) in enumerate(spans):
                m = dve.did(V.tensor_tensor_reduce(lg[:, b, cols], bank[2 + b][:, cols], table[:, h, tc], 1.0, LOWEST,
                                                   ALU.add, ALU.max, s6[:, 0, n:n + 1]))
            scored[h] = m
            dve.wait(m)
            m = dve.did(V.tensor_scalar(s6[:, 1, :], s6[:, 0, :], -0.125, None, ALU.mult))
            act.wait(m)
            for n, (b, cols, tc, rt, br) in enumerate(spans):
                m = act.did(AC.activation(lg[:, b, cols], lg[:, b, cols], ACT.Exp, bias=s6[:, 1, n:n + 1], scale=0.125,
                                          accum_out=s6[:, 2, n:n + 1]))
            dve.wait(m, gate_ready)
            m = dve.did(V.reciprocal(s6[:, 3, :], s6[:, 2, :]))
            dve.wait(m)
            for rt, at in ((1, 0), (0, 3)):
                dve.did(V.tensor_tensor(s6[:, 3, at:at + 2], s6[:, 3, at:at + 2], gate24[:, rt, 8 + h:24:8], ALU.mult))
                m = dve.did(V.tensor_tensor(s6[:, 3, at + 2:at + 3], s6[:, 3, at + 2:at + 3], gate24[:, rt, h:h + 1], ALU.mult))
            dve.wait(m)
            m = dve.did(V.tensor_tensor(s6[:, 3, 5:6], s6[:, 3, 5:6], c("late"), ALU.mult))
            dve.wait(m)
            for n, (b, cols, tc, rt, br) in enumerate(spans):
                m = dve.did(V.tensor_scalar(lg[:, b, cols], lg[:, b, cols], s6[:, 3, n:n + 1], None, ALU.mult))
            return m

        def nsa_transpose(h):
            lg = logit[h % 2]
            pe.wait(probs[h], pTs.get(h - 1))
            for b in range(2):
                for to, frm in ((0, S), (1, 0), (2, P)):
                    mm = T.transpose(bank[4 + b][:, to * P:(to + 1) * P], lg[:, b, frm:frm + P], c("ident"))
            T.transpose(bank[6][0:N_CMP0, 0:P], lg[:, 0, CE], c("ident"))
            mm = T.transpose(bank[6][0:N_CMP, P:S], lg[:, 0, CL], c("ident"))
            transposed[h] = pe.did(mm)
            act.wait(transposed[h], valued.get(h - 2))
            dve.wait(transposed[h], valued.get(h - 2))
            a = act.did(AC.activation(probT[h % 2][:, 0, 0:384], bank[4][:, 0:384], ACT.Copy))
            d = dve.did(V.tensor_copy(probT[h % 2][:, 1, 0:384], bank[5][:, 0:384]))
            cp = sq[0:N_CMP, h % 2, :]
            act.did(AC.activation(cp[0:N_CMP0, 0:P], bank[6][0:N_CMP0, 0:P], ACT.Copy))
            a = act.did(AC.activation(cp[:, P:S], bank[6][0:N_CMP, P:S], ACT.Copy))
            return [a, d]

        def nsa_values(h):
            g, t = h // 4, h % 4
            pr = slice(g * HD, (g + 1) * HD)
            o = bank[7][pr, 0:S]
            cp = sq[0:N_CMP, h % 2, :]
            pe.wait(pTs[h], ysplit.get(h - 1))
            for b in range(2):
                v = lambda kt: proj[:, 8, kt, b * P + g * HD:b * P + (g + 1) * HD]
                causal_values(o, v, probT[h % 2][:, b, :], b == 0, False)
            T.matmul(o[:, 0:P], vc[0:N_CMP0, pr], cp[0:N_CMP0, 0:P], start=False, stop=False, skip_group_check=True)
            valued[h] = pe.did(T.matmul(o[:, P:S], vc[:, pr], cp[:, P:S], start=False, stop=True, skip_group_check=True))
            ysplit[h] = split_out(y_hi[pr, t, :], y_lo[pr, t, :], o, valued[h])

        for n in range(8 + 2):
            if n < 8:
                probs[n] = nsa_softmax(n, nsa_scores(n))
            if 1 <= n < 9:
                pTs[n - 1] = nsa_transpose(n - 1)
            if n >= 2:
                nsa_values(n - 2)

        scored, probs, pTs, transposed, valued = {}, {}, {}, {}, {}
        for e in (pe, act, dve):
            e.wait(pe.now(), act.now(), dve.now())
        for n in range(4 + 2):
            if n < 4:
                h = n
                g, t = h // 2, h % 2
                pr = slice(g * HD, (g + 1) * HD)
                q, k, out = proj[pr, 6, t, :], proj[pr, 7, 0, :], bank[2 + h % 2]
                pe.wait(scored.get(h - 2))
                T.matmul(out[:, 0:S], q[:, P:S], k, start=True, stop=True)
                m = pe.did(T.matmul(out[:, S:S + P], q[:, 0:P], k[:, 0:P], start=True, stop=True))
                lg, s4 = logit[h % 2][:, 0, :], stat[:, 0:4, 16 + 4 * (h % 2):18 + 4 * (h % 2)]
                e4 = stat[:, 0, 18 + 4 * (h % 2):20 + 4 * (h % 2)]
                sink = sm("sinks")[:, h:h + 1]
                dve.wait(m, transposed.get(h - 2))
                dve.settle()
                dve.did(V.tensor_tensor_reduce(lg[:, 0:S], out[:, 0:S], table[:, 8 + h, :], 1.0, LOWEST,
                                               ALU.add, ALU.max, s4[:, 0, 0:1]))
                m = dve.did(V.tensor_tensor_reduce(lg[:, S:S + P], out[:, S:S + P], table[:, 8 + h, P:S], 1.0, LOWEST,
                                                   ALU.add, ALU.max, s4[:, 0, 1:2]))
                scored[h] = m
                dve.wait(m)
                m = dve.did(V.tensor_scalar(s4[:, 0, :], s4[:, 0, :], 0.125, sink, ALU.mult, ALU.max))
                dve.wait(m)
                m = dve.did(V.tensor_scalar(s4[:, 1, :], s4[:, 0, :], -1.0, None, ALU.mult))
                act.wait(m)
                act.did(AC.activation(e4, s4[:, 1, :], ACT.Exp, bias=sink))
                act.did(AC.activation(lg[:, 0:S], lg[:, 0:S], ACT.Exp, bias=s4[:, 1, 0:1], scale=0.125,
                                      accum_out=s4[:, 2, 0:1]))
                m = act.did(AC.activation(lg[:, S:S + P], lg[:, S:S + P], ACT.Exp, bias=s4[:, 1, 1:2], scale=0.125,
                                          accum_out=s4[:, 2, 1:2]))
                dve.wait(m)
                m = dve.did(V.tensor_tensor(s4[:, 3, :], s4[:, 2, :], e4, ALU.add))
                dve.wait(m)
                m = dve.did(V.reciprocal(s4[:, 3, :], s4[:, 3, :]))
                dve.wait(m)
                dve.did(V.tensor_scalar(lg[:, 0:S], lg[:, 0:S], s4[:, 3, 0:1], None, ALU.mult))
                probs[h] = dve.did(V.tensor_scalar(lg[:, S:S + P], lg[:, S:S + P], s4[:, 3, 1:2], None, ALU.mult))
            if 1 <= n < 5:
                h = n - 1
                pe.wait(probs[h], valued.get(h - 2))
                for to, frm in ((0, S), (1, 0), (2, P)):
                    m = T.transpose(bank[4 + h % 2][:, to * P:(to + 1) * P], logit[h % 2][:, 0, frm:frm + P], c("ident"))
                transposed[h] = pe.did(m)
                act.wait(transposed[h], valued.get(h - 2))
                pTs[h] = act.did(AC.activation(probT[h % 2][:, 0, 0:384], bank[4 + h % 2][:, 0:384], ACT.Copy))
            if n >= 2:
                h = n - 2
                g, t = h // 2, h % 2
                pr = slice(g * HD, (g + 1) * HD)
                o = bank[6 + h % 2][pr, 0:S]
                pe.wait(pTs[h], ysplit.get(("w", h - 2)))
                v = lambda kt: proj[:, 7, 1, kt * P + g * HD:kt * P + (g + 1) * HD]
                valued[h] = pe.did(causal_values(o, v, probT[h % 2][:, 0, :]))
                ysplit[("w", h)] = split_out(y_hi[pr, 6 + t, :], y_lo[pr, 6 + t, :], o, valued[h])

        read = {}
        for e in (pe, act, dve):
            e.wait(pe.now(), act.now(), dve.now())
        for h in range(4):
            q, k = proj[head_rows(h), 4, h // 2, :], proj[head_rows(h), 5, h // 2, :]
            b, ab = bank[2 + h % 2], bank[4 + h % 2]
            zt, spt = logit[h % 2][:, 0, 0:384], logit[h % 2][:, 1, 0:384]
            wt = probT[h % 2][:, 0, 0:384]
            pe.wait(read.get(h - 2))
            T.matmul(b[:, 0:S], k[:, 0:P], q, start=True, stop=True)
            m = pe.did(T.matmul(b[:, S:S + P], k[:, P:S], q[:, P:S], start=True, stop=True))
            act.wait(m, read.get(h - 2))
            zc = act.did(AC.activation(zt, b[:, 0:384], ACT.Copy, scale=0.125))
            a = act.did(AC.activation(spt, b[:, 0:384], ACT.Abs, scale=0.125))
            act.wait(a)
            a = act.did(AC.activation(spt, spt, ACT.Exp, scale=-1.0))
            act.wait(a)
            a = act.did(AC.activation(spt, spt, ACT.Ln, bias=one))
            dve.wait(zc, a)
            m = dve.did(V.scalar_tensor_tensor(spt, zt, 0.0, spt, ALU.max, ALU.add))
            dve.wait(m)
            for cols in (slice(0, P), slice(S, S + P)):
                m = dve.did(V.tensor_tensor(spt[:, cols], spt[:, cols], c("strict"), ALU.mult))
            pe.wait(m)
            T.matmul(ab[:, 0:S], c("tri"), spt[:, 0:S], start=True, stop=False, skip_group_check=True)
            T.matmul(ab[:, P:S], ones, spt[:, S:S + P], start=False, stop=True, skip_group_check=True)
            m = pe.did(T.matmul(ab[:, S:S + P], c("tri"), spt[:, S:S + P], start=True, stop=True, skip_group_check=True))
            dve.wait(m)
            m = dve.did(V.tensor_tensor(zt, zt, ab[:, 0:384], ALU.subtract))
            dve.wait(m)
            for cols in (slice(0, P), slice(S, S + P)):
                m = dve.did(V.tensor_tensor(zt[:, cols], zt[:, cols], c("strict_add"), ALU.add))
            act.wait(m, read.get(h - 2))
            m = act.did(AC.activation(wt, zt, ACT.Exp))
            o = bank[6 + (h // 2) % 2]
            pe.wait(m)
            v = lambda kt: proj[:, 9, kt, h * HD:(h + 1) * HD]
            read[h] = pe.did(causal_values(o[head_rows(h), 0:S], v, wt))
            if h % 2:
                sb_done = split_out(y_hi[:, 4 + h // 2, :], y_lo[:, 4 + h // 2, :], o[:, 0:S], read[h])

        pe.wait(sb_done)
        for e in (act, dve):
            e.wait(pe.now(), act.now(), dve.now())
        up_banks = [dense[0], dense[1], acc[0]]
        with L.run(2) as loop:
            for half in range(2):
                b = loop.i * 4 + half * 2
                before = loop.last("merged1", dve.counter) if half == 0 else low
                pe.wait(before)
                r = take()
                for n, kts in enumerate((range(0, 4), range(4, 6), range(6, 8))):
                    for ct in range(2):
                        mm = columns_T(up_banks[n][:, ct, :], ct, r, y_hi, y_lo, kts)
                got = used.did(mm)
                dve.wait(got, before)
                t3 = [sq[:, 2 * n:2 * n + 2, :] for n in range(3)]
                for n in range(3):
                    m = dve.did(V.tensor_tensor(t3[n], up_banks[n], gates[:, bass.ds(b + 8 * n, 2), :], ALU.mult))
                dve.wait(m)
                m = dve.did(V.tensor_tensor(t3[0], t3[0], t3[1], ALU.add))
                dve.wait(m)
                m = dve.did(V.tensor_tensor(t3[0], t3[0], t3[2], ALU.add))
                act.wait(m)
                hh = act.did(AC.activation(xn_hi[:, bass.ds(b, 2), :], t3[0], ACT.Copy))
                dve.wait(hh)
                low = dve.did(V.tensor_tensor(xn_lo[:, bass.ds(b, 2), :], t3[0],
                                              xn_hi[:, bass.ds(b, 2), :].bitcast(F32), ALU.subtract))
                if half:
                    loop.keep("merged1", low)
        got = out_projection(xn_hi, xn_lo, [dve.now(), act.now()], None)
        for b in range(4):
            dve.wait(got[b])
            m = dve.did(V.tensor_tensor(x[:, 2 * b:2 * b + 2, :], x[:, 2 * b:2 * b + 2, :], acc[b], ALU.add))
        x_ready = half_ffn(sm("ffn2"), m, False)

    pool.wait(dve.now())
    stored = Counter(L, "stored", 16)
    out_done = stored.did(G.dma_start(A["out"], x))
    pool.wait(out_done)
    return L


def constants():
    out = np.zeros((P, CON_W), np.float32)
    i, j = np.arange(P)[:, None], np.arange(P)[None, :]
    out[:, CON["ident"]] = i == j
    out[:, CON["blk"]] = (i // HD == j // HD) / HD
    out[:, CON["tri"]] = i >= j
    rot = np.zeros((P, P), np.float32)
    for p in range(P):
        if p % HD < HD // 2:
            rot[p + HD // 2, p] = -1
        else:
            rot[p - HD // 2, p] = 1
    out[:, CON["rot"]] = rot
    out[:, CON["causal"]] = np.where(P + i - np.arange(S)[None, :] >= 0, 0, BIG)
    out[:, CON["strict"]] = i < j
    out[:, CON["strict_add"]] = np.where(i < j, 0, BIG)
    gamma = 1 - 2.0 ** (-5.0 - np.arange(4))
    diff = j - i
    for h in range(4):
        diag = np.where(diff >= 0, gamma[h] ** np.maximum(diff, 0), 0)
        out[:, CON["decay"]][:, h * S:(h + 1) * S] = np.concatenate([diag, gamma[h] ** (P + diff)], 1) * HD ** -0.5
    half = HD // 2
    out[:, CON["inv_freq"]] = (np.float32(10000.0) ** (-(np.arange(P) % half).astype(np.float32) / half))[:, None]
    out[:, CON["late"]] = (np.arange(P) >= 31)[:, None]
    early = np.zeros((34, EARLY_W), np.float32)
    for h in range(8):
        early[h, EARLY["nsel"].start + h * P:EARLY["nsel"].start + (h + 1) * P] = -1
    dist = S - 1 - np.arange(VEC)
    big = 16 + (np.log(np.maximum(dist, 1).astype(np.float32) / 16) / np.float32(np.log(8)) * 16).astype(np.int32)
    bucket = np.where(np.maximum(dist, 0) < 16, np.maximum(dist, 0), np.minimum(big, 31))
    onehot = early[:, EARLY["onehot"]]
    onehot[bucket, np.arange(VEC)] = 1
    onehot[32] = dist < 0
    onehot[33] = dist >= P
    return out, early


def lay_out(a):
    def feature_major(t):
        return np.ascontiguousarray(t.reshape(S, KT, P).transpose(2, 1, 0)).reshape(P, KT * S)

    def cols(v):
        return v.reshape(-1, P).T

    def pair(w):
        return w.reshape(-1, P, w.shape[1]).transpose(1, 0, 2).reshape(P, -1)

    stream = np.zeros((N_SLOTS, P, SLOT), np.float32)
    at = [0]

    def put(block):
        stream[at[0], :, :block.shape[1]] = block
        at[0] += 1

    def dense(w):
        for c in range(0, w.shape[1], COLS):
            put(pair(w[:, c:c + COLS]))

    def ffn(gate, up, down):
        for c in range(0, FF, COLS):
            put(pair(gate[:, c:c + COLS]))
            put(pair(up[:, c:c + COLS]))
        for j in range(FT // 2):
            put(pair(down[2 * j * P:2 * (j + 1) * P]))

    small1 = np.zeros((DEPTH, P, SM1_W), np.float32)
    small2 = np.zeros((DEPTH, P, SM2_W), np.float32)
    for l in range(DEPTH):
        w = a["w_in"][l]
        lx, ly, fq, fk, fv, ff, rq, rk, rv, rg = np.split(w, np.cumsum(
            [256, 256, 512, 512, 512, 8, 256, 256, 256, 256])[:-1], axis=1)
        for part in (fq, fk, rq, rk, rg, lx, ly):
            dense(part)
        f = np.zeros((D, COLS), np.float32)
        f[:, 0:8] = ff
        put(pair(f))
        dense(fv)
        dense(rv)
        for name in ("w_out", "w_cq", "w_ck", "w_cv", "w_co"):
            dense(a[name][l])
        ffn(a["w_gate"][l], a["w_up"][l], a["w_down"][l])
        s = small1[l]
        for name in ("pre_mix", "post_mix", "pre_cross", "post_cross", "pre_ffn", "post_ffn"):
            s[:, SM1[name]] = cols(a[name + "_g"][l])
        s[:, SM1["conv_w"]] = np.concatenate([cols(a["conv_w"][l, n]) for n in range(4)], 1)
        for name, src in (("conv_b", "conv_b"), ("b_rg", "b_rg"), ("b_ig", "b_ig"), ("lam", "lru_lambda")):
            s[:, SM1[name]] = cols(a[src][l])
        s[0:8, SM1["fox_b"]] = a["fox_b_f"][l][:, None]
        for name in ("w_rg", "w_ig"):
            for n in range(4):
                r, o = (n % 2) * HD, SM1[name].start + n * HD
                s[r:r + HD, o:o + HD] = a[name][l, n]
    for l in range(DEPTH):
        ffn(a["ffn1_w_gate_2"][l], a["ffn1_w_up_2"][l], a["ffn1_w_down_2"][l])
        w = a["w_in_2"][l]
        (nq, nkc, nvc, nks, nvs, nkw, nvw, ngate, sq, sk, sv, wq, wk, wv, bgate) = np.split(w, np.cumsum(
            [512, 128, 128, 128, 128, 128, 128, 24, 256, 256, 256, 256, 128, 128, 3072])[:-1], axis=1)
        by_group8 = np.concatenate([np.arange(h * HD, (h + 1) * HD) for t in range(4) for h in (t, t + 4)])
        by_group4 = np.concatenate([np.arange(h * HD, (h + 1) * HD) for t in range(2) for h in (t, t + 2)])
        dense(nq[:, by_group8])
        dense(np.concatenate([nkc, nvc], 1))
        dense(np.concatenate([nks, nkw], 1))
        dense(sq)
        dense(sk)
        dense(wq[:, by_group4])
        dense(np.concatenate([wk, wv], 1))
        dense(np.concatenate([nvs, nvw], 1))
        dense(sv)
        dense(bgate)
        for name in ("nsa_cmp_k_w1_2", "nsa_cmp_v_w1_2"):
            for half in range(2):
                put(pair(a[name][l][half * D:(half + 1) * D]))
        up = np.concatenate([a["w_up_nsa_2"][l][by_group8], a["w_up_sb_2"][l], a["w_up_swa_2"][l][by_group4]], 0)
        dense(up)
        dense(a["w_out_2"][l])
        ffn(a["ffn2_w_gate_2"][l], a["ffn2_w_up_2"][l], a["ffn2_w_down_2"][l])
        s = small2[l]
        for name, src in (("ffn1", "ffn1_norm_2"), ("mix", "mix_norm_2"), ("ffn2", "ffn2_norm_2")):
            s[:, SM2[name]] = cols(a[src][l])
        for name, src in (("nsa_q", "nsa_q_norm_2"), ("nsa_k", "nsa_k_norm_2"), ("swa_q", "swa_q_norm_2"),
                          ("swa_k", "swa_k_norm_2")):
            s[:, SM2[name]] = np.concatenate([a[src][l]] * 2)[:, None]
        s[:, SM2["sinks"]] = a["swa_sinks_2"][l][None, :]
        s[:, SM2["cmp_pos"]] = a["nsa_cmp_pos_2"][l].reshape(16, P).T
        for name, src in (("w2k", "nsa_cmp_k_w2_2"), ("w2v", "nsa_cmp_v_w2_2")):
            s[:, SM2[name]] = pair(a[src][l])
        s[:, SM2["w_gate"]] = pair(ngate)
    assert at[0] == N_SLOTS, (at[0], N_SLOTS)

    con, early = constants()
    con[:, CON["mem_g"]] = cols(a["mem_norm_g"])
    bias = np.zeros((34, 12), np.float32)
    bias[0:32] = a["rel_bias_2"]
    bias[32] = BIG / 8
    bias[33, 8:] = BIG / 8
    return {
        "stream": stream, "x": feature_major(a["x"]), "mem": feature_major(a["mem"]),
        "positions": np.ascontiguousarray(np.broadcast_to(a["positions"].reshape(1, S), (P, S))),
        "rel_bias": bias, "con": con, "early": early, "small1": small1, "small2": small2,
    }


def program(nc, arrays, known, final):
    A = {n: nc.dram_tensor("in_" + n, a.shape, mybir.dt.from_np(a.dtype), kind="ExternalInput").ap()
         for n, a in arrays.items()}
    for n in ("x", "mem"):
        A[n] = A[n].rearrange("p (k s) -> p k s", k=KT)
    A["out"] = nc.dram_tensor("out", (P, KT, S), F32, kind="ExternalOutput").ap()
    A["skew"] = nc.dram_tensor("skew", (P * 12 * VEC,), F32, kind="Internal").ap()
    build(nc, A, known, final)


def kernel(**inputs):
    import concourse.bacc as bacc
    from concourse.bass_utils import run_bass_kernel_spmd

    arrays = lay_out({n: np.asarray(v) for n, v in inputs.items()})
    known = {}
    for final in (False, True):
        nc = bacc.Bacc("TRN2", target_bir_lowering=False, num_devices=1)
        program(nc, arrays, known, final)
    r = run_bass_kernel_spmd(nc, [{"in_" + n: v for n, v in arrays.items()}], core_ids=[0])
    out = r.results[0]["out"].reshape(P, KT, S)
    return np.ascontiguousarray(out.transpose(2, 1, 0)).reshape(1, S, D)
```

```python
from contextlib import ExitStack, contextmanager

import numpy as np

import concourse.bass as bass
from concourse import mybir

F32 = mybir.dt.float32
F32R = mybir.dt.float32r
I32 = mybir.dt.int32
ACT = mybir.ActivationFunctionType
ALU = mybir.AluOpType
AX = mybir.AxisListType

P = 128
D = 1024
KT = D // P
S = 256
ST = S // P
DEPTH = 2
HD = 64
EPS = 1e-6
FF = 2816
FT = FF // P
BIG = -8e30
LOWEST = -3e38
COLS = 256
SLOT = KT * COLS
HK = KT // 2
RING = 4
N_CMP = (S - 32) // 16 + 1
N_CMP0 = (P - 32) // 16 + 1
VEC = 3 * P

B1_SLOTS = 13 + 4 + 4 + 4 + 4 + 4 + 2 * (FF // COLS) + FT // 2
B2_SLOTS = 2 * (2 * (FF // COLS) + FT // 2) + 10 + 12 + 4 + 4 + 4
N_SLOTS = DEPTH * (B1_SLOTS + B2_SLOTS)


def columns(**widths):
    at, out = 0, {}
    for name, w in widths.items():
        out[name] = slice(at, at + w)
        at += w
    return out, at


SM1, SM1_W = columns(pre_mix=KT, post_mix=KT, pre_cross=KT, post_cross=KT, pre_ffn=KT, post_ffn=KT,
                     conv_w=8, conv_b=2, b_rg=2, b_ig=2, lam=2, fox_b=1, w_rg=256, w_ig=256)
SM2, SM2_W = columns(ffn1=KT, mix=KT, ffn2=KT, nsa_q=1, nsa_k=1, swa_q=1, swa_k=1, sinks=4,
                     cmp_pos=16, w2k=128, w2v=128, w_gate=KT * 24)
CON, CON_W = columns(ident=P, blk=P, tri=P, rot=P, causal=S, strict=P, decay=4 * S, strict_add=P, inv_freq=1,
                     late=1, mem_g=KT)
EARLY, EARLY_W = columns(onehot=VEC, nsel=8 * P)


class Counter:

    def __init__(self, loops, name, step=1):
        self.loops, self.name, self.step = loops, name, step
        self.sem = loops.nc.alloc_semaphore(name)
        self.done = 0
        loops.counters.append(self)

    def did(self, instruction):
        instruction.then_inc(self.sem, self.step)
        self.done += self.step
        return self.at(self.done)

    def at(self, value):
        return Mark(self, value, tuple(self.loops.open))

    def now(self):
        return self.at(self.done)


class Mark:

    def __init__(self, counter, value, loops):
        self.counter, self.value, self.loops = counter, value, loops

    def number(self):
        out = self.value
        for loop in self.loops:
            per = loop.adds(self.counter.name)
            if per:
                out = loop.i * per + out
        return out


class Loop:
    def __init__(self, key, known):
        self.key, self.i = key, None
        self.known = known.setdefault(key, {})
        self.found, self.start, self.kept = {}, {}, {}

    def adds(self, name):
        return self.known.get(name, 0)

    def keep(self, label, mark):
        self.found["keep " + label] = mark.value - self.start[mark.counter.name]
        self.kept[label] = mark.counter

    def last(self, label, counter):
        off = self.known.get("keep " + label, 0)
        return counter.at(self.start[counter.name] + off - self.adds(counter.name))


class Loops:

    def __init__(self, nc, known, final):
        self.nc, self.known, self.final = nc, known, final
        self.counters, self.open, self.engines, self.n = [], [], [], 0

    @contextmanager
    def run(self, rounds, engines=mybir.ALL_ENGINES):
        loop = Loop(self.n, self.known)
        self.n += 1
        for c in self.counters:
            loop.start[c.name] = c.done
        for e in self.engines:
            e.passed.clear()
            e.settle()
        with self.nc.Fori(0, rounds, engines=engines) as i:
            loop.i = i
            self.open.append(loop)
            yield loop
            self.open.pop()
        for e in self.engines:
            e.passed.clear()
        for c in self.counters:
            add = c.done - loop.start.get(c.name, 0)
            loop.found[c.name] = add
            c.done = loop.start.get(c.name, 0) + rounds * add
        if self.final:
            assert loop.found == loop.known, f"loop {loop.key} adds otherwise than counted"
        else:
            loop.known.update(loop.found)


class Engine:

    def __init__(self, loops, eng, name):
        self.eng, self.counter, self.passed = eng, Counter(loops, "steps_" + name), {}
        self.settled = loops.nc.alloc_semaphore("settled_" + name)
        loops.engines.append(self)

    def wait(self, *marks):
        for m in marks:
            if m is None:
                continue
            if isinstance(m, (list, tuple)):
                self.wait(*m)
                continue
            key = (m.counter.name, m.loops)
            if m.value <= self.passed.get(key, 0):
                continue
            self.passed[key] = m.value
            self.eng.wait_ge(m.counter.sem, m.number())

    def did(self, instruction):
        return self.counter.did(instruction)

    def settle(self):
        self.eng.sem_inc(self.settled)

    def now(self):
        return self.counter.now()


def build(nc, A, known, final):
    L = Loops(nc, known, final)
    pe, act, dve, pool = (Engine(L, e, n) for e, n in (
        (nc.tensor, "pe"), (nc.scalar, "act"), (nc.vector, "dve"), (nc.gpsimd, "pool")))
    T, AC, V, G = nc.tensor, nc.scalar, nc.vector, nc.gpsimd

    def sb(name, shape, dt=F32):
        return nc.alloc_sbuf_tensor(name, shape, dt)[tuple(slice(None) for _ in shape)]

    def sb_at(name, shape, dt, offset):
        return nc.alloc_sbuf_tensor_at(name, shape, dt, offset=offset)[tuple(slice(None) for _ in shape)]

    base = (nc.sbuf_base + 31) // 32 * 32
    shared = 13 * 2048 + 24 * 1024 + 16384
    nc.alloc_sbuf_tensor("shared", [P, shared // 4 + 16], F32)
    proj = sb_at("proj", [P, 13, 2, COLS], F32, base)
    gates = sb_at("gates", [P, 24, S], F32, base + 13 * 2048)
    hid_hi = sb_at("hid_hi", [P, FT, S], F32R, base)
    hid_lo = sb_at("hid_lo", [P, FT, S], F32R, base + FT * 1024)
    lru_at = [base + 13 * 2048 + n * 2048 for n in range(8)]
    xc, lru_r, lru_i, lru_a, lru_t, lru_u, lru_h, lru_g = (
        sb_at(f"lru{n}", [P, 2, S], F32, at) for n, at in enumerate(lru_at))
    mem_hi = sb_at("mem_hi", [P, KT, S], F32R, base + 13 * 2048 + 24 * 1024)
    mem_lo = sb_at("mem_lo", [P, KT, S], F32R, base + 13 * 2048 + 24 * 1024 + 8192)
    table = sb_at("table", [P, 12, S], F32, base + 13 * 2048 + 24 * 1024)

    raw = [sb(f"raw{r}", [P, HK, COLS]) for r in range(RING)]
    w_hi = [sb(f"w_hi{r}", [P, HK, COLS], F32R) for r in range(RING)]
    w_lo = [sb(f"w_lo{r}", [P, HK, COLS], F32R) for r in range(RING)]
    x = sb("x", [P, KT, S])
    xn = sb("xn", [P, KT, S])
    xn_hi, xn_lo = sb("xn_hi", [P, KT, S], F32R), sb("xn_lo", [P, KT, S], F32R)
    y_hi, y_lo = sb("y_hi", [P, KT, S], F32R), sb("y_lo", [P, KT, S], F32R)
    sq = sb("sq", [P, KT, S])
    con = sb("con", [P, CON_W])
    ones = sb("ones", [P, P])
    ones_row = sb("ones_row", [8, S])
    small = sb("small", [P, max(SM1_W, SM2_W)])
    root, rinv = sb("root", [P, 2, S]), sb("rinv", [P, 2, S])
    act_t = sb("act_t", [P, 2, S])
    logit = [sb(f"logit{i}", [P, 2, 512]) for i in range(2)]
    probT = [sb(f"probT{i}", [P, 2, 512]) for i in range(2)]
    stat = sb("stat", [P, 8, 32])
    f8 = act_t[0:8]
    tbl34 = sb("tbl34", [34, 12])
    avg = sb("avg", [P, P])
    eps_t = sb("eps_t", [P, 2])
    kv_c = sb("kv_c", [P, 16 + 2 * HD])
    rows_8 = sb_at("rows_8", [8, 8 * P], F32, base + 45056)
    cos, sin = (sb_at(n, [P, S], F32, base + 45056 + 4096 + at) for n, at in (("cos", 0), ("sin", 1024)))
    onehot = sb_at("onehot", [34, VEC], F32, lru_at[3])
    c_late, c_early = xn, sq.rearrange("p a s -> p (a s)")[:, 0:8 * P].rearrange("p (h s) -> p h s", h=8)

    bank = [nc.alloc_psum_tensor(f"bank{i}", [P, 512], F32)[:, :] for i in range(8)]
    two = lambda b: b.rearrange("p (a s) -> p a s", a=2)
    dense = [two(bank[0]), two(bank[1])]
    acc = [two(bank[i]) for i in range(2, 6)]
    misc = [two(bank[6]), two(bank[7])]

    def c(name):
        return con[:, CON[name]]

    loaded = [Counter(L, f"loaded{r}", 16) for r in range(RING)]
    used = Counter(L, "halves_used")
    hi_done, lo_done = Counter(L, "halves_hi"), Counter(L, "halves_lo")
    stream = A["stream"]

    def load(n, r):
        nc.sync.dma_start(raw[r], stream[bass.ds(n, 1)].rearrange("o p (k c) -> (o p) k c", k=HK)
                          ).then_inc(loaded[r].sem, 16)

    for r in range(RING):
        load(r, r)
    with nc.Fori(1, 2 * N_SLOTS // RING, engines=[mybir.EngineType.SP]) as i:
        for r in range(RING):
            nc.sync.wait_ge(lo_done.sem, i * RING + (r - RING + 1))
            load(i * RING + r, r)

    def split():
        for _ in range(2):
            m = hi_done.done
            r = m % RING
            loaded[r].done += 16
            free = used.at(m - RING + 1) if m >= RING else None
            act.wait(loaded[r].now(), free)
            hi = hi_done.did(AC.activation(w_hi[r], raw[r], ACT.Copy))
            dve.wait(hi, free)
            lo_done.did(V.tensor_tensor(w_lo[r], raw[r], w_hi[r].bitcast(F32), ALU.subtract))

    def halves(ahead=True):
        if hi_done.done == used.done:
            split()
        if ahead:
            split()
        for half in range(2):
            m = used.done
            pe.wait(lo_done.at(m + 1))
            yield half, m % RING
            assert used.done == m + 1

    def products(out, lhs, rhs, first):
        for j, (a, b) in enumerate([(lhs[0], rhs[0]), (lhs[0], rhs[1]), (lhs[1], rhs[0])]):
            m = T.matmul(out, a, b, start=first and j == 0, stop=True, skip_group_check=True)
        return m

    def tile(r, k, cols):
        return [t[r][:, k, cols] for t in (w_hi, w_lo)]

    def slot_T(out, hi, lo, ahead=True, cts=(0, 1)):
        for half, r in halves(ahead):
            for ct in cts:
                for k in range(HK):
                    m = products(out[:, ct, :], tile(r, k, slice(ct * P, (ct + 1) * P)),
                                 [t[:, half * HK + k, :] for t in (hi, lo)], half == 0 and k == 0 and ct == cts[0])
            got = used.did(m)
        return got

    def slot_rows(out, hi, lo, ahead=True):
        for half, r in halves(ahead):
            for rt in range(ST):
                for k in range(HK):
                    m = products(out[:, rt, :], [t[:, half * HK + k, rt * P:(rt + 1) * P] for t in (hi, lo)],
                                 tile(r, k, slice(0, COLS)), half == 0 and k == 0 and rt == 0)
            got = used.did(m)
        return got

    got_con, got_x, got_small = Counter(L, "got_con", 16), Counter(L, "got_x", 16), Counter(L, "got_small", 16)
    got_con.did(G.dma_start(rows_8, A["early"][0:8, EARLY["nsel"]]))
    got_con.did(G.dma_start(onehot, A["early"][0:34, EARLY["onehot"]]))
    con_in = got_con.did(G.dma_start(con, A["con"]))
    x_in = got_x.did(G.dma_start(x, A["x"]))
    got_mem = Counter(L, "got_mem", 16)
    mem_in = got_mem.did(G.dma_start(xn, A["mem"]))
    got_pos = Counter(L, "got_pos", 16)
    pos_raw = stat.rearrange("p a b -> p (a b)").bitcast(I32)
    pos_in = got_pos.did(G.dma_start(pos_raw, A["positions"]))
    got_bias = Counter(L, "got_bias", 16)
    bias_in = got_bias.did(G.dma_start(tbl34, A["rel_bias"]))
    ones_set = pool.did(G.memset(ones, 1.0))
    avg_set = pool.did(G.memset(avg, 1.0 / D))
    row_set = pool.did(G.memset(ones_row, 1.0))

    bcast = sb_at("bcast", [34, 12, P], F32, lru_at[0])
    dve.wait(bias_in, ones_set)
    for h in range(12):
        m = dve.did(V.tensor_scalar(bcast[:, h, :], ones[0:34, :], tbl34[:, h:h + 1], 8.0, ALU.mult, ALU.mult))
    pe.wait(con_in, m)
    wrote_vec = Counter(L, "wrote_vec", 16)
    vec_sb = sb_at("vec_sb", [P, 12, VEC], F32, base)
    vec_out = {}
    for h in range(12):
        pe.wait(vec_out.get(h - 2))
        m = pe.did(T.matmul(bank[h % 2][:, 0:VEC], bcast[:, h, :], onehot, start=True, stop=True))
        dve.wait(m)
        vec_out[h] = dve.did(V.tensor_copy(vec_sb[:, h, :], bank[h % 2][:, 0:VEC]))
    pool.wait(vec_out[11])
    skew_out = wrote_vec.did(G.dma_start(A["skew"].rearrange("(p h v) -> p h v", h=12, v=VEC), vec_sb))

    def mean_square(src_of, n_src, out, after, also=None):
        sums = None
        for b in range(n_src):
            act.wait(after[b])
            s = act.did(AC.activation(sq[:, 2 * b:2 * b + 2, :], src_of(b), ACT.Square))
            pe.wait(s)
            for k in (2 * b, 2 * b + 1):
                sums = T.matmul(out, avg, sq[:, k, :], start=k == 0, stop=k == KT - 1)
        return pe.did(sums)

    def inverse_root(src, w, ready):
        act.wait(ready)
        m = act.did(AC.activation(root_f[:, 0:w], src, ACT.Sqrt, bias=eps))
        dve.wait(m)
        return dve.did(V.reciprocal(rinv_f[:, 0:w], root_f[:, 0:w]))

    root_f = root.rearrange("p a s -> p (a s)")
    rinv_f = rinv.rearrange("p a s -> p (a s)")
    pool.did(G.memset(eps_t[:, 0:1], EPS))
    eps_set = pool.did(G.memset(eps_t[:, 1:2], 1.0))
    eps, one = eps_t[:, 0:1], eps_t[:, 1:2]

    def norm_in(src, gain, hi, lo, src_ready, free):
        ms = mean_square(lambda b: src[:, 2 * b:2 * b + 2, :], 4, misc[0][:, 0, :], [src_ready] * 4)
        r = inverse_root(misc[0][:, 0, :], S, ms)
        dve.wait(free, r)
        act.wait(free)
        marks = []
        for b in range(4):
            for k in (2 * b, 2 * b + 1):
                n = dve.did(V.scalar_tensor_tensor(xn[:, k, :], src[:, k, :], gain[:, k:k + 1], rinv[:, 0, :],
                                                   ALU.mult, ALU.mult))
            pair = slice(2 * b, 2 * b + 2)
            act.wait(n)
            h = act.did(AC.activation(hi[:, pair, :], xn[:, pair, :], ACT.Copy))
            dve.wait(h)
            marks.append(dve.did(V.tensor_tensor(lo[:, pair, :], xn[:, pair, :], hi[:, pair, :].bitcast(F32),
                                                 ALU.subtract)))
        return marks[-1]

    def norm_add(gain, ready):
        ms = mean_square(lambda b: acc[b], 4, misc[0][:, 0, :], ready)
        r = inverse_root(misc[0][:, 0, :], S, ms)
        dve.wait(r)
        for k in range(KT):
            n = dve.did(V.scalar_tensor_tensor(sq[:, k, :], acc[k // 2][:, k % 2, :], gain[:, k:k + 1],
                                               rinv[:, 0, :], ALU.mult, ALU.mult))
        dve.wait(n)
        return dve.did(V.tensor_tensor(x, x, sq, ALU.add))

    def split_out(hi, lo, psum, ready):
        act.wait(ready)
        h = act.did(AC.activation(hi, psum, ACT.Copy))
        dve.wait(h)
        return dve.did(V.tensor_tensor(lo, psum, hi.bitcast(F32), ALU.subtract))

    def ffn(hi, lo, ready, last_ahead):
        pe.wait(ready)
        act.wait(pe.now(), dve.now(), act.now())
        dve.wait(pe.now(), act.now())
        pe.wait(act.now(), dve.now())
        with L.run(FF // COLS) as loop:
            j = loop.i
            pe.wait(loop.last("silu", act.counter))
            up_free = loop.last("up", dve.counter)
            gate = slot_T(dense[0], hi, lo)
            act.wait(gate, up_free)
            silu = act.did(AC.activation(act_t, dense[0], ACT.Silu))
            loop.keep("silu", silu)
            pe.wait(up_free)
            up = slot_T(dense[1], hi, lo)
            dve.wait(up, silu)
            h = dve.did(V.tensor_tensor(act_t, act_t, dense[1], ALU.mult))
            act.wait(h)
            hh = act.did(AC.activation(hid_hi[:, bass.ds(j * 2, 2), :], act_t, ACT.Copy))
            dve.wait(hh)
            low = dve.did(V.tensor_tensor(hid_lo[:, bass.ds(j * 2, 2), :], act_t,
                                          hid_hi[:, bass.ds(j * 2, 2), :].bitcast(F32), ALU.subtract))
            loop.keep("up", low)
        pe.wait(dve.now(), act.now())

        def down(j, start, ahead=True):
            for k, r in halves(ahead):
                for ct in range(KT):
                    w = [t[r].rearrange("p k c -> p (k c)")[:, ct * P:(ct + 1) * P] for t in (w_hi, w_lo)]
                    h = [t[:, bass.ds(j * 2 + k, 1), :].rearrange("p o s -> p (o s)") for t in (hid_hi, hid_lo)]
                    m = products(acc[ct // 2][:, ct % 2, :], w, h, start and k == 0 and ct % 2 == 0)
                got = used.did(m)
            return got

        n = FT // 2
        down(0, True)
        with L.run((n - 3) // 2) as loop:
            down(loop.i * 2 + 1, False)
            down(loop.i * 2 + 2, False)
        down(n - 2, False)
        return [down(n - 1, False, last_ahead)] * 4

    def out_projection(hi, lo, ready, first_free):
        pe.wait(ready, first_free)
        return [slot_T(acc[b], hi, lo) for b in range(4)]

    mem_g = c("mem_g")
    act.wait(mem_in, eps_set, con_in)
    dve.wait(con_in)
    pe.wait(avg_set)
    ms = mean_square(lambda b: xn[:, 2 * b:2 * b + 2, :], 4, misc[0][:, 0, :], [mem_in] * 4)
    r = inverse_root(misc[0][:, 0, :], S, ms)
    dve.wait(r, mem_in)
    for b in range(4):
        for k in (2 * b, 2 * b + 1):
            n = dve.did(V.scalar_tensor_tensor(xn[:, k, :], xn[:, k, :], mem_g[:, k:k + 1], rinv[:, 0, :],
                                               ALU.mult, ALU.mult))
        pair = slice(2 * b, 2 * b + 2)
        act.wait(n)
        h = act.did(AC.activation(mem_hi[:, pair, :], xn[:, pair, :], ACT.Copy))
        dve.wait(h)
        mem_ready = dve.did(V.tensor_tensor(mem_lo[:, pair, :], xn[:, pair, :], mem_hi[:, pair, :].bitcast(F32),
                                            ALU.subtract))

    TWO_PI = 2 * np.pi
    C1 = 6.28125
    C2 = float((np.array([TWO_PI - C1], np.float32).view(np.uint32) & np.uint32(0xfffff000)).view(np.float32)[0])
    C3 = float(TWO_PI - C1 - C2)
    MAGIC = 1.5 * 2.0 ** 23
    posf, ang, turn, red = (logit[1][:, n // 2, (n % 2) * S:(n % 2 + 1) * S] for n in range(4))
    dve.wait(pos_in)
    p0 = dve.did(V.tensor_copy(posf, pos_raw))
    dve.wait(p0)
    p0 = dve.did(V.tensor_scalar(ang, posf, c("inv_freq"), None, ALU.mult))
    dve.wait(p0)
    for out, quarter in ((sin, 0.0), (cos, 0.25)):
        m = dve.did(V.tensor_scalar(turn, ang, 1.0 / TWO_PI, quarter, ALU.mult, ALU.add))
        for k in (MAGIC, -MAGIC):
            dve.wait(m)
            m = dve.did(V.tensor_scalar(turn, turn, k, None, ALU.add))
        dve.wait(m)
        m = dve.did(V.scalar_tensor_tensor(red, turn, -C1, ang, ALU.mult, ALU.add))
        for k in (C2, C3):
            dve.wait(m)
            m = dve.did(V.scalar_tensor_tensor(red, turn, -k, red, ALU.mult, ALU.add))
        dve.wait(m)
        m = dve.did(V.tensor_scalar(red, red, quarter * TWO_PI, float(np.float32(3.1415925)), ALU.add, ALU.min))
        dve.wait(m)
        m = dve.did(V.tensor_scalar(red, red, -float(np.float32(3.1415925)), None, ALU.max))
        act.wait(m)
        trig = act.did(AC.activation(out, red, ACT.Sin))
        dve.wait(trig)


    def causal_values(out, v_of, pT, first=True, last=True):
        T.matmul(out, v_of(0), pT[:, 0:S], start=first, stop=False, skip_group_check=True)
        return T.matmul(out[:, P:S], v_of(1), pT[:, S:S + P], start=False, stop=last, skip_group_check=True)

    def slot_of(t, n):
        return t[:, bass.ds(n, 1), :, :].rearrange("p o a s -> p (o a) s")

    def head_rows(h):
        return slice((h % 2) * HD, (h % 2 + 1) * HD)

    act.wait(skew_out)
    with L.run(DEPTH) as layer:
        l = layer.i
        sm = lambda name: small[:, SM1[name]]
        pool.wait(pe.now(), act.now(), dve.now())
        small_in = got_small.did(G.dma_start(small[:, 0:SM1_W], A["small1"][bass.ds(l, 1)].rearrange("o p c -> (o p) c")))
        for e in (dve, act, pe):
            e.wait(small_in, pe.now(), act.now(), dve.now(), pool.now())
        split()
        ready = norm_in(x, sm("pre_mix"), xn_hi, xn_lo, x_in, None)

        pe.wait(ready)
        with L.run(4) as loop:
            for r in range(2):
                pe.wait(loop.last(f"out{r}", act.counter))
                got = slot_T(dense[r], xn_hi, xn_lo)
                act.wait(got)
                loop.keep(f"out{r}", act.did(AC.activation(slot_of(proj, loop.i * 2 + r), dense[r], ACT.Copy)))
        pe.wait(act.now())
        got = slot_T(dense[0], xn_hi, xn_lo)
        act.wait(got)
        ly_done = act.did(AC.activation(proj[:, 8, :, :], dense[0], ACT.Copy))
        forget = slot_T(dense[1], xn_hi, xn_lo, cts=(0,))
        pe.wait(ly_done)
        got = slot_rows(dense[0], xn_hi, xn_lo)
        act.wait(got)
        v0_done = act.did(AC.activation(proj[:, 10, :, :], dense[0], ACT.Copy))

        dve.wait(forget)
        z = dve.did(V.tensor_scalar(f8[:, 0, :], dense[1][0:8, 0, :], small[0:8, SM1["fox_b"]], 0.0, ALU.add, ALU.min))
        act.wait(forget, z)
        a = act.did(AC.activation(f8[:, 1, :], dense[1][0:8, 0, :], ACT.Abs, bias=small[0:8, SM1["fox_b"]]))
        act.wait(a)
        a = act.did(AC.activation(f8[:, 1, :], f8[:, 1, :], ACT.Exp, scale=-1.0))
        act.wait(a)
        a = act.did(AC.activation(f8[:, 1, :], f8[:, 1, :], ACT.Ln, bias=one[0:8]))
        dve.wait(z, a)
        m = dve.did(V.tensor_tensor(f8[:, 0, :], f8[:, 0, :], f8[:, 1, :], ALU.subtract))
        dve.wait(m)
        m = dve.did(V.tensor_tensor_scan(f8[:, 1, :], ones_row, f8[:, 0, :], 0.0, ALU.mult, ALU.add))
        dve.wait(m)
        c_ready = dve.did(V.tensor_scalar(f8[:, 1, :], f8[:, 1, :], 8.0, None, ALU.mult))

        pe.wait(c_ready)
        got = slot_rows(dense[1], xn_hi, xn_lo)
        act.wait(got)
        v1_done = act.did(AC.activation(proj[:, 11, :, :], dense[1], ACT.Copy))
        pe.wait(v0_done)
        got = slot_rows(dense[0], xn_hi, xn_lo)
        act.wait(got)
        rv_done = act.did(AC.activation(proj[:, 12, :, :], dense[0], ACT.Copy))
        pe.wait(v1_done, rv_done)

        lx, ly = proj[:, 7, :, :], proj[:, 8, :, :]
        dve.wait(ly_done)
        for ct in range(2):
            w = lambda n: small[:, SM1["conv_w"].start + 2 * n + ct:SM1["conv_w"].start + 2 * n + ct + 1]
            m = dve.did(V.tensor_scalar(xc[:, ct, :], lx[:, ct, :], w(3), sm("conv_b")[:, ct:ct + 1], ALU.mult, ALU.add))
            for n in (2, 1, 0):
                back = 3 - n
                dve.wait(m)
                m = dve.did(V.scalar_tensor_tensor(xc[:, ct, back:S], lx[:, ct, 0:S - back], w(n), xc[:, ct, back:S],
                                                   ALU.mult, ALU.add))
        xc_done = m
        pe.wait(xc_done)
        for dst, name in ((misc[0], "w_rg"), (misc[1], "w_ig")):
            for ct in range(2):
                m = T.matmul(dst[:, ct, :], sm(name)[:, ct * P:(ct + 1) * P], xc[:, ct, :], start=True, stop=True)
        gated = pe.did(m)
        act.wait(gated)
        for dst, src, b in ((lru_r, misc[0], "b_rg"), (lru_i, misc[1], "b_ig")):
            for ct in range(2):
                m = act.did(AC.activation(dst[:, ct, :], src[:, ct, :], ACT.Sigmoid, bias=sm(b)[:, ct:ct + 1]))
        st = lambda n, w=2: stat[:, n, 0:w]
        a = act.did(AC.activation(st(0), sm("lam"), ACT.Abs))
        act.wait(a)
        a = act.did(AC.activation(st(0), st(0), ACT.Exp, scale=-1.0))
        act.wait(a)
        a = act.did(AC.activation(st(0), st(0), ACT.Ln, bias=one))
        sp0 = dve.did(V.tensor_scalar(st(1), sm("lam"), -1.0, 0.0, ALU.mult, ALU.max))
        dve.wait(sp0, a)
        sp0 = dve.did(V.tensor_tensor(st(1), st(1), st(0), ALU.add))
        dve.wait(sp0)
        dve.did(V.tensor_scalar(st(2), st(1), -8.0, None, ALU.mult))
        sp = dve.did(V.tensor_scalar(st(3), st(1), 8.0, None, ALU.mult))
        act.wait(m, sp)
        for ct in range(2):
            ea = act.did(AC.activation(lru_a[:, ct, :], lru_r[:, ct, :], ACT.Exp, scale=stat[:, 2, ct:ct + 1]))
            act.wait(ea)
            th = act.did(AC.activation(lru_t[:, ct, :], lru_r[:, ct, :], ACT.Tanh, scale=stat[:, 3, ct:ct + 1]))
        dve.wait(th)
        m = dve.did(V.tensor_tensor(lru_u, lru_a, lru_a, ALU.mult))
        dve.wait(m)
        m = dve.did(V.scalar_tensor_tensor(lru_u, lru_u, 1.0, lru_t, ALU.add, ALU.mult))
        act.wait(m)
        m = act.did(AC.activation(lru_u, lru_u, ACT.Sqrt))
        g = act.did(AC.activation(lru_g, ly, ACT.Gelu_apprx_tanh))
        m2 = dve.did(V.tensor_tensor(lru_i, lru_i, xc, ALU.mult))
        dve.wait(m, m2)
        m = dve.did(V.tensor_tensor(lru_u, lru_u, lru_i, ALU.mult))
        dve.wait(m)
        for ct in range(2):
            m = dve.did(V.tensor_tensor_scan(lru_h[:, ct, :], lru_a[:, ct, :], lru_u[:, ct, :], 0.0, ALU.mult, ALU.add))
        dve.wait(m, g)
        m = dve.did(V.tensor_tensor(lru_h, lru_h, lru_g, ALU.mult))
        split_out(y_hi[:, 0:2, :], y_lo[:, 0:2, :], lru_h, m)

        pe.wait(c_ready)
        read = {}
        for h in range(8):
            pe.wait(read.get(h - 2))
            nsel = rows_8[:, h * P:(h + 1) * P]
            m = pe.did(T.matmul(acc[2 + h % 2][:, 0, :], nsel, f8[:, 1, :], start=True, stop=True))
            dve.wait(m)
            dve.did(V.tensor_tensor(c_late[:, h, :], acc[2 + h % 2][:, 0, :], c("causal"), ALU.add))
            read[h] = dve.did(V.tensor_tensor(c_early[:, h, :], acc[2 + h % 2][:, 0, 0:P],
                                              c("causal")[:, P:S], ALU.add))

        def fox_scores(h):
            q, k = proj[head_rows(h), h // 4, (h // 2) % 2, :], proj[head_rows(h), 2 + h // 4, (h // 2) % 2, :]
            out = acc[h % 2].rearrange("p a s -> p (a s)")
            pe.wait(scored.get(h - 2))
            for rt, cols, nk in ((1, slice(0, S), S), (0, slice(S, S + P), P)):
                m = T.matmul(out[:, cols], q[:, rt * P:(rt + 1) * P], k[:, 0:nk], start=True, stop=True)
            return pe.did(m)

        def fox_softmax(h, ready):
            src = acc[h % 2].rearrange("p a s -> p (a s)")
            lg = logit[h % 2][:, 0, :]
            s4 = stat[:, 0:4, 16 + 2 * (h % 2):18 + 2 * (h % 2)]
            dve.wait(ready, transposed.get(h - 2))
            dve.settle()
            dve.did(V.tensor_tensor_reduce(lg[:, 0:S], src[:, 0:S], c_late[:, h, :], 1.0, LOWEST, ALU.add, ALU.max, s4[:, 0, 0:1]))
            m = dve.did(V.tensor_tensor_reduce(lg[:, S:S + P], src[:, S:S + P], c_early[:, h, :], 1.0, LOWEST,
                                               ALU.add, ALU.max, s4[:, 0, 1:2]))
            scored[h] = m
            dve.wait(m)
            m = dve.did(V.tensor_scalar(s4[:, 1, :], s4[:, 0, :], -0.125, None, ALU.mult))
            act.wait(m)
            act.did(AC.activation(lg[:, 0:S], lg[:, 0:S], ACT.Exp, bias=s4[:, 1, 0:1], scale=0.125,
                                  accum_out=s4[:, 2, 0:1]))
            m = act.did(AC.activation(lg[:, S:S + P], lg[:, S:S + P], ACT.Exp, bias=s4[:, 1, 1:2], scale=0.125,
                                      accum_out=s4[:, 2, 1:2]))
            dve.wait(m)
            m = dve.did(V.reciprocal(s4[:, 3, :], s4[:, 2, :]))
            dve.wait(m)
            dve.did(V.tensor_scalar(lg[:, 0:S], lg[:, 0:S], s4[:, 3, 0:1], None, ALU.mult))
            return dve.did(V.tensor_scalar(lg[:, S:S + P], lg[:, S:S + P], s4[:, 3, 1:2], None, ALU.mult))

        def causal_transpose(n, lg, dst_bank, dst, ready, free):
            pe.wait(ready, free)
            for to, frm in ((0, S), (1, 0), (2, P)):
                m = T.transpose(dst_bank[:, to * P:(to + 1) * P], lg[:, frm:frm + P], c("ident"))
            m = pe.did(m)
            transposed[n] = m
            act.wait(m, free)
            return act.did(AC.activation(dst[:, 0:384], dst_bank[:, 0:384], ACT.Copy))

        scored, transposed, valued, ysplit, probs, pTs = {}, {}, {}, {}, {}, {}
        for n in range(8 + 2):
            if n < 8:
                s = fox_scores(n)
                probs[n] = fox_softmax(n, s)
            if 1 <= n < 9:
                h = n - 1
                pTs[h] = causal_transpose(h, logit[h % 2][:, 0, :], bank[4 + h % 2], probT[h % 2][:, 0, :],
                                          probs[h], valued.get(h - 2))
            if n >= 2:
                h = n - 2
                o = misc[(h // 2) % 2][:, 0, :]
                pe.wait(pTs[h], ysplit.get(h // 2 - 2))
                v = lambda kt: proj[:, 10 + h // 4, kt, (h % 4) * HD:(h % 4 + 1) * HD]
                valued[h] = pe.did(causal_values(o[head_rows(h), :], v, probT[h % 2][:, 0, :]))
                if h % 2:
                    ysplit[h // 2] = split_out(y_hi[:, 2 + h // 2, :], y_lo[:, 2 + h // 2, :], o, valued[h])
        fox_done = ysplit[3]

        rq, rk, rg = proj[:, 4, :, :], proj[:, 5, :, :], proj[:, 6, :, :]
        pe.wait(fox_done)
        rot_done = []
        for n, src in enumerate((rq, rk)):
            m = pe.did(T.matmul(misc[n].rearrange("p a s -> p (a s)"), c("rot"), src.rearrange("p a s -> p (a s)"),
                                start=True, stop=True))
            dve.wait(m)
            dst = (lru_a, lru_t)[n]
            other = (lru_u, lru_h)[n]
            dve.wait(act.now())
            a1 = dve.did(V.tensor_tensor(dst, src, cos.unsqueeze(1).broadcast_to([P, 2, S]), ALU.mult))
            a2 = dve.did(V.tensor_tensor(other, misc[n], sin.unsqueeze(1).broadcast_to([P, 2, S]), ALU.mult))
            dve.wait(a2)
            rot_done.append(dve.did(V.tensor_tensor(dst, dst, other, ALU.add)))
        pe.wait(rot_done[1])
        read = {}
        for h in range(4):
            q, k = lru_a[head_rows(h), h // 2, :], lru_t[head_rows(h), h // 2, :]
            b = acc[h % 2].rearrange("p a s -> p (a s)")
            pe.wait(read.get(h - 2))
            T.matmul(b[:, 0:S], k[:, 0:P], q[:, :], start=True, stop=True)
            m = pe.did(T.matmul(b[:, S:S + P], k[:, P:S], q[:, P:S], start=True, stop=True))
            dve.wait(m, read.get(("v", h - 2)))
            dec = con[:, CON["decay"].start + h * S:CON["decay"].start + (h + 1) * S]
            dve.did(V.tensor_tensor(probT[h % 2][:, 0, 0:S], b[:, 0:S], dec, ALU.mult))
            read[h] = dve.did(V.tensor_tensor(probT[h % 2][:, 0, S:S + P], b[:, S:S + P], dec[:, 0:P], ALU.mult))
            pe.wait(read[h])
            v = lambda kt: proj[:, 12, kt, h * HD:(h + 1) * HD]
            read[("v", h)] = pe.did(causal_values(acc[2 + h // 2][head_rows(h), 0, :], v, probT[h % 2][:, 0, :]))
        yr = lru_u
        act.wait(read[("v", 3)])
        for t in range(2):
            m = act.did(AC.activation(yr[:, t, :], acc[2 + t][:, 0, :], ACT.Copy))
        pe.wait(m)
        mean = pe.did(T.matmul(bank[6], c("blk"), yr.rearrange("p a s -> p (a s)"), start=True, stop=True))
        dve.wait(mean)
        m = dve.did(V.tensor_tensor(yr, yr, misc[0], ALU.subtract))
        act.wait(m)
        m = act.did(AC.activation(lru_h, yr, ACT.Square))
        pe.wait(m)
        var = pe.did(T.matmul(bank[7], c("blk"), lru_h.rearrange("p a s -> p (a s)"), start=True, stop=True))
        r = inverse_root(bank[7], 512, var)
        sg = act.did(AC.activation(lru_g, rg, ACT.Silu))
        dve.wait(r)
        m = dve.did(V.tensor_tensor(yr, yr, rinv, ALU.mult))
        dve.wait(m, sg)
        m = dve.did(V.tensor_tensor(yr, yr, lru_g, ALU.mult))
        ret_done = split_out(y_hi[:, 6:8, :], y_lo[:, 6:8, :], yr, m)

        got = out_projection(y_hi, y_lo, ret_done, None)
        x_ready = norm_add(sm("post_mix"), got)

        ready = norm_in(x, sm("pre_cross"), xn_hi, xn_lo, x_ready, None)
        pe.wait(ready, mem_ready)
        for form, first, hi, lo in ((slot_T, 0, xn_hi, xn_lo), (slot_T, 4, mem_hi, mem_lo), (slot_rows, 8, mem_hi, mem_lo)):
            with L.run(2) as loop:
                for r in range(2):
                    pe.wait(loop.last(f"out{r}", act.counter))
                    got = form(dense[r], hi, lo)
                    act.wait(got)
                    loop.keep(f"out{r}", act.did(AC.activation(slot_of(proj, loop.i * 2 + (r + first)),
                                                               dense[r], ACT.Copy)))
            pe.wait(act.now())
        scored, transposed, valued, ysplit, probs, pTs = {}, {}, {}, {}, {}, {}
        for n in range(4 + 2):
            if n < 4:
                h = n
                pe.wait(scored.get(h - 2))
                for rt in range(2):
                    for dt in range(2):
                        m = T.matmul(acc[h % 2][:, rt, :], proj[:, h, dt, rt * P:(rt + 1) * P], proj[:, 4 + h, dt, :],
                                     start=dt == 0, stop=dt == 1)
                m = pe.did(m)
                s4 = stat[:, 0:4, 16 + 2 * (h % 2):18 + 2 * (h % 2)]
                dve.wait(m, scored.get(h - 2))
                m = dve.did(V.tensor_reduce(s4[:, 0, :], acc[h % 2], AX.X, ALU.max))
                dve.wait(m)
                m = dve.did(V.tensor_scalar(s4[:, 1, :], s4[:, 0, :], -0.0625, None, ALU.mult))
                act.wait(m, transposed.get(h - 2))
                for rt in range(2):
                    m = act.did(AC.activation(logit[h % 2][:, 0, rt * S:(rt + 1) * S], acc[h % 2][:, rt, :], ACT.Exp,
                                              bias=s4[:, 1, rt:rt + 1], scale=0.0625, accum_out=s4[:, 2, rt:rt + 1]))
                scored[h] = m
                dve.wait(m)
                m = dve.did(V.reciprocal(s4[:, 3, :], s4[:, 2, :]))
                dve.wait(m)
                for rt in range(2):
                    probs[h] = dve.did(V.tensor_scalar(logit[h % 2][:, 0, rt * S:(rt + 1) * S],
                                                       logit[h % 2][:, 0, rt * S:(rt + 1) * S],
                                                       s4[:, 3, rt:rt + 1], None, ALU.mult))
            if 1 <= n < 5:
                h = n - 1
                pe.wait(probs[h], pTs.get(h - 1))
                for kt in range(2):
                    for rt in range(2):
                        m = T.transpose(bank[4 + h % 2][:, kt * S + rt * P:kt * S + (rt + 1) * P],
                                        logit[h % 2][:, 0, rt * S + kt * P:rt * S + (kt + 1) * P], c("ident"))
                transposed[h] = pe.did(m)
                act.wait(transposed[h], valued.get(h - 2))
                pTs[h] = act.did(AC.activation(probT[h % 2][:, 0, :], bank[4 + h % 2], ACT.Copy))
            if n >= 2:
                h = n - 2
                pe.wait(pTs[h], ysplit.get(h - 2))
                for dt in range(2):
                    for kt in range(2):
                        m = T.matmul(misc[h % 2][:, dt, :], proj[:, 8 + h, kt, dt * P:(dt + 1) * P],
                                     probT[h % 2][:, 0, kt * S:(kt + 1) * S], start=kt == 0, stop=kt == 1)
                valued[h] = pe.did(m)
                ysplit[h] = split_out(y_hi[:, 2 * h:2 * h + 2, :], y_lo[:, 2 * h:2 * h + 2, :], misc[h % 2], valued[h])
        got = out_projection(y_hi, y_lo, ysplit[3], None)
        x_ready = norm_add(sm("post_cross"), got)

        ready = norm_in(x, sm("pre_ffn"), xn_hi, xn_lo, x_ready, None)
        got = ffn(xn_hi, xn_lo, ready, False)
        x_ready = norm_add(sm("post_ffn"), got)

    got_table = Counter(L, "got_table", 16)
    pool.wait(skew_out, pe.now())
    by_row = A["skew"][P - 1:P - 1 + P * (12 * VEC - 1)].rearrange("(p v) -> p v", v=12 * VEC - 1)
    got_table.did(G.dma_start(table[:, 0:11, :], by_row[:, 0:11 * VEC].rearrange("p (h v) -> p h v", v=VEC)[:, :, 0:S]))
    table_in = got_table.did(G.dma_start(table[:, 11, :], by_row[:, 11 * VEC:11 * VEC + S]))

    got_y2 = x_ready
    with L.run(DEPTH) as layer:
        l = layer.i
        sm = lambda name: small[:, SM2[name]]
        pool.wait(pe.now(), act.now(), dve.now())
        small_in = got_small.did(G.dma_start(small[:, 0:SM2_W], A["small2"][bass.ds(l, 1)].rearrange("o p c -> (o p) c")))
        for e in (dve, act, pe):
            e.wait(small_in, pe.now(), act.now(), dve.now(), pool.now(), table_in)
        split()

        def half_ffn(gain, x_ready, last_ahead):
            ready = norm_in(x, gain, xn_hi, xn_lo, x_ready, None)
            got = ffn(xn_hi, xn_lo, ready, last_ahead)
            dve.wait(got)
            for b in range(4):
                m = dve.did(V.scalar_tensor_tensor(x[:, 2 * b:2 * b + 2, :], acc[b], 0.5, x[:, 2 * b:2 * b + 2, :],
                                                   ALU.mult, ALU.add))
            return m

        x_ready = half_ffn(sm("ffn1"), None, True)
        ready = norm_in(x, sm("mix"), xn_hi, xn_lo, x_ready, pe.now())

        pe.wait(ready, act.now(), dve.now())
        act.wait(pe.now(), dve.now())
        with L.run(2) as loop:
            for r in range(2):
                pe.wait(loop.last(f"out{r}", act.counter))
                got = slot_T(dense[r], xn_hi, xn_lo)
                act.wait(got)
                loop.keep(f"out{r}", act.did(AC.activation(slot_of(proj, loop.i * 2 + r), dense[r], ACT.Copy)))
        free = {0: act.now(), 1: act.now()}
        slots_out = {}

        def project(slot, form=slot_T):
            r = slot % 2
            pe.wait(free[r])
            got = form(dense[r], xn_hi, xn_lo)
            act.wait(got)
            slots_out[slot] = free[r] = act.did(AC.activation(proj[:, slot, :, :], dense[r], ACT.Copy))

        def swa_kv(out, hi, lo):
            for half, r in halves():
                for k in range(HK):
                    a = [t[:, half * HK + k, :] for t in (hi, lo)]
                    products(out[:, 0, :], tile(r, k, slice(0, P)), a, half == 0 and k == 0)
                    for rt in range(ST):
                        mm = products(out[:, 1, rt * P:(rt + 1) * P], [t[:, rt * P:(rt + 1) * P] for t in a],
                                      tile(r, k, slice(P, 2 * P)), False)
                got = used.did(mm)
            return got

        norm_n = [0]
        root_read = [None, None]

        def squares(tiles, ready):
            n, w = norm_n[0], tiles.shape[1]
            norm_n[0] += 1
            dst = sq[:, 2 * (n % 4):2 * (n % 4) + w, :]
            act.wait(ready, squares_read.get(n - 4))
            return n, act.did(AC.activation(dst, tiles, ACT.Square))

        squares_read, roots_read = {}, {}

        def head_norm(tiles, gain, squared):
            n, m = squared
            w = tiles.shape[1]
            b = bank[4 + n % 2]
            pe.wait(m, roots_read.get(n - 2))
            squares_read[n] = m = pe.did(T.matmul(
                b[:, 0:w * S], c("blk"), sq[:, 2 * (n % 4):2 * (n % 4) + w, :].rearrange("p a s -> p (a s)"),
                start=True, stop=True))
            act.wait(m, root_read[0])
            roots_read[n] = m = act.did(AC.activation(root_f[:, 0:w * S], b[:, 0:w * S], ACT.Sqrt, bias=eps))
            dve.wait(m, root_read[1])
            root_read[0] = m = dve.did(V.reciprocal(rinv_f[:, 0:w * S], root_f[:, 0:w * S]))
            dve.wait(m)
            root_read[1] = dve.did(V.scalar_tensor_tensor(tiles, tiles, gain, rinv[:, 0:w, :], ALU.mult, ALU.mult))
            return root_read[1]

        cmp_w = 2 * N_CMP
        blocks = act_t.rearrange("p a s -> p (a s)")[:, 0:16 * cmp_w].rearrange("p (t n) -> p t n", n=cmp_w)
        hid_c = [logit[1][:, 0, 64 * n:64 * n + 2 * cmp_w].rearrange("p (t n) -> p t n", n=cmp_w) for n in range(2)]
        k_root = logit[1][:, 0, 256:256 + N_CMP]
        kc = kv_c[:, 0:N_CMP]
        vc = kv_c[0:N_CMP, 16:16 + 2 * HD]
        parts = {}

        def cmp_parts(which):
            return [t[:, 2 * which:2 * which + 2, :].rearrange("p a s -> p (a s)")[:, 0:16 * cmp_w]
                    .rearrange("p (t n) -> p t n", n=cmp_w) for t in (y_hi, y_lo)]

        def cmp_blocks(which, ready):
            src = proj[:, 3, which, :]
            dve.wait(ready, parts.get(0))
            for g in range(2):
                for par in range(2):
                    rs, ps_ = slice(par * HD, (par + 1) * HD), slice(g * HD, (g + 1) * HD)
                    by_two = src[ps_, :].rearrange("p (n t q) -> p t n q", t=8, q=2)
                    for u in range(2):
                        m = dve.did(V.tensor_copy(blocks[rs, 8 * u:8 * u + 8, g * N_CMP:(g + 1) * N_CMP],
                                                  by_two[:, :, u:u + N_CMP, par]))
            dve.wait(m)
            for g in range(2):
                pos = small[:, SM2["cmp_pos"]].unsqueeze(2).broadcast_to([P, 16, N_CMP])
                m = dve.did(V.tensor_tensor(blocks[:, :, g * N_CMP:(g + 1) * N_CMP],
                                            blocks[:, :, g * N_CMP:(g + 1) * N_CMP], pos, ALU.add))
            parts[which] = split_out(*cmp_parts(which), blocks, m)

        def cmp_hidden(which, part):
            pe.wait(parts[which], parts.get(("hid", 0)))
            for half, r in halves():
                for ct in range(2):
                    for k in range(HK):
                        b = [t[:, part * KT + half * HK + k, :] for t in cmp_parts(which)]
                        mm = products(acc[ct][:, 0, 0:cmp_w], tile(r, k, slice(ct * P, (ct + 1) * P)), b,
                                      part == half == k == 0)
                m = used.did(mm)
            if part == 1:
                act.wait(m)
                for ct in range(2):
                    m = act.did(AC.activation(hid_c[which][:, ct, :], acc[ct][:, 0, 0:cmp_w], ACT.Silu))
                parts[("hid", which)] = m

        def cmp_out(which):
            w2 = small[:, SM2["w2v" if which else "w2k"]].rearrange("p (t d) -> p t d", t=2)
            pe.wait(parts[("hid", which)])
            for g in range(2):
                for t in range(2):
                    h = hid_c[which][:, t, g * N_CMP:(g + 1) * N_CMP]
                    if which == 0:
                        mm = T.matmul(misc[0][g * HD:(g + 1) * HD, 0, 0:N_CMP], w2[:, t, :], h, start=t == 0, stop=t == 1)
                    else:
                        mm = T.matmul(misc[1][0:N_CMP, 0, g * HD:(g + 1) * HD], h, w2[:, t, :], start=t == 0, stop=t == 1)
            m = pe.did(mm)
            act.wait(m)
            if which:
                return act.did(AC.activation(vc, misc[1][0:N_CMP, 0, 0:P], ACT.Copy))
            act.did(AC.activation(kc, misc[0][:, 0, 0:N_CMP], ACT.Copy))
            return act.did(AC.activation(k_root, misc[0][:, 0, 0:N_CMP], ACT.Square))

        def cmp_k_norm(ready):
            pe.wait(ready)
            m = pe.did(T.matmul(misc[0][:, 1, 0:N_CMP], c("blk"), k_root, start=True, stop=True))
            act.wait(m)
            m = act.did(AC.activation(k_root, misc[0][:, 1, 0:N_CMP], ACT.Sqrt, bias=eps))
            dve.wait(m)
            m = dve.did(V.reciprocal(k_root, k_root))
            dve.wait(m)
            return dve.did(V.scalar_tensor_tensor(kc, kc, sm("nsa_k"), k_root, ALU.mult, ALU.mult))

        m = act.now()
        cmp_blocks(0, m)
        s0, s1, s2 = (squares(proj[:, n, :, :], m) for n in range(3))
        project(4)
        head_norm(proj[:, 0, :, :], sm("nsa_q"), s0)
        project(5)
        cmp_blocks(1, m)
        head_norm(proj[:, 1, :, :], sm("nsa_q"), s1)
        cmp_hidden(0, 0)
        project(6)
        head_norm(proj[:, 2, :, :], sm("nsa_k"), s2)
        cmp_hidden(0, 1)
        s3 = squares(proj[:, 6, :, :], slots_out[6])
        project(7, swa_kv)
        s4 = squares(proj[:, 7, 0:1, :], slots_out[7])
        head_norm(proj[:, 6, :, :], sm("swa_q"), s3)
        k_in = cmp_out(0)
        cmp_hidden(1, 0)
        project(8, slot_rows)
        head_norm(proj[:, 7, 0:1, :], sm("swa_k"), s4)
        cmp_k_norm(k_in)
        cmp_hidden(1, 1)
        gate24 = stat[:, 4:6, 0:24]
        wg = sm("w_gate").rearrange("p (k n) -> p k n", k=KT)
        pe.wait(roots_read[4])
        for rt in range(2):
            for k in range(KT):
                mm = T.matmul(bank[4][:, rt * 24:(rt + 1) * 24], xn[:, k, rt * P:(rt + 1) * P], wg[:, k, :],
                              start=k == 0, stop=k == KT - 1)
        gate_in = pe.did(mm)
        project(9, slot_rows)
        cmp_out(1)
        act.wait(gate_in)
        gate_ready = act.did(AC.activation(gate24, bank[4][:, 0:48].rearrange("p (r n) -> p r n", r=2), ACT.Sigmoid))
        pending = []

        def gate_slot(n):
            read_gate_slot()
            pe.wait(free[n % 2])
            pending.append((n, slot_T(dense[n % 2], xn_hi, xn_lo)))

        def read_gate_slot():
            if pending:
                n, got = pending.pop()
                act.wait(got)
                free[n % 2] = act.did(AC.activation(gates[:, 2 * n:2 * n + 2, :], dense[n % 2], ACT.Copy))

        CL, CE = slice(384, 384 + N_CMP), slice(384 + N_CMP, 384 + N_CMP + N_CMP0)
        scored, transposed, valued, ysplit, pTs = {}, {}, {}, {}, {}
        for e in (pe, act, dve):
            e.wait(pe.now(), act.now(), dve.now())

        def nsa_scores(h):
            g, t = h // 4, h % 4
            pr = slice(g * HD, (g + 1) * HD)
            q = proj[pr, t // 2, t % 2, :]
            pe.wait(scored.get(h - 1))
            for b in range(2):
                k, out = proj[pr, 2, b, :], bank[2 + b]
                T.matmul(out[:, 0:S], q[:, P:S], k, start=True, stop=True)
                mm = T.matmul(out[:, S:S + P], q[:, 0:P], k[:, 0:P], start=True, stop=True)
                if b == 0:
                    T.matmul(out[:, CL], q[:, P:S], kc[pr, :], start=True, stop=True)
                    mm = T.matmul(out[:, CE], q[:, 0:P], kc[pr, 0:N_CMP0], start=True, stop=True)
            return pe.did(mm)

        spans = [(0, slice(0, S), slice(0, S)), (1, slice(0, S), slice(0, S)), (0, CL, slice(31, S, 16)),
                 (0, slice(S, S + P), slice(P, S)), (1, slice(S, S + P), slice(P, S)), (0, CE, slice(P + 31, S, 16))]

        def nsa_exps(h, ready):
            lg = logit[h % 2]
            s6 = stat[:, 0:4, 8 * (h % 2):8 * (h % 2) + 6]
            dve.wait(ready, transposed.get(h - 2))
            dve.settle()
            for n, (b, cols, tc) in enumerate(spans):
                m = dve.did(V.tensor_tensor_reduce(lg[:, b, cols], bank[2 + b][:, cols], table[:, h, tc], 1.0, LOWEST,
                                                   ALU.add, ALU.max, s6[:, 0, n:n + 1]))
            scored[h] = m
            dve.wait(m)
            m = dve.did(V.tensor_scalar(s6[:, 1, :], s6[:, 0, :], -0.125, None, ALU.mult))
            act.wait(m)
            for n, (b, cols, tc) in enumerate(spans):
                m = act.did(AC.activation(lg[:, b, cols], lg[:, b, cols], ACT.Exp, bias=s6[:, 1, n:n + 1], scale=0.125,
                                          accum_out=s6[:, 2, n:n + 1]))
            return m

        def nsa_weights(h, ready):
            lg = logit[h % 2]
            s6 = stat[:, 0:4, 8 * (h % 2):8 * (h % 2) + 6]
            dve.wait(ready, gate_ready)
            m = dve.did(V.reciprocal(s6[:, 3, :], s6[:, 2, :]))
            dve.wait(m)
            for rt, at in ((1, 0), (0, 3)):
                dve.did(V.tensor_tensor(s6[:, 3, at:at + 2], s6[:, 3, at:at + 2], gate24[:, rt, 8 + h:24:8], ALU.mult))
                m = dve.did(V.tensor_tensor(s6[:, 3, at + 2:at + 3], s6[:, 3, at + 2:at + 3], gate24[:, rt, h:h + 1], ALU.mult))
            dve.wait(m)
            m = dve.did(V.tensor_tensor(s6[:, 3, 5:6], s6[:, 3, 5:6], c("late"), ALU.mult))
            dve.wait(m)
            for n, (b, cols, tc) in enumerate(spans):
                m = dve.did(V.tensor_scalar(lg[:, b, cols], lg[:, b, cols], s6[:, 3, n:n + 1], None, ALU.mult))
            return m

        def nsa_transpose(h, ready):
            lg = logit[h % 2]
            pe.wait(ready, pTs.get(h - 1))
            for b in range(2):
                for to, frm in ((0, S), (1, 0), (2, P)):
                    mm = T.transpose(bank[4 + b][:, to * P:(to + 1) * P], lg[:, b, frm:frm + P], c("ident"))
            T.transpose(bank[6][0:N_CMP0, 0:P], lg[:, 0, CE], c("ident"))
            mm = T.transpose(bank[6][0:N_CMP, P:S], lg[:, 0, CL], c("ident"))
            transposed[h] = pe.did(mm)
            act.wait(transposed[h], valued.get(h - 2))
            dve.wait(transposed[h], valued.get(h - 2))
            cp = sq[0:N_CMP, h % 2, :]
            act.did(AC.activation(cp[0:N_CMP0, 0:P], bank[6][0:N_CMP0, 0:P], ACT.Copy))
            act.did(AC.activation(cp[:, P:S], bank[6][0:N_CMP, P:S], ACT.Copy))
            a = act.did(AC.activation(probT[h % 2][:, 0, 0:384], bank[4][:, 0:384], ACT.Copy))
            d = dve.did(V.tensor_copy(probT[h % 2][:, 1, 0:384], bank[5][:, 0:384]))
            pTs[h] = [a, d]

        def nsa_values(h):
            g, t = h // 4, h % 4
            pr = slice(g * HD, (g + 1) * HD)
            o = bank[7][pr, 0:S]
            cp = sq[0:N_CMP, h % 2, :]
            pe.wait(pTs[h], ysplit.get(h - 1))
            for b in range(2):
                v = lambda kt: proj[:, 8, kt, b * P + g * HD:b * P + (g + 1) * HD]
                causal_values(o, v, probT[h % 2][:, b, :], b == 0, False)
            T.matmul(o[:, 0:P], vc[0:N_CMP0, pr], cp[0:N_CMP0, 0:P], start=False, stop=False, skip_group_check=True)
            valued[h] = pe.did(T.matmul(o[:, P:S], vc[:, pr], cp[:, P:S], start=False, stop=True, skip_group_check=True))
            ysplit[h] = split_out(y_hi[pr, t, :], y_lo[pr, t, :], o, valued[h])

        for n in range(8 + 2):
            if 1 <= n < 9:
                w = nsa_weights(n - 1, e)
            if n < 8:
                e = nsa_exps(n, nsa_scores(n))
                gate_slot(n)
            if 1 <= n < 9:
                nsa_transpose(n - 1, w)
            if n >= 2:
                nsa_values(n - 2)
        nsa_end = [pe.now(), act.now(), dve.now()]

        scored, transposed, valued, ysplit, pTs, read = {}, {}, {}, {}, {}, {}
        for e in (pe, act, dve):
            e.wait(nsa_end)

        def swa_scores(h):
            g, t = h // 2, h % 2
            pr = slice(g * HD, (g + 1) * HD)
            q, k, out = proj[pr, 6, t, :], proj[pr, 7, 0, :], bank[2]
            pe.wait(scored.get(h - 1))
            T.matmul(out[:, 0:S], q[:, P:S], k, start=True, stop=True)
            return pe.did(T.matmul(out[:, S:S + P], q[:, 0:P], k[:, 0:P], start=True, stop=True))

        def swa_exps(h, ready):
            out, lg, s4 = bank[2], logit[0][:, h % 2, :], stat[:, 0:4, 16 + 4 * (h % 2):18 + 4 * (h % 2)]
            e2 = stat[:, 0, 18 + 4 * (h % 2):20 + 4 * (h % 2)]
            sink = sm("sinks")[:, h:h + 1]
            dve.wait(ready, transposed.get(h - 2))
            dve.settle()
            dve.did(V.tensor_tensor_reduce(lg[:, 0:S], out[:, 0:S], table[:, 8 + h, :], 1.0, LOWEST,
                                           ALU.add, ALU.max, s4[:, 0, 0:1]))
            m = dve.did(V.tensor_tensor_reduce(lg[:, S:S + P], out[:, S:S + P], table[:, 8 + h, P:S], 1.0, LOWEST,
                                               ALU.add, ALU.max, s4[:, 0, 1:2]))
            scored[h] = m
            dve.wait(m)
            m = dve.did(V.tensor_scalar(s4[:, 0, :], s4[:, 0, :], 0.125, sink, ALU.mult, ALU.max))
            dve.wait(m)
            m = dve.did(V.tensor_scalar(s4[:, 1, :], s4[:, 0, :], -1.0, None, ALU.mult))
            act.wait(m)
            act.did(AC.activation(e2, s4[:, 1, :], ACT.Exp, bias=sink))
            act.did(AC.activation(lg[:, 0:S], lg[:, 0:S], ACT.Exp, bias=s4[:, 1, 0:1], scale=0.125,
                                  accum_out=s4[:, 2, 0:1]))
            return act.did(AC.activation(lg[:, S:S + P], lg[:, S:S + P], ACT.Exp, bias=s4[:, 1, 1:2], scale=0.125,
                                         accum_out=s4[:, 2, 1:2]))

        def swa_weights(h, ready):
            lg, s4 = logit[0][:, h % 2, :], stat[:, 0:4, 16 + 4 * (h % 2):18 + 4 * (h % 2)]
            e2 = stat[:, 0, 18 + 4 * (h % 2):20 + 4 * (h % 2)]
            dve.wait(ready)
            m = dve.did(V.tensor_tensor(s4[:, 3, :], s4[:, 2, :], e2, ALU.add))
            dve.wait(m)
            m = dve.did(V.reciprocal(s4[:, 3, :], s4[:, 3, :]))
            dve.wait(m)
            dve.did(V.tensor_scalar(lg[:, 0:S], lg[:, 0:S], s4[:, 3, 0:1], None, ALU.mult))
            return dve.did(V.tensor_scalar(lg[:, S:S + P], lg[:, S:S + P], s4[:, 3, 1:2], None, ALU.mult))

        def swa_transpose(h, ready):
            pe.wait(ready, pTs.get(h - 1))
            for to, frm in ((0, S), (1, 0), (2, P)):
                m = T.transpose(bank[4][:, to * P:(to + 1) * P], logit[0][:, h % 2, frm:frm + P], c("ident"))
            transposed[h] = pe.did(m)
            act.wait(transposed[h], valued.get(h - 2))
            pTs[h] = act.did(AC.activation(probT[0][:, h % 2, 0:384], bank[4][:, 0:384], ACT.Copy))

        def swa_values(h):
            g, t = h // 2, h % 2
            pr = slice(g * HD, (g + 1) * HD)
            o = bank[6][pr, 0:S]
            pe.wait(pTs[h], ysplit.get(h - 1))
            v = lambda kt: proj[:, 7, 1, kt * P + g * HD:kt * P + (g + 1) * HD]
            valued[h] = pe.did(causal_values(o, v, probT[0][:, h % 2, :]))
            ysplit[h] = split_out(y_hi[pr, 6 + t, :], y_lo[pr, 6 + t, :], o, valued[h])

        zt, spt = logit[1][:, 0, 0:384], logit[1][:, 1, 0:384]
        diagonal = (slice(0, P), slice(S, S + P))

        def sb_scores(h):
            q, k, b = proj[head_rows(h), 4, h // 2, :], proj[head_rows(h), 5, h // 2, :], bank[3]
            pe.wait(read.get(("z", h - 1)))
            T.matmul(b[:, 0:S], k[:, 0:P], q, start=True, stop=True)
            return pe.did(T.matmul(b[:, S:S + P], k[:, P:S], q[:, P:S], start=True, stop=True))

        def sb_softplus(h, ready):
            b = bank[3]
            act.wait(ready, read.get(("w", h - 1)))
            zc = act.did(AC.activation(zt, b[:, 0:384], ACT.Copy, scale=0.125))
            a = act.did(AC.activation(spt, b[:, 0:384], ACT.Abs, scale=0.125))
            read[("z", h)] = a
            act.wait(a)
            a = act.did(AC.activation(spt, spt, ACT.Exp, scale=-1.0))
            act.wait(a)
            a = act.did(AC.activation(spt, spt, ACT.Ln, bias=one))
            dve.wait(zc, a)
            m = dve.did(V.scalar_tensor_tensor(spt, zt, 0.0, spt, ALU.max, ALU.add))
            dve.wait(m)
            for cols in diagonal:
                m = dve.did(V.tensor_tensor(spt[:, cols], spt[:, cols], c("strict"), ALU.mult))
            return m

        def sb_sums(h, ready):
            ab = bank[5]
            pe.wait(ready, read.get(("a", h - 1)))
            T.matmul(ab[:, 0:S], c("tri"), spt[:, 0:S], start=True, stop=False, skip_group_check=True)
            T.matmul(ab[:, P:S], ones, spt[:, S:S + P], start=False, stop=True, skip_group_check=True)
            m = pe.did(T.matmul(ab[:, S:S + P], c("tri"), spt[:, S:S + P], start=True, stop=True, skip_group_check=True))
            dve.wait(m)
            m = dve.did(V.tensor_tensor(zt, zt, ab[:, 0:384], ALU.subtract))
            read[("a", h)] = m
            dve.wait(m)
            for cols in diagonal:
                m = dve.did(V.tensor_tensor(zt[:, cols], zt[:, cols], c("strict_add"), ALU.add))
            act.wait(m, read.get(("v", h - 2)))
            read[("w", h)] = act.did(AC.activation(probT[1][:, h % 2, 0:384], zt, ACT.Exp))

        def sb_values(h):
            o = bank[7]
            pe.wait(read[("w", h)], read.get(("y", h // 2 - 1)))
            v = lambda kt: proj[:, 9, kt, h * HD:(h + 1) * HD]
            read[("v", h)] = pe.did(causal_values(o[head_rows(h), 0:S], v, probT[1][:, h % 2, :]))
            if h % 2:
                read[("y", h // 2)] = split_out(y_hi[:, 4 + h // 2, :], y_lo[:, 4 + h // 2, :], o[:, 0:S], read[("v", h)])

        for n in range(4 + 2):
            if 1 <= n < 5:
                w = swa_weights(n - 1, e)
            if n < 4:
                zs = sb_scores(n)
                e = swa_exps(n, swa_scores(n))
                sp = sb_softplus(n, zs)
                gate_slot(8 + n)
            if 1 <= n < 5:
                sb_values(n - 1)
                swa_transpose(n - 1, w)
            if n < 4:
                sb_sums(n, sp)
            if n >= 2:
                swa_values(n - 2)
        read_gate_slot()
        sb_done = [ysplit[3], read[("y", 1)]]

        pe.wait(sb_done, act.now(), dve.now())
        for e in (act, dve):
            e.wait(pe.now(), act.now(), dve.now())
        up_banks = [dense[0], dense[1], acc[0]]
        with L.run(2) as loop:
            for half in range(2):
                b = loop.i * 4 + half * 2
                before = loop.last("merged1", dve.counter) if half == 0 else low
                pe.wait(before)
                for part, r in halves():
                    for k in range(HK):
                        n = 0 if part == 0 else 1 + k // 2
                        for ct in range(2):
                            mm = products(up_banks[n][:, ct, :], tile(r, k, slice(ct * P, (ct + 1) * P)),
                                          [t[:, part * HK + k, :] for t in (y_hi, y_lo)],
                                          k == (0, 0, 2)[n] and ct == 0)
                    got = used.did(mm)
                act.wait(gates_read if half else loop.last("gates_read1", dve.counter))
                g3 = [act_t, root, rinv]
                for n in range(3):
                    sg = act.did(AC.activation(g3[n], gates[:, bass.ds(b + 8 * n, 2), :], ACT.Sigmoid))
                dve.wait(got, before, sg)
                t3 = [sq[:, 2 * n:2 * n + 2, :] for n in range(3)]
                for n in range(3):
                    m = dve.did(V.tensor_tensor(t3[n], up_banks[n], g3[n], ALU.mult))
                gates_read = m
                dve.wait(m)
                m = dve.did(V.tensor_tensor(t3[0], t3[0], t3[1], ALU.add))
                dve.wait(m)
                m = dve.did(V.tensor_tensor(t3[0], t3[0], t3[2], ALU.add))
                act.wait(m)
                hh = act.did(AC.activation(xn_hi[:, bass.ds(b, 2), :], t3[0], ACT.Copy))
                dve.wait(hh)
                low = dve.did(V.tensor_tensor(xn_lo[:, bass.ds(b, 2), :], t3[0],
                                              xn_hi[:, bass.ds(b, 2), :].bitcast(F32), ALU.subtract))
                if half:
                    loop.keep("merged1", low)
                    loop.keep("gates_read1", gates_read)
        got = out_projection(xn_hi, xn_lo, [dve.now(), act.now()], None)
        for b in range(4):
            dve.wait(got[b])
            m = dve.did(V.tensor_tensor(x[:, 2 * b:2 * b + 2, :], x[:, 2 * b:2 * b + 2, :], acc[b], ALU.add))
        x_ready = half_ffn(sm("ffn2"), m, False)

    pool.wait(dve.now())
    stored = Counter(L, "stored", 16)
    out_done = stored.did(G.dma_start(A["out"], x))
    pool.wait(out_done)
    return L


def constants():
    out = np.zeros((P, CON_W), np.float32)
    i, j = np.arange(P)[:, None], np.arange(P)[None, :]
    out[:, CON["ident"]] = i == j
    out[:, CON["blk"]] = (i // HD == j // HD) / HD
    out[:, CON["tri"]] = i >= j
    rot = np.zeros((P, P), np.float32)
    for p in range(P):
        if p % HD < HD // 2:
            rot[p + HD // 2, p] = -1
        else:
            rot[p - HD // 2, p] = 1
    out[:, CON["rot"]] = rot
    out[:, CON["causal"]] = np.where(P + i - np.arange(S)[None, :] >= 0, 0, BIG)
    out[:, CON["strict"]] = i < j
    out[:, CON["strict_add"]] = np.where(i < j, 0, BIG)
    gamma = 1 - 2.0 ** (-5.0 - np.arange(4))
    diff = j - i
    for h in range(4):
        diag = np.where(diff >= 0, gamma[h] ** np.maximum(diff, 0), 0)
        out[:, CON["decay"]][:, h * S:(h + 1) * S] = np.concatenate([diag, gamma[h] ** (P + diff)], 1) * HD ** -0.5
    half = HD // 2
    out[:, CON["inv_freq"]] = (np.float32(10000.0) ** (-(np.arange(P) % half).astype(np.float32) / half))[:, None]
    out[:, CON["late"]] = (np.arange(P) >= 31)[:, None]
    early = np.zeros((34, EARLY_W), np.float32)
    for h in range(8):
        early[h, EARLY["nsel"].start + h * P:EARLY["nsel"].start + (h + 1) * P] = -1
    dist = S - 1 - np.arange(VEC)
    big = 16 + (np.log(np.maximum(dist, 1).astype(np.float32) / 16) / np.float32(np.log(8)) * 16).astype(np.int32)
    bucket = np.where(np.maximum(dist, 0) < 16, np.maximum(dist, 0), np.minimum(big, 31))
    onehot = early[:, EARLY["onehot"]]
    onehot[bucket, np.arange(VEC)] = 1
    onehot[32] = dist < 0
    onehot[33] = dist >= P
    return out, early


def lay_out(a):
    def feature_major(t):
        return np.ascontiguousarray(t.reshape(S, KT, P).transpose(2, 1, 0)).reshape(P, KT * S)

    def cols(v):
        return v.reshape(-1, P).T

    def pair(w):
        return w.reshape(-1, P, w.shape[1]).transpose(1, 0, 2).reshape(P, -1)

    stream = np.zeros((2 * N_SLOTS, P, SLOT // 2), np.float32)
    at = [0]

    def put(block):
        for half in range(2):
            stream[at[0]] = block[:, half * SLOT // 2:(half + 1) * SLOT // 2]
            at[0] += 1

    def dense(w):
        for c in range(0, w.shape[1], COLS):
            put(pair(w[:, c:c + COLS]))

    def ffn(gate, up, down):
        for c in range(0, FF, COLS):
            put(pair(gate[:, c:c + COLS]))
            put(pair(up[:, c:c + COLS]))
        for j in range(FT // 2):
            put(pair(down[2 * j * P:2 * (j + 1) * P]))

    small1 = np.zeros((DEPTH, P, SM1_W), np.float32)
    small2 = np.zeros((DEPTH, P, SM2_W), np.float32)
    for l in range(DEPTH):
        w = a["w_in"][l]
        lx, ly, fq, fk, fv, ff, rq, rk, rv, rg = np.split(w, np.cumsum(
            [256, 256, 512, 512, 512, 8, 256, 256, 256, 256])[:-1], axis=1)
        for part in (fq, fk, rq, rk, rg, lx, ly):
            dense(part)
        f = np.zeros((D, COLS), np.float32)
        f[:, 0:8] = ff
        put(pair(f))
        dense(fv)
        dense(rv)
        for name in ("w_out", "w_cq", "w_ck", "w_cv", "w_co"):
            dense(a[name][l])
        ffn(a["w_gate"][l], a["w_up"][l], a["w_down"][l])
        s = small1[l]
        for name in ("pre_mix", "post_mix", "pre_cross", "post_cross", "pre_ffn", "post_ffn"):
            s[:, SM1[name]] = cols(a[name + "_g"][l])
        s[:, SM1["conv_w"]] = np.concatenate([cols(a["conv_w"][l, n]) for n in range(4)], 1)
        for name, src in (("conv_b", "conv_b"), ("b_rg", "b_rg"), ("b_ig", "b_ig"), ("lam", "lru_lambda")):
            s[:, SM1[name]] = cols(a[src][l])
        s[0:8, SM1["fox_b"]] = a["fox_b_f"][l][:, None]
        for name in ("w_rg", "w_ig"):
            for n in range(4):
                r, o = (n % 2) * HD, SM1[name].start + n * HD
                s[r:r + HD, o:o + HD] = a[name][l, n]
    for l in range(DEPTH):
        ffn(a["ffn1_w_gate_2"][l], a["ffn1_w_up_2"][l], a["ffn1_w_down_2"][l])
        w = a["w_in_2"][l]
        (nq, nkc, nvc, nks, nvs, nkw, nvw, ngate, sq, sk, sv, wq, wk, wv, bgate) = np.split(w, np.cumsum(
            [512, 128, 128, 128, 128, 128, 128, 24, 256, 256, 256, 256, 128, 128, 3072])[:-1], axis=1)
        by_group8 = np.concatenate([np.arange(h * HD, (h + 1) * HD) for t in range(4) for h in (t, t + 4)])
        by_group4 = np.concatenate([np.arange(h * HD, (h + 1) * HD) for t in range(2) for h in (t, t + 2)])
        dense(nq[:, by_group8])
        dense(np.concatenate([nks, nkw], 1))
        dense(np.concatenate([nkc, nvc], 1))
        dense(sq)
        dense(sk)
        w1 = {(n, part): a["nsa_cmp_%s_w1_2" % n][l][part * D:(part + 1) * D] for n in "kv" for part in range(2)}
        dense(w1["k", 0])
        dense(wq[:, by_group4])
        dense(w1["k", 1])
        dense(np.concatenate([wk, wv], 1))
        dense(w1["v", 0])
        dense(np.concatenate([nvs, nvw], 1))
        dense(w1["v", 1])
        dense(sv)
        dense(bgate)
        up = np.concatenate([a["w_up_nsa_2"][l][by_group8], a["w_up_sb_2"][l], a["w_up_swa_2"][l][by_group4]], 0)
        dense(up)
        dense(a["w_out_2"][l])
        ffn(a["ffn2_w_gate_2"][l], a["ffn2_w_up_2"][l], a["ffn2_w_down_2"][l])
        s = small2[l]
        for name, src in (("ffn1", "ffn1_norm_2"), ("mix", "mix_norm_2"), ("ffn2", "ffn2_norm_2")):
            s[:, SM2[name]] = cols(a[src][l])
        for name, src in (("nsa_q", "nsa_q_norm_2"), ("nsa_k", "nsa_k_norm_2"), ("swa_q", "swa_q_norm_2"),
                          ("swa_k", "swa_k_norm_2")):
            s[:, SM2[name]] = np.concatenate([a[src][l]] * 2)[:, None]
        s[:, SM2["sinks"]] = a["swa_sinks_2"][l][None, :]
        s[:, SM2["cmp_pos"]] = a["nsa_cmp_pos_2"][l].reshape(16, P).T
        for name, src in (("w2k", "nsa_cmp_k_w2_2"), ("w2v", "nsa_cmp_v_w2_2")):
            s[:, SM2[name]] = pair(a[src][l])
        s[:, SM2["w_gate"]] = pair(ngate)
    assert at[0] == 2 * N_SLOTS

    con, early = constants()
    con[:, CON["mem_g"]] = cols(a["mem_norm_g"])
    bias = np.zeros((34, 12), np.float32)
    bias[0:32] = a["rel_bias_2"]
    bias[32] = BIG / 8
    bias[33, 8:] = BIG / 8
    return {
        "stream": stream, "x": feature_major(a["x"]), "mem": feature_major(a["mem"]),
        "positions": np.ascontiguousarray(np.broadcast_to(a["positions"].reshape(1, S), (P, S))),
        "rel_bias": bias, "con": con, "early": early, "small1": small1, "small2": small2,
    }


def program(nc, arrays, known, final):
    A = {n: nc.dram_tensor("in_" + n, a.shape, mybir.dt.from_np(a.dtype), kind="ExternalInput").ap()
         for n, a in arrays.items()}
    for n in ("x", "mem"):
        A[n] = A[n].rearrange("p (k s) -> p k s", k=KT)
    A["out"] = nc.dram_tensor("out", (P, KT, S), F32, kind="ExternalOutput").ap()
    A["skew"] = nc.dram_tensor("skew", (P * 12 * VEC,), F32, kind="Internal").ap()
    build(nc, A, known, final)


def kernel(**inputs):
    import concourse.bacc as bacc
    from concourse.bass_utils import run_bass_kernel_spmd

    arrays = lay_out({n: np.asarray(v) for n, v in inputs.items()})
    known = {}
    for final in (False, True):
        nc = bacc.Bacc("TRN2", target_bir_lowering=False, num_devices=1)
        program(nc, arrays, known, final)
    r = run_bass_kernel_spmd(nc, [{"in_" + n: v for n, v in arrays.items()}], core_ids=[0])
    out = r.results[0]["out"].reshape(P, KT, S)
    return np.ascontiguousarray(out.transpose(2, 1, 0)).reshape(1, S, D)
```

```python
from contextlib import ExitStack, contextmanager

import numpy as np

import concourse.bass as bass
from concourse import mybir

F32 = mybir.dt.float32
F32R = mybir.dt.float32r
I32 = mybir.dt.int32
ACT = mybir.ActivationFunctionType
ALU = mybir.AluOpType
AX = mybir.AxisListType

P = 128
D = 1024
KT = D // P
S = 256
ST = S // P
DEPTH = 2
HD = 64
EPS = 1e-6
FF = 2816
FT = FF // P
BIG = -8e30
LOWEST = -3e38
COLS = 256
SLOT = KT * COLS
HK = KT // 2
RING = 4
N_CMP = (S - 32) // 16 + 1
N_CMP0 = (P - 32) // 16 + 1
VEC = 3 * P

B1_SLOTS = 13 + 4 + 4 + 4 + 4 + 4 + 2 * (FF // COLS) + FT // 2
B2_SLOTS = 2 * (2 * (FF // COLS) + FT // 2) + 10 + 12 + 4 + 4 + 4
N_SLOTS = DEPTH * (B1_SLOTS + B2_SLOTS)


def columns(**widths):
    at, out = 0, {}
    for name, w in widths.items():
        out[name] = slice(at, at + w)
        at += w
    return out, at


SM1, SM1_W = columns(pre_mix=KT, post_mix=KT, pre_cross=KT, post_cross=KT, pre_ffn=KT, post_ffn=KT,
                     conv_w=8, conv_b=2, b_rg=2, b_ig=2, lam=2, fox_b=1, w_rg=256, w_ig=256)
SM2, SM2_W = columns(ffn1=KT, mix=KT, ffn2=KT, nsa_q=1, nsa_k=1, swa_q=1, swa_k=1, sinks=4,
                     cmp_pos=16, w2k=128, w2v=128, w_gate=KT * 24)
SM_W = max(SM1_W, SM2_W)
CON, CON_W = columns(ident=P, blk=P, tri=P, rot=P, causal=S, strict=P, decay=4 * S, strict_add=P, inv_freq=1,
                     late=1, mem_g=KT)
EARLY, EARLY_W = columns(onehot=VEC, nsel=8 * P)


class Counter:

    def __init__(self, loops, name, step=1):
        self.loops, self.name, self.step = loops, name, step
        self.sem = loops.nc.alloc_semaphore(name)
        self.done = 0
        loops.counters.append(self)

    def did(self, instruction):
        instruction.then_inc(self.sem, self.step)
        self.done += self.step
        return self.at(self.done)

    def at(self, value):
        return Mark(self, value, tuple(self.loops.open))

    def now(self):
        return self.at(self.done)


class Mark:

    def __init__(self, counter, value, loops):
        self.counter, self.value, self.loops = counter, value, loops

    def number(self):
        assert self.value > 0 or not self.loops or not self.counter.loops.final
        out = self.value
        for loop in self.loops:
            per = loop.adds(self.counter.name)
            if per:
                out = loop.i * per + out
        return out


class Loop:
    def __init__(self, key, known):
        self.key, self.i = key, None
        self.known = known.setdefault(key, {})
        self.found, self.start, self.kept = {}, {}, {}

    def adds(self, name):
        return self.known.get(name, 0)

    def keep(self, label, mark):
        self.found["keep " + label] = mark.value - self.start[mark.counter.name]
        self.kept[label] = mark.counter

    def last(self, label, counter):
        off = self.known.get("keep " + label, 0)
        return counter.at(self.start[counter.name] + off - self.adds(counter.name))


    def ended(self, label):
        counter = self.kept[label]
        return counter.at(counter.done - self.found[counter.name] + self.found["keep " + label])


class Loops:

    def __init__(self, nc, known, final):
        self.nc, self.known, self.final = nc, known, final
        self.counters, self.open, self.engines, self.n = [], [], [], 0

    @contextmanager
    def run(self, rounds, engines=mybir.ALL_ENGINES):
        loop = Loop(self.n, self.known)
        self.n += 1
        for c in self.counters:
            loop.start[c.name] = c.done
        for e in self.engines:
            e.passed.clear()
            e.settle()
        with self.nc.Fori(0, rounds, engines=engines) as i:
            loop.i = i
            self.open.append(loop)
            yield loop
            self.open.pop()
        for e in self.engines:
            e.passed.clear()
        for c in self.counters:
            add = c.done - loop.start.get(c.name, 0)
            loop.found[c.name] = add
            c.done = loop.start.get(c.name, 0) + rounds * add
        if self.final:
            assert loop.found == loop.known, f"loop {loop.key} adds otherwise than counted"
        else:
            loop.known.update(loop.found)


class Engine:

    def __init__(self, loops, eng, name):
        self.eng, self.counter, self.passed = eng, Counter(loops, "steps_" + name), {}
        self.settled = loops.nc.alloc_semaphore("settled_" + name)
        loops.engines.append(self)

    def wait(self, *marks):
        for m in marks:
            if m is None:
                continue
            if isinstance(m, (list, tuple)):
                self.wait(*m)
                continue
            key = (m.counter.name, m.loops)
            if m.value <= self.passed.get(key, 0):
                continue
            self.passed[key] = m.value
            self.eng.wait_ge(m.counter.sem, m.number())

    def did(self, instruction):
        return self.counter.did(instruction)

    def settle(self):
        self.eng.sem_inc(self.settled)

    def now(self):
        return self.counter.now()


def build(nc, A, known, final):
    L = Loops(nc, known, final)
    pe, act, dve, pool = (Engine(L, e, n) for e, n in (
        (nc.tensor, "pe"), (nc.scalar, "act"), (nc.vector, "dve"), (nc.gpsimd, "pool")))
    T, AC, V, G = nc.tensor, nc.scalar, nc.vector, nc.gpsimd

    def sb(name, shape, dt=F32):
        return nc.alloc_sbuf_tensor(name, shape, dt)[tuple(slice(None) for _ in shape)]

    def sb_at(name, shape, dt, offset):
        return nc.alloc_sbuf_tensor_at(name, shape, dt, offset=offset)[tuple(slice(None) for _ in shape)]

    base = (nc.sbuf_base + 31) // 32 * 32
    shared = 13 * 2048 + 24 * 1024 + 16384
    nc.alloc_sbuf_tensor("shared", [P, shared // 4 + 16], F32)
    proj = sb_at("proj", [P, 13, 2, COLS], F32, base)
    gates = sb_at("gates", [P, 24, S], F32, base + 13 * 2048)
    hid_hi = sb_at("hid_hi", [P, FT, S], F32R, base)
    hid_lo = sb_at("hid_lo", [P, FT, S], F32R, base + FT * 1024)
    lru_at = [base + 13 * 2048 + n * 2048 for n in range(8)]
    xc, lru_r, lru_i, lru_a, lru_t, lru_u, lru_h, lru_g = (
        sb_at(f"lru{n}", [P, 2, S], F32, at) for n, at in enumerate(lru_at))
    mem_hi = sb_at("mem_hi", [P, KT, S], F32R, base + 13 * 2048 + 24 * 1024)
    mem_lo = sb_at("mem_lo", [P, KT, S], F32R, base + 13 * 2048 + 24 * 1024 + 8192)
    table = sb_at("table", [P, 12, S], F32, base + 13 * 2048 + 24 * 1024)

    raw = [sb(f"raw{r}", [P, HK, COLS]) for r in range(RING)]
    w_hi = [sb(f"w_hi{r}", [P, HK, COLS], F32R) for r in range(RING)]
    w_lo = [sb(f"w_lo{r}", [P, HK, COLS], F32R) for r in range(RING)]
    x = sb("x", [P, KT, S])
    xn = sb("xn", [P, KT, S])
    xn_hi, xn_lo = sb("xn_hi", [P, KT, S], F32R), sb("xn_lo", [P, KT, S], F32R)
    y_hi, y_lo = sb("y_hi", [P, KT, S], F32R), sb("y_lo", [P, KT, S], F32R)
    sq = sb("sq", [P, KT, S])
    con = sb("con", [P, CON_W])
    ones = sb("ones", [P, P])
    ones_row = sb("ones_row", [8, S])
    small = sb("small", [P, SM_W])
    root, rinv = sb("root", [P, 2, S]), sb("rinv", [P, 2, S])
    scale, scale_col = sb("scale", [P, S]), sb("scale_col", [P, 4])
    act_t = sb("act_t", [P, 2, S])
    logit = [sb(f"logit{i}", [P, 2, 512]) for i in range(2)]
    probT = [sb(f"probT{i}", [P, 2, 512]) for i in range(2)]
    stat = sb("stat", [P, 8, 32])
    f8 = act_t[0:8]
    tbl34 = sb("tbl34", [34, 12])
    avg = sb("avg", [P, P])
    eps_t = sb("eps_t", [P, 2])
    kv_c = sb("kv_c", [P, 16 + 2 * HD])
    rows_8 = sb_at("rows_8", [8, 8 * P], F32, base + 45056)
    cos, sin = (sb_at(n, [P, S], F32, base + 45056 + 4096 + at) for n, at in (("cos", 0), ("sin", 1024)))
    onehot = sb_at("onehot", [34, VEC], F32, lru_at[3])
    c_late, c_early = xn, sq.rearrange("p a s -> p (a s)")[:, 0:8 * P].rearrange("p (h s) -> p h s", h=8)

    bank = [nc.alloc_psum_tensor(f"bank{i}", [P, 512], F32)[:, :] for i in range(8)]
    two = lambda b: b.rearrange("p (a s) -> p a s", a=2)
    dense = [two(bank[0]), two(bank[1])]
    acc = [two(bank[i]) for i in range(2, 6)]
    misc = [two(bank[6]), two(bank[7])]

    def c(name):
        return con[:, CON[name]]

    loaded = [Counter(L, f"loaded{r}", 16) for r in range(RING)]
    used = Counter(L, "halves_used")
    hi_done, lo_done = Counter(L, "halves_hi"), Counter(L, "halves_lo")
    stream = A["stream"]

    def load(n, r):
        nc.sync.dma_start(raw[r], stream[bass.ds(n, 1)].rearrange("o p (k c) -> (o p) k c", k=HK)
                          ).then_inc(loaded[r].sem, 16)

    for r in range(RING):
        load(r, r)
    with nc.Fori(1, 2 * N_SLOTS // RING, engines=[mybir.EngineType.SP]) as i:
        for r in range(RING):
            nc.sync.wait_ge(lo_done.sem, i * RING + (r - RING + 1))
            load(i * RING + r, r)
    for r in range(2):
        nc.sync.wait_ge(lo_done.sem, 2 * N_SLOTS + r - RING + 1)
        load(2 * N_SLOTS + r, r)

    def split():
        for _ in range(2):
            m = hi_done.done
            r = m % RING
            loaded[r].done += 16
            free = used.at(m - RING + 1) if m >= RING else None
            act.wait(loaded[r].now(), free)
            hi = hi_done.did(AC.activation(w_hi[r], raw[r], ACT.Copy))
            dve.wait(hi, free)
            lo_done.did(V.tensor_tensor(w_lo[r], raw[r], w_hi[r].bitcast(F32), ALU.subtract))

    def halves(ahead=True):
        if hi_done.done == used.done:
            split()
        if ahead:
            split()
        for half in range(2):
            m = used.done
            pe.wait(lo_done.at(m + 1))
            yield half, m % RING
            assert used.done == m + 1

    def products(out, lhs, rhs, first):
        for j, (a, b) in enumerate([(lhs[0], rhs[0]), (lhs[0], rhs[1]), (lhs[1], rhs[0])]):
            m = T.matmul(out, a, b, start=first and j == 0, stop=True, skip_group_check=True)
        return m

    def tile(r, k, cols):
        return [t[r][:, k, cols] for t in (w_hi, w_lo)]

    def slot_T(out, hi, lo, ahead=True, cts=(0, 1), fed=None):
        for half, r in halves(ahead):
            if fed:
                pe.wait(fed[2 * half:2 * half + 2])
            for ct in cts:
                for k in range(HK):
                    m = products(out[:, ct, :], tile(r, k, slice(ct * P, (ct + 1) * P)),
                                 [t[:, half * HK + k, :] for t in (hi, lo)], half == 0 and k == 0 and ct == cts[0])
            got = used.did(m)
        return got

    def slot_rows(out, hi, lo, ahead=True):
        for half, r in halves(ahead):
            for rt in range(ST):
                for k in range(HK):
                    m = products(out[:, rt, :], [t[:, half * HK + k, rt * P:(rt + 1) * P] for t in (hi, lo)],
                                 tile(r, k, slice(0, COLS)), half == 0 and k == 0 and rt == 0)
            got = used.did(m)
        return got

    got_con, got_x, got_small = Counter(L, "got_con", 16), Counter(L, "got_x", 16), Counter(L, "got_small", 16)
    got_mem, got_pos, got_bias = Counter(L, "got_mem", 16), Counter(L, "got_pos", 16), Counter(L, "got_bias", 16)
    con_in = got_con.did(AC.dma_start(con, A["con"]))
    mem_in = got_mem.did(AC.dma_start(xn, A["mem"]))
    x_in = got_x.did(AC.dma_start(x, A["x"]))
    small_next = logit[1].rearrange("p a c -> p (a c)")[:, 0:SM_W]

    def fetch_small(n):
        return got_small.did(G.dma_start(small_next, A["small"][bass.ds(n, 1)].rearrange("o p c -> (o p) c")))

    got_small.did(G.dma_start(small_next, A["small"][0]))
    pos_raw = stat.rearrange("p a b -> p (a b)").bitcast(I32)
    pos_in = got_pos.did(G.dma_start(pos_raw, A["positions"]))
    bias_in = got_bias.did(G.dma_start(tbl34, A["rel_bias"]))
    early_in = got_bias.did(G.dma_start(onehot, A["early"][0:34, EARLY["onehot"]]))
    early_in = got_bias.did(G.dma_start(rows_8, A["early"][0:8, EARLY["nsel"]]))
    ones_set = pool.did(G.memset(ones, 1.0))
    avg_set = pool.did(G.memset(avg, 1.0 / D))
    row_set = pool.did(G.memset(ones_row, 1.0))

    def bias_vectors():
        pe.wait(early_in)
        m = pe.did(T.matmul(bank[1][0:12, 0:VEC], tbl34, onehot, start=True, stop=True))
        act.wait(m)
        m = act.did(AC.activation(vec_sb, bank[1][0:12, 0:VEC], ACT.Copy, scale=8.0))
        pool.wait(m)
        return wrote_vec.did(G.dma_start(A["skew"].rearrange("(p h v) -> h p v", h=12, v=VEC),
                                         vec_sb.unsqueeze(1).broadcast_to([12, P, VEC])))

    wrote_vec = Counter(L, "wrote_vec", 16)
    vec_sb = logit[0][0:12, 0, 0:VEC]

    root_f = root.rearrange("p a s -> p (a s)")
    rinv_f = rinv.rearrange("p a s -> p (a s)")
    pool.did(G.memset(eps_t[:, 0:1], EPS))
    eps_set = pool.did(G.memset(eps_t[:, 1:2], 1.0))
    eps, one = eps_t[:, 0:1], eps_t[:, 1:2]
    scale_2 = scale.unsqueeze(1).broadcast_to([P, 2, S])

    def pair_of(b):
        return slice(2 * b, 2 * b + 2)

    def load_sqrt():
        act.did(AC.activation(scale_col[:, 2:3], eps, ACT.Sqrt))

    def sum_squares(src_of, after, adder):
        for b in range(4):
            act.wait(after[b])
            m = act.did(AC.activation(sq[:, pair_of(b), :], src_of(b), ACT.Square))
            if b:
                adder.wait(m)
                m = adder.did(adder.eng.tensor_tensor(sq[:, 0:2, :], sq[:, 0:2, :], sq[:, pair_of(b), :], ALU.add))
                adder.wait(m)
        return m

    def mean_square(summed, out):
        pe.wait(summed)
        for k in range(2):
            m = T.matmul(out, avg, sq[:, k, :], start=k == 0, stop=k == 1)
        return pe.did(m)

    def inverse_root(src, w, ready, bias=eps):
        act.wait(ready)
        m = act.did(AC.activation(root_f[:, 0:w], src, ACT.Sqrt, bias=bias))
        dve.wait(m)
        return dve.did(V.reciprocal(rinv_f[:, 0:w], root_f[:, 0:w]))

    def norm_in(gain, hi, lo, update, free):
        load_sqrt()
        updated, his, marks = [], [], []
        act.wait(free)
        dve.wait(free)
        for b in range(5):
            if b < 4:
                updated.append(update(b))
                act.wait(updated[b])
                for k in (2 * b, 2 * b + 1):
                    m = act.did(AC.activation(hi[:, k, :], x[:, k, :], ACT.Copy, scale=gain[:, k:k + 1]))
                his.append(m)
            if b:
                dve.wait(his[b - 1])
                for k in (2 * b - 2, 2 * b - 1):
                    m = dve.did(V.scalar_tensor_tensor(lo[:, k, :], x[:, k, :], gain[:, k:k + 1],
                                                       hi[:, k, :].bitcast(F32), ALU.mult, ALU.subtract))
                marks.append(m)
        return marks, sum_squares(lambda b: x[:, pair_of(b), :], updated, pool)

    def norm_scale(summed, by_rows=False):
        m = mean_square(summed, misc[0][:, 0, :])
        if by_rows:
            for rt in range(ST):
                for k in range(2):
                    mm = T.matmul(misc[1][:, 0, rt:rt + 1], sq[:, k, rt * P:(rt + 1) * P], avg[:, 0:1],
                                  start=k == 0, stop=k == 1)
            m = pe.did(mm)
        act.wait(m)
        m = act.did(AC.activation(root[:, 0, :], misc[0][:, 0, :], ACT.Sqrt, bias=eps))
        if by_rows:
            m = act.did(AC.activation(scale_col[:, 2:4], misc[1][:, 0, 0:2], ACT.Sqrt, bias=eps))
        dve.wait(m)
        m = dve.did(V.reciprocal(scale, root[:, 0, :]))
        if by_rows:
            m = dve.did(V.reciprocal(scale_col[:, 0:2], scale_col[:, 2:4]))
        return m

    def norm_add(gain, ready, scaled=False):
        load_sqrt()
        if scaled:
            m = dve.did(V.scalar_tensor_tensor(root[:, 1, :], root[:, 0, :], EPS, root[:, 0, :], ALU.mult, ALU.mult))
        ms = mean_square(sum_squares(lambda b: acc[b], ready, dve), misc[0][:, 0, :])
        if scaled:
            dve.wait(m, ms)
            m = dve.did(V.tensor_tensor(root[:, 1, :], misc[0][:, 0, :], root[:, 1, :], ALU.add))
            r = inverse_root(root[:, 1, :], S, m, 0.0)
        else:
            r = inverse_root(misc[0][:, 0, :], S, ms)

        def update(b):
            dve.wait(r)
            for k in (2 * b, 2 * b + 1):
                n = dve.did(V.scalar_tensor_tensor(sq[:, k, :], acc[b][:, k % 2, :], gain[:, k:k + 1],
                                                   rinv[:, 0, :], ALU.mult, ALU.mult))
            dve.wait(n)
            return dve.did(V.tensor_tensor(x[:, pair_of(b), :], x[:, pair_of(b), :], sq[:, pair_of(b), :], ALU.add))
        return update

    def split_out(hi, lo, psum, ready):
        act.wait(ready)
        h = act.did(AC.activation(hi, psum, ACT.Copy))
        dve.wait(h)
        return dve.did(V.tensor_tensor(lo, psum, hi.bitcast(F32), ALU.subtract))

    def ffn(gain, update, last_ahead, free=None):
        before = [pe.now(), act.now(), dve.now()]
        fed, summed = norm_in(gain, xn_hi, xn_lo, update, free)
        act.wait(before)
        dve.wait(before)
        pe.wait(before)

        def gate(fed=None):
            return slot_T(dense[0], xn_hi, xn_lo, fed=fed)

        def silu(got):
            dve.wait(got, dve.now())
            g = dve.did(V.tensor_tensor(act_t, dense[0], scale_2, ALU.mult))
            act.wait(g)
            return g, act.did(AC.activation(act_t, act_t, ACT.Silu))

        def hidden(j, got, gated):
            at = bass.ds(j * 2, 2)
            dve.wait(got, gated)
            h = dve.did(V.tensor_tensor(act_t, act_t, dense[1], ALU.mult))
            act.wait(h)
            hh = act.did(AC.activation(hid_hi[:, at, :], act_t, ACT.Copy))
            dve.wait(hh)
            return h, dve.did(V.tensor_tensor(hid_lo[:, at, :], act_t, hid_hi[:, at, :].bitcast(F32), ALU.subtract))

        got = gate(fed)
        dve.wait(norm_scale(summed))
        read0, gated = silu(got)
        with L.run(FF // COLS - 1) as loop:
            pe.wait(loop.last("up read", dve.counter))
            up = slot_T(dense[1], xn_hi, xn_lo)
            read1, low = hidden(loop.i, up, loop.last("gated", act.counter))
            loop.keep("up read", read1)
            loop.keep("hidden", low)
            pe.wait(loop.last("gate read", dve.counter))
            read0, gated = silu(gate())
            loop.keep("gate read", read0)
            loop.keep("gated", gated)
        pe.wait(loop.ended("up read"))
        _, last_hidden = hidden(FF // COLS - 1, slot_T(dense[1], xn_hi, xn_lo), act.now())
        pe.wait(loop.ended("hidden"))

        def down(j, start, ahead=True):
            for k, r in halves(ahead):
                for ct in range(KT):
                    m = down_tile(j, k, r, ct, start)
                used.did(m)

        def down_tile(j, k, r, ct, start=False):
            w = [t[r].rearrange("p k c -> p (k c)")[:, ct * P:(ct + 1) * P] for t in (w_hi, w_lo)]
            h = [t[:, bass.ds(j * 2 + k, 1), :].rearrange("p o s -> p (o s)") for t in (hid_hi, hid_lo)]
            return products(acc[ct // 2][:, ct % 2, :], w, h, start and k == 0 and ct % 2 == 0)

        n = FT // 2
        down(0, True)
        with L.run((n - 3) // 2) as loop:
            down(loop.i * 2 + 1, False)
            down(loop.i * 2 + 2, False)
        down(n - 2, False)
        if last_ahead:
            split()
        m = used.done
        pe.wait(lo_done.at(m + 2), last_hidden)
        complete = []
        for ct in range(KT):
            for k in range(2):
                mm = down_tile(n - 1, k, (m + k) % RING, ct)
                if ct == KT - 1:
                    used.did(mm)
            if ct % 2:
                complete.append(used.now() if ct == KT - 1 else pe.did(mm))
        return complete

    def out_projection(hi, lo, ready, first_free, all_ready=None):
        pe.wait(ready, first_free)
        return [slot_T(acc[b], hi, lo, fed=[None, None, all_ready, None]) for b in range(4)]

    mem_g = c("mem_g")
    act.wait(mem_in, eps_set, con_in)
    dve.wait(con_in)
    pe.wait(avg_set)
    ms = mean_square(sum_squares(lambda b: xn[:, pair_of(b), :], [mem_in] * 4, dve), misc[0][:, 0, :])
    r = inverse_root(misc[0][:, 0, :], S, ms)
    dve.wait(r, mem_in)
    for b in range(4):
        for k in (2 * b, 2 * b + 1):
            n = dve.did(V.scalar_tensor_tensor(xn[:, k, :], xn[:, k, :], mem_g[:, k:k + 1], rinv[:, 0, :],
                                               ALU.mult, ALU.mult))
        act.wait(n)
        h = act.did(AC.activation(mem_hi[:, pair_of(b), :], xn[:, pair_of(b), :], ACT.Copy))
        dve.wait(h)
        mem_ready = dve.did(V.tensor_tensor(mem_lo[:, pair_of(b), :], xn[:, pair_of(b), :],
                                            mem_hi[:, pair_of(b), :].bitcast(F32), ALU.subtract))

    TWO_PI = 2 * np.pi
    C1 = 6.28125
    C2 = float((np.array([TWO_PI - C1], np.float32).view(np.uint32) & np.uint32(0xfffff000)).view(np.float32)[0])
    C3 = float(TWO_PI - C1 - C2)
    MAGIC = 1.5 * 2.0 ** 23
    posf, ang, turn, red = (probT[1][:, n // 2, (n % 2) * S:(n % 2 + 1) * S] for n in range(4))
    pool.wait(pos_in, con_in)
    p0 = pool.did(G.tensor_copy(posf, pos_raw))
    pool.wait(p0)
    p0 = pool.did(G.tensor_scalar(ang, posf, c("inv_freq"), None, ALU.mult))
    pool.wait(p0)
    for out, quarter in ((sin, 0.0), (cos, 0.25)):
        m = pool.did(G.tensor_scalar(turn, ang, 1.0 / TWO_PI, quarter, ALU.mult, ALU.add))
        for k in (MAGIC, -MAGIC):
            pool.wait(m)
            m = pool.did(G.tensor_scalar(turn, turn, k, None, ALU.add))
        pool.wait(m)
        for k, of in ((C1, ang), (C2, red), (C3, red)):
            m = pool.did(G.tensor_scalar(posf, turn, -k, None, ALU.mult))
            pool.wait(m)
            m = pool.did(G.tensor_tensor(red, posf, of, ALU.add))
            pool.wait(m)
        pool.wait(m)
        m = pool.did(G.tensor_scalar(red, red, quarter * TWO_PI, float(np.float32(3.1415925)), ALU.add, ALU.min))
        pool.wait(m)
        m = pool.did(G.tensor_scalar(red, red, -float(np.float32(3.1415925)), None, ALU.max))
        act.wait(m)
        trig = act.did(AC.activation(out, red, ACT.Sin))
        pool.wait(trig)


    def out_T(dst, r, got):
        dve.wait(got)
        return dve.did(V.tensor_tensor(dst, dense[r], scale_2, ALU.mult))

    def out_rows(dst, r, got):
        act.wait(got)
        for rt in range(ST):
            m = act.did(AC.activation(dst[:, rt, :], dense[r][:, rt, :], ACT.Copy, scale=scale_col[:, rt:rt + 1]))
        return m

    def causal_values(out, v_of, pT, first=True, last=True):
        T.matmul(out, v_of(0), pT[:, 0:S], start=first, stop=False, skip_group_check=True)
        return T.matmul(out[:, P:S], v_of(1), pT[:, S:S + P], start=False, stop=last, skip_group_check=True)

    def slot_of(t, n):
        return t[:, bass.ds(n, 1), :, :].rearrange("p o a s -> p (o a) s")

    def head_rows(h):
        return slice((h % 2) * HD, (h % 2 + 1) * HD)

    def start_layer():
        dve.wait(got_small.now(), pe.now(), act.now(), pool.now())
        m = dve.did(V.tensor_copy(small, small_next))
        for e in (dve, act, pe, pool):
            e.wait(m, pe.now(), act.now(), pool.now())

    skew_out = bias_vectors()
    split()
    with L.run(DEPTH) as layer:
        l = layer.i
        sm = lambda name: small[:, SM1[name]]
        start_layer()
        free = {0: dve.now(), 1: dve.now()}
        fed, summed = norm_in(sm("pre_mix"), xn_hi, xn_lo, lambda b: x_in, None)

        got = [slot_T(dense[0], xn_hi, xn_lo, fed=fed)]
        squares_read = norm_scale(summed, True)
        dve.wait(squares_read)
        got.append(slot_T(dense[1], xn_hi, xn_lo))
        for r in range(2):
            out_T(proj[:, r, :, :], r, got[r])
        with L.run(3) as loop:
            for r in range(2):
                pe.wait(loop.last(f"out{r}", dve.counter))
                loop.keep(f"out{r}", out_T(slot_of(proj, loop.i * 2 + (2 + r)), r, slot_T(dense[r], xn_hi, xn_lo)))
        pe.wait(dve.now())
        ly_done = out_T(proj[:, 8, :, :], 0, slot_T(dense[0], xn_hi, xn_lo))
        forget = slot_T(dense[1], xn_hi, xn_lo, cts=(0,))
        pe.wait(ly_done)
        v0_done = out_rows(proj[:, 10, :, :], 0, slot_rows(dense[0], xn_hi, xn_lo))

        dve.wait(forget)
        z = dve.did(V.tensor_tensor(f8[:, 0, :], dense[1][0:8, 0, :], scale[0:8, :], ALU.mult))
        forget_read = z
        act.wait(z)
        a = act.did(AC.activation(f8[:, 1, :], f8[:, 0, :], ACT.Abs, bias=small[0:8, SM1["fox_b"]]))
        dve.wait(z, a)
        z = dve.did(V.tensor_scalar(f8[:, 0, :], f8[:, 0, :], small[0:8, SM1["fox_b"]], 0.0, ALU.add, ALU.min))
        act.wait(a)
        a = act.did(AC.activation(f8[:, 1, :], f8[:, 1, :], ACT.Exp, scale=-1.0))
        act.wait(a)
        a = act.did(AC.activation(f8[:, 1, :], f8[:, 1, :], ACT.Ln, bias=one[0:8]))
        dve.wait(z, a)
        m = dve.did(V.tensor_tensor(f8[:, 0, :], f8[:, 0, :], f8[:, 1, :], ALU.subtract))
        dve.wait(m)
        m = dve.did(V.tensor_tensor_scan(f8[:, 1, :], ones_row, f8[:, 0, :], 0.0, ALU.mult, ALU.add))
        dve.wait(m)
        c_ready = dve.did(V.tensor_scalar(f8[:, 1, :], f8[:, 1, :], 8.0, None, ALU.mult))

        pe.wait(forget_read)
        v1_done = out_rows(proj[:, 11, :, :], 1, slot_rows(dense[1], xn_hi, xn_lo))
        dve.wait(squares_read)
        read = {}
        pe.wait(c_ready)
        for h in range(8):
            pe.wait(read.get(h - 4))
            nsel = rows_8[:, h * P:(h + 1) * P]
            m = pe.did(T.matmul(acc[h % 4][:, 0, :], nsel, f8[:, 1, :], start=True, stop=True))
            dve.wait(m)
            dve.did(V.tensor_tensor(c_late[:, h, :], acc[h % 4][:, 0, :], c("causal"), ALU.add))
            read[h] = dve.did(V.tensor_tensor(c_early[:, h, :], acc[h % 4][:, 0, 0:P], c("causal")[:, P:S], ALU.add))
        pe.wait(v0_done)
        rv_done = out_rows(proj[:, 12, :, :], 0, slot_rows(dense[0], xn_hi, xn_lo))
        pe.wait(v1_done, rv_done, mem_ready)
        free = {0: rv_done, 1: v1_done}
        filled = []

        mem_kv = [proj[:, 9, :, :], probT[0][:, 1, :], probT[1][:, 1, :], logit[0][:, 1, :],
                  proj[:, 7, :, :], proj[:, 8, :, :], xc, lru_r]
        mem_kv = [t if len(t.shape) == 3 else t.rearrange("p (a s) -> p a s", a=2) for t in mem_kv]

        def memory_slot():
            n = len(filled)
            read_memory_slot()
            pe.wait(free[n % 2])
            filled.append((slot_T if n < 4 else slot_rows)(dense[n % 2], mem_hi, mem_lo))

        def read_memory_slot():
            if filled:
                n = len(filled) - 1
                act.wait(filled[n], dve.now())
                free[n % 2] = act.did(AC.activation(mem_kv[n], dense[n % 2], ACT.Copy))

        lx, ly = proj[:, 7, :, :], proj[:, 8, :, :]
        dve.wait(ly_done)
        for ct in range(2):
            w = lambda n: small[:, SM1["conv_w"].start + 2 * n + ct:SM1["conv_w"].start + 2 * n + ct + 1]
            m = dve.did(V.tensor_scalar(xc[:, ct, :], lx[:, ct, :], w(3), sm("conv_b")[:, ct:ct + 1], ALU.mult, ALU.add))
            for n in (2, 1, 0):
                back = 3 - n
                dve.wait(m)
                m = dve.did(V.scalar_tensor_tensor(xc[:, ct, back:S], lx[:, ct, 0:S - back], w(n), xc[:, ct, back:S],
                                                   ALU.mult, ALU.add))
        xc_done = m
        pe.wait(xc_done)
        for dst, name in ((misc[0], "w_rg"), (misc[1], "w_ig")):
            for ct in range(2):
                m = T.matmul(dst[:, ct, :], sm(name)[:, ct * P:(ct + 1) * P], xc[:, ct, :], start=True, stop=True)
        gated = pe.did(m)
        act.wait(gated)
        for dst, src, b in ((lru_r, misc[0], "b_rg"), (lru_i, misc[1], "b_ig")):
            for ct in range(2):
                m = act.did(AC.activation(dst[:, ct, :], src[:, ct, :], ACT.Sigmoid, bias=sm(b)[:, ct:ct + 1]))
        memory_slot()
        st = lambda n, w=2: stat[:, n, 0:w]
        a = act.did(AC.activation(st(0), sm("lam"), ACT.Abs))
        act.wait(a)
        a = act.did(AC.activation(st(0), st(0), ACT.Exp, scale=-1.0))
        act.wait(a)
        a = act.did(AC.activation(st(0), st(0), ACT.Ln, bias=one))
        sp0 = dve.did(V.tensor_scalar(st(1), sm("lam"), -1.0, 0.0, ALU.mult, ALU.max))
        dve.wait(sp0, a)
        sp0 = dve.did(V.tensor_tensor(st(1), st(1), st(0), ALU.add))
        dve.wait(sp0)
        dve.did(V.tensor_scalar(st(2), st(1), -8.0, None, ALU.mult))
        sp = dve.did(V.tensor_scalar(st(3), st(1), 8.0, None, ALU.mult))
        act.wait(m, sp)
        for ct in range(2):
            ea = act.did(AC.activation(lru_a[:, ct, :], lru_r[:, ct, :], ACT.Exp, scale=stat[:, 2, ct:ct + 1]))
            act.wait(ea)
            th = act.did(AC.activation(lru_t[:, ct, :], lru_r[:, ct, :], ACT.Tanh, scale=stat[:, 3, ct:ct + 1]))
        memory_slot()
        dve.wait(th)
        m = dve.did(V.tensor_tensor(lru_u, lru_a, lru_a, ALU.mult))
        dve.wait(m)
        m = dve.did(V.scalar_tensor_tensor(lru_u, lru_u, 1.0, lru_t, ALU.add, ALU.mult))
        act.wait(m)
        m = act.did(AC.activation(lru_u, lru_u, ACT.Sqrt))
        g = act.did(AC.activation(lru_g, ly, ACT.Gelu_apprx_tanh))
        m2 = dve.did(V.tensor_tensor(lru_i, lru_i, xc, ALU.mult))
        dve.wait(m, m2)
        m = dve.did(V.tensor_tensor(lru_u, lru_u, lru_i, ALU.mult))
        dve.wait(m)
        for ct in range(2):
            m = dve.did(V.tensor_tensor_scan(lru_h[:, ct, :], lru_a[:, ct, :], lru_u[:, ct, :], 0.0, ALU.mult, ALU.add))
        dve.wait(m, g)
        m = dve.did(V.tensor_tensor(lru_h, lru_h, lru_g, ALU.mult))
        split_out(y_hi[:, 0:2, :], y_lo[:, 0:2, :], lru_h, m)

        memory_slot()

        rq, rk, rg = proj[:, 4, :, :], proj[:, 5, :, :], proj[:, 6, :, :]
        rot_done = []
        for n, src in enumerate((rq, rk)):
            m = pe.did(T.matmul(misc[n].rearrange("p a s -> p (a s)"), c("rot"), src.rearrange("p a s -> p (a s)"),
                                start=True, stop=True))
            dve.wait(m)
            dst = (lru_a, lru_t)[n]
            other = (lru_u, lru_h)[n]
            dve.wait(act.now())
            a1 = dve.did(V.tensor_tensor(dst, src, cos.unsqueeze(1).broadcast_to([P, 2, S]), ALU.mult))
            a2 = dve.did(V.tensor_tensor(other, misc[n], sin.unsqueeze(1).broadcast_to([P, 2, S]), ALU.mult))
            dve.wait(a2)
            rot_done.append(dve.did(V.tensor_tensor(dst, dst, other, ALU.add)))

        def fox_scores(h):
            q, k = proj[head_rows(h), h // 4, (h // 2) % 2, :], proj[head_rows(h), 2 + h // 4, (h // 2) % 2, :]
            out = acc[h % 2].rearrange("p a s -> p (a s)")
            pe.wait(scored.get(h - 2))
            for rt, cols, nk in ((1, slice(0, S), S), (0, slice(S, S + P), P)):
                m = T.matmul(out[:, cols], q[:, rt * P:(rt + 1) * P], k[:, 0:nk], start=True, stop=True)
            return pe.did(m)

        def fox_softmax(h, ready):
            src = acc[h % 2].rearrange("p a s -> p (a s)")
            lg = logit[h % 2][:, 0, :]
            s4 = stat[:, 0:4, 16 + 2 * (h % 2):18 + 2 * (h % 2)]
            dve.wait(ready, transposed.get(h - 2))
            dve.settle()
            dve.did(V.tensor_tensor_reduce(lg[:, 0:S], src[:, 0:S], c_late[:, h, :], 1.0, LOWEST, ALU.add, ALU.max, s4[:, 0, 0:1]))
            m = dve.did(V.tensor_tensor_reduce(lg[:, S:S + P], src[:, S:S + P], c_early[:, h, :], 1.0, LOWEST,
                                               ALU.add, ALU.max, s4[:, 0, 1:2]))
            scored[h] = m
            dve.wait(m)
            m = dve.did(V.tensor_scalar(s4[:, 1, :], s4[:, 0, :], -0.125, None, ALU.mult))
            act.wait(m)
            act.did(AC.activation(lg[:, 0:S], lg[:, 0:S], ACT.Exp, bias=s4[:, 1, 0:1], scale=0.125,
                                  accum_out=s4[:, 2, 0:1]))
            m = act.did(AC.activation(lg[:, S:S + P], lg[:, S:S + P], ACT.Exp, bias=s4[:, 1, 1:2], scale=0.125,
                                      accum_out=s4[:, 2, 1:2]))
            dve.wait(m)
            m = dve.did(V.reciprocal(s4[:, 3, :], s4[:, 2, :]))
            dve.wait(m)
            dve.did(V.tensor_scalar(lg[:, 0:S], lg[:, 0:S], s4[:, 3, 0:1], None, ALU.mult))
            return dve.did(V.tensor_scalar(lg[:, S:S + P], lg[:, S:S + P], s4[:, 3, 1:2], None, ALU.mult))

        def causal_transpose(n, lg, dst_bank, dst, ready, free):
            pe.wait(ready, free)
            for to, frm in ((0, S), (1, 0), (2, P)):
                m = T.transpose(dst_bank[:, to * P:(to + 1) * P], lg[:, frm:frm + P], c("ident"))
            m = pe.did(m)
            transposed[n] = m
            act.wait(m, free)
            return act.did(AC.activation(dst[:, 0:384], dst_bank[:, 0:384], ACT.Copy))

        scored, transposed, valued, ysplit, probs, pTs = {}, {}, {}, {}, {}, {}
        dve.wait(skew_out)
        for n in range(8 + 2):
            if n < 8:
                s = fox_scores(n)
                probs[n] = fox_softmax(n, s)
            if n in (1, 4):
                memory_slot()
            if 1 <= n < 9:
                h = n - 1
                pTs[h] = causal_transpose(h, logit[h % 2][:, 0, :], bank[4 + h % 2], probT[h % 2][:, 0, :],
                                          probs[h], valued.get(h - 2))
            if n >= 2:
                h = n - 2
                o = misc[(h // 2) % 2][:, 0, :]
                pe.wait(pTs[h], ysplit.get(h // 2 - 2))
                v = lambda kt: proj[:, 10 + h // 4, kt, (h % 4) * HD:(h % 4 + 1) * HD]
                valued[h] = pe.did(causal_values(o[head_rows(h), :], v, probT[h % 2][:, 0, :]))
                if h % 2:
                    ysplit[h // 2] = split_out(y_hi[:, 2 + h // 2, :], y_lo[:, 2 + h // 2, :], o, valued[h])
        fox_done = ysplit[3]

        pe.wait(rot_done[1])
        read = {}
        for h in range(4):
            q, k = lru_a[head_rows(h), h // 2, :], lru_t[head_rows(h), h // 2, :]
            b = acc[h % 2].rearrange("p a s -> p (a s)")
            pe.wait(read.get(h - 2))
            T.matmul(b[:, 0:S], k[:, 0:P], q[:, :], start=True, stop=True)
            m = pe.did(T.matmul(b[:, S:S + P], k[:, P:S], q[:, P:S], start=True, stop=True))
            dve.wait(m, read.get(("v", h - 2)))
            dec = con[:, CON["decay"].start + h * S:CON["decay"].start + (h + 1) * S]
            dve.did(V.tensor_tensor(probT[h % 2][:, 0, 0:S], b[:, 0:S], dec, ALU.mult))
            read[h] = dve.did(V.tensor_tensor(probT[h % 2][:, 0, S:S + P], b[:, S:S + P], dec[:, 0:P], ALU.mult))
            v = lambda kt: proj[:, 12, kt, h * HD:(h + 1) * HD]
            if h == 0:
                memory_slot()
            pe.wait(read[h])
            read[("v", h)] = pe.did(causal_values(acc[2 + h // 2][head_rows(h), 0, :], v, probT[h % 2][:, 0, :]))
        yr = lru_u
        act.wait(read[("v", 3)])
        for t in range(2):
            m = act.did(AC.activation(yr[:, t, :], acc[2 + t][:, 0, :], ACT.Copy))
        yr_read = m
        pe.wait(m)
        mean = pe.did(T.matmul(bank[6], c("blk"), yr.rearrange("p a s -> p (a s)"), start=True, stop=True))
        dve.wait(mean)
        m = dve.did(V.tensor_tensor(yr, yr, misc[0], ALU.subtract))
        memory_slot()
        act.wait(m)
        m = act.did(AC.activation(lru_h, yr, ACT.Square))
        pe.wait(m)
        var = pe.did(T.matmul(bank[7], c("blk"), lru_h.rearrange("p a s -> p (a s)"), start=True, stop=True))
        r = inverse_root(bank[7], 512, var)
        memory_slot()
        sg = act.did(AC.activation(lru_g, rg, ACT.Silu))
        dve.wait(r)
        m = dve.did(V.tensor_tensor(yr, yr, rinv, ALU.mult))
        dve.wait(m, sg)
        m = dve.did(V.tensor_tensor(yr, yr, lru_g, ALU.mult))
        ret_done = split_out(y_hi[:, 6:8, :], y_lo[:, 6:8, :], yr, m)

        read_memory_slot()
        got = out_projection(y_hi, y_lo, fox_done, yr_read, ret_done)
        update = norm_add(sm("post_mix"), got)

        fed, summed = norm_in(sm("pre_cross"), xn_hi, xn_lo, update, None)
        for n in range(4):
            pe.wait(free.get(n))
            got = slot_T(dense[n % 2], xn_hi, xn_lo, fed=fed if n == 0 else None)
            if n == 0:
                dve.wait(norm_scale(summed))
            free[n + 2] = out_T(proj[:, n, :, :], n % 2, got)
        pe.wait(free[4], free[5])
        scored, transposed, valued, ysplit, probs, pTs = {}, {}, {}, {}, {}, {}
        for n in range(4 + 2):
            if n < 4:
                h = n
                pe.wait(scored.get(h - 2))
                for rt in range(2):
                    for dt in range(2):
                        m = T.matmul(acc[h % 2][:, rt, :], proj[:, h, dt, rt * P:(rt + 1) * P], mem_kv[h][:, dt, :],
                                     start=dt == 0, stop=dt == 1)
                m = pe.did(m)
                s4 = stat[:, 0:4, 16 + 2 * (h % 2):18 + 2 * (h % 2)]
                dve.wait(m, scored.get(h - 2))
                m = dve.did(V.tensor_reduce(s4[:, 0, :], acc[h % 2], AX.X, ALU.max))
                dve.wait(m)
                m = dve.did(V.tensor_scalar(s4[:, 1, :], s4[:, 0, :], -0.0625, None, ALU.mult))
                act.wait(m, transposed.get(h - 2))
                for rt in range(2):
                    m = act.did(AC.activation(logit[h % 2][:, 0, rt * S:(rt + 1) * S], acc[h % 2][:, rt, :], ACT.Exp,
                                              bias=s4[:, 1, rt:rt + 1], scale=0.0625, accum_out=s4[:, 2, rt:rt + 1]))
                scored[h] = m
                dve.wait(m)
                m = dve.did(V.reciprocal(s4[:, 3, :], s4[:, 2, :]))
                dve.wait(m)
                for rt in range(2):
                    probs[h] = dve.did(V.tensor_scalar(logit[h % 2][:, 0, rt * S:(rt + 1) * S],
                                                       logit[h % 2][:, 0, rt * S:(rt + 1) * S],
                                                       s4[:, 3, rt:rt + 1], None, ALU.mult))
            if 1 <= n < 5:
                h = n - 1
                pe.wait(probs[h], pTs.get(h - 1))
                for kt in range(2):
                    for rt in range(2):
                        m = T.transpose(bank[4 + h % 2][:, kt * S + rt * P:kt * S + (rt + 1) * P],
                                        logit[h % 2][:, 0, rt * S + kt * P:rt * S + (kt + 1) * P], c("ident"))
                transposed[h] = pe.did(m)
                act.wait(transposed[h], valued.get(h - 2))
                pTs[h] = act.did(AC.activation(probT[h % 2][:, 0, :], bank[4 + h % 2], ACT.Copy))
            if n >= 2:
                h = n - 2
                pe.wait(pTs[h], ysplit.get(h - 2))
                for dt in range(2):
                    for kt in range(2):
                        m = T.matmul(misc[h % 2][:, dt, :], mem_kv[4 + h][:, kt, dt * P:(dt + 1) * P],
                                     probT[h % 2][:, 0, kt * S:(kt + 1) * S], start=kt == 0, stop=kt == 1)
                valued[h] = pe.did(m)
                ysplit[h] = split_out(y_hi[:, 2 * h:2 * h + 2, :], y_lo[:, 2 * h:2 * h + 2, :], misc[h % 2], valued[h])
        got = out_projection(y_hi, y_lo, ysplit[3], None)
        pool.wait(got)
        fetch_small(l + 1)
        got = ffn(sm("pre_ffn"), norm_add(sm("post_cross"), got), True)
        update = norm_add(sm("post_ffn"), got, True)
        for b in range(4):
            x_ready = update(b)

    got_table = Counter(L, "got_table", 16)
    pool.wait(skew_out, pe.now())
    by_row = A["skew"][P - 1:P - 1 + P * (12 * VEC - 1)].rearrange("(p v) -> p v", v=12 * VEC - 1)
    got_table.did(G.dma_start(table[:, 0:11, :], by_row[:, 0:11 * VEC].rearrange("p (h v) -> p h v", v=VEC)[:, :, 0:S]))
    table_in = got_table.did(G.dma_start(table[:, 11, :], by_row[:, 11 * VEC:11 * VEC + S]))

    with L.run(DEPTH) as layer:
        l = layer.i
        sm = lambda name: small[:, SM2[name]]
        start_layer()
        wg = sm("w_gate").rearrange("p (k n) -> p k n", k=KT)
        wg_ready = dve.did(V.tensor_tensor(wg, wg, sm("mix").unsqueeze(2).broadcast_to([P, KT, 24]), ALU.mult))

        def half_ffn(gain, update, last_ahead, free=None):
            got = ffn(gain, update, last_ahead, free)

            def add(b):
                dve.wait(got[b])
                m = dve.did(V.scalar_tensor_tensor(sq[:, pair_of(b), :], acc[b], 0.5, scale_2, ALU.mult, ALU.mult))
                dve.wait(m)
                return dve.did(V.tensor_tensor(x[:, pair_of(b), :], x[:, pair_of(b), :], sq[:, pair_of(b), :], ALU.add))
            return add

        update = half_ffn(sm("ffn1"), lambda b: None, True)
        fed, summed = norm_in(sm("mix"), xn_hi, xn_lo, update, pe.now())

        free, slots_out = {0: None, 1: None}, {}

        def project(slot, form=slot_T):
            r = slot % 2
            pe.wait(free[r])
            out = out_T if form is slot_T else out_rows
            slots_out[slot] = free[r] = out(proj[:, slot, :, :], r, form(dense[r], xn_hi, xn_lo))

        got = slot_T(dense[0], xn_hi, xn_lo, fed=fed)
        act.wait(got)
        dve.wait(norm_scale(summed, True), got)
        slots_out[0] = free[0] = out_T(proj[:, 0, :, :], 0, got)
        for n in range(1, 4):
            project(n)

        def swa_kv(out, hi, lo):
            for half, r in halves():
                for k in range(HK):
                    a = [t[:, half * HK + k, :] for t in (hi, lo)]
                    products(out[:, 0, :], tile(r, k, slice(0, P)), a, half == 0 and k == 0)
                    for rt in range(ST):
                        mm = products(out[:, 1, rt * P:(rt + 1) * P], [t[:, rt * P:(rt + 1) * P] for t in a],
                                      tile(r, k, slice(P, 2 * P)), False)
                got = used.did(mm)
            return got

        norm_n = [0]
        root_read = [None, None]

        def squares(tiles, ready):
            n, w = norm_n[0], tiles.shape[1]
            norm_n[0] += 1
            dst = sq[:, 2 * (n % 4):2 * (n % 4) + w, :]
            act.wait(ready, squares_read.get(n - 4))
            return n, act.did(AC.activation(dst, tiles, ACT.Square))

        squares_read, roots_read = {}, {}

        def head_norm(tiles, gain, squared):
            n, m = squared
            w = tiles.shape[1]
            b = bank[4 + n % 2]
            pe.wait(m, roots_read.get(n - 2))
            squares_read[n] = m = pe.did(T.matmul(
                b[:, 0:w * S], c("blk"), sq[:, 2 * (n % 4):2 * (n % 4) + w, :].rearrange("p a s -> p (a s)"),
                start=True, stop=True))
            act.wait(m, root_read[0])
            roots_read[n] = m = act.did(AC.activation(root_f[:, 0:w * S], b[:, 0:w * S], ACT.Sqrt, bias=eps))
            dve.wait(m, root_read[1])
            root_read[0] = m = dve.did(V.reciprocal(rinv_f[:, 0:w * S], root_f[:, 0:w * S]))
            dve.wait(m)
            root_read[1] = dve.did(V.scalar_tensor_tensor(tiles, tiles, gain, rinv[:, 0:w, :], ALU.mult, ALU.mult))
            return root_read[1]

        cmp_w = 2 * N_CMP
        blocks = act_t.rearrange("p a s -> p (a s)")[:, 0:16 * cmp_w].rearrange("p (t n) -> p t n", n=cmp_w)
        hid_c = [logit[1][:, 0, 64 * n:64 * n + 2 * cmp_w].rearrange("p (t n) -> p t n", n=cmp_w) for n in range(2)]
        k_root = logit[1][:, 0, 256:256 + N_CMP]
        kc = kv_c[:, 0:N_CMP]
        vc = kv_c[0:N_CMP, 16:16 + 2 * HD]
        parts = {}

        def cmp_parts(which):
            return [t[:, 2 * which:2 * which + 2, :].rearrange("p a s -> p (a s)")[:, 0:16 * cmp_w]
                    .rearrange("p (t n) -> p t n", n=cmp_w) for t in (y_hi, y_lo)]

        def cmp_blocks(which, ready):
            src = proj[:, 3, which, :]
            dve.wait(ready, parts.get(0))
            for g in range(2):
                for par in range(2):
                    rs, ps_ = slice(par * HD, (par + 1) * HD), slice(g * HD, (g + 1) * HD)
                    by_two = src[ps_, :].rearrange("p (n t q) -> p t n q", t=8, q=2)
                    for u in range(2):
                        m = dve.did(V.tensor_copy(blocks[rs, 8 * u:8 * u + 8, g * N_CMP:(g + 1) * N_CMP],
                                                  by_two[:, :, u:u + N_CMP, par]))
            dve.wait(m)
            for g in range(2):
                pos = small[:, SM2["cmp_pos"]].unsqueeze(2).broadcast_to([P, 16, N_CMP])
                m = dve.did(V.tensor_tensor(blocks[:, :, g * N_CMP:(g + 1) * N_CMP],
                                            blocks[:, :, g * N_CMP:(g + 1) * N_CMP], pos, ALU.add))
            parts[which] = split_out(*cmp_parts(which), blocks, m)

        hid_rows = [logit[0][0:cmp_w, 0, S * n:S * (n + 1)] for n in range(2)]

        def cmp_hidden(which, part):
            out = bank[2][0:cmp_w, 0:COLS]
            pe.wait(parts[which], parts.get(("hid", 0)))
            for half, r in halves():
                for k in range(HK):
                    b = [t[:, part * KT + half * HK + k, :] for t in cmp_parts(which)]
                    mm = products(out, b, tile(r, k, slice(0, COLS)), part == half == k == 0)
                m = used.did(mm)
            if part == 1:
                act.wait(m)
                parts[("hid", which)] = act.did(AC.activation(hid_rows[which], out, ACT.Silu))

        def cmp_turn(which):
            pe.wait(parts[("hid", which)], parts.get(("turned", 0)))
            pe.settle()
            for t in range(2):
                mm = T.transpose(bank[3][:, t * 32:t * 32 + cmp_w], hid_rows[which][:, t * P:(t + 1) * P],
                                 c("ident")[0:cmp_w, 0:cmp_w])
            m = pe.did(mm)
            act.wait(m)
            turned = bank[3][:, 0:64].rearrange("p (t n) -> p t n", t=2)[:, :, 0:cmp_w]
            parts[("turned", which)] = act.did(AC.activation(hid_c[which], turned, ACT.Copy))

        def cmp_out(which):
            w2 = small[:, SM2["w2v" if which else "w2k"]].rearrange("p (t d) -> p t d", t=2)
            pe.wait(parts[("turned", which)])
            for g in range(2):
                for t in range(2):
                    h = hid_c[which][:, t, g * N_CMP:(g + 1) * N_CMP]
                    if which == 0:
                        mm = T.matmul(misc[0][g * HD:(g + 1) * HD, 0, 0:N_CMP], w2[:, t, :], h, start=t == 0, stop=t == 1)
                    else:
                        mm = T.matmul(misc[1][0:N_CMP, 0, g * HD:(g + 1) * HD], h, w2[:, t, :], start=t == 0, stop=t == 1)
            m = pe.did(mm)
            act.wait(m)
            if which:
                return act.did(AC.activation(vc, misc[1][0:N_CMP, 0, 0:P], ACT.Copy))
            act.did(AC.activation(kc, misc[0][:, 0, 0:N_CMP], ACT.Copy))
            return act.did(AC.activation(k_root, misc[0][:, 0, 0:N_CMP], ACT.Square))

        def cmp_k_norm(ready):
            pe.wait(ready)
            m = pe.did(T.matmul(misc[0][:, 1, 0:N_CMP], c("blk"), k_root, start=True, stop=True))
            act.wait(m)
            m = act.did(AC.activation(k_root, misc[0][:, 1, 0:N_CMP], ACT.Sqrt, bias=eps))
            dve.wait(m)
            m = dve.did(V.reciprocal(k_root, k_root))
            dve.wait(m)
            return dve.did(V.scalar_tensor_tensor(kc, kc, sm("nsa_k"), k_root, ALU.mult, ALU.mult))

        m = slots_out[3]
        cmp_blocks(0, m)
        s0, s1, s2 = (squares(proj[:, n, :, :], m) for n in range(3))
        project(4)
        head_norm(proj[:, 0, :, :], sm("nsa_q"), s0)
        project(5)
        cmp_blocks(1, m)
        cmp_hidden(0, 0)
        head_norm(proj[:, 1, :, :], sm("nsa_q"), s1)
        project(6)
        s3 = squares(proj[:, 6, :, :], slots_out[6])
        cmp_hidden(0, 1)
        head_norm(proj[:, 2, :, :], sm("nsa_k"), s2)
        pe.wait(free[1])
        got = swa_kv(dense[1], xn_hi, xn_lo)
        dve.wait(got)
        k7 = dve.did(V.tensor_tensor(proj[:, 7, 0, :], dense[1][:, 0, :], scale, ALU.mult))
        act.wait(got, k7)
        for rt in range(ST):
            m = act.did(AC.activation(proj[:, 7, 1, rt * P:(rt + 1) * P], dense[1][:, 1, rt * P:(rt + 1) * P], ACT.Copy,
                                      scale=scale_col[:, rt:rt + 1]))
        slots_out[7] = free[1] = m
        s4 = squares(proj[:, 7, 0:1, :], slots_out[7])
        cmp_turn(0)
        cmp_hidden(1, 0)
        k_in = cmp_out(0)
        head_norm(proj[:, 6, :, :], sm("swa_q"), s3)
        project(8, slot_rows)
        cmp_hidden(1, 1)
        head_norm(proj[:, 7, 0:1, :], sm("swa_k"), s4)
        cmp_k_norm(k_in)
        gate24 = stat[:, 4:6, 0:24]
        pe.wait(wg_ready)
        pe.wait(roots_read[4])
        for rt in range(2):
            for k in range(KT):
                mm = T.matmul(bank[4][:, rt * 24:(rt + 1) * 24], x[:, k, rt * P:(rt + 1) * P], wg[:, k, :],
                              start=k == 0, stop=k == KT - 1)
        gate_in = pe.did(mm)
        cmp_turn(1)
        project(9, slot_rows)
        cmp_out(1)
        act.wait(gate_in)
        for rt in range(ST):
            gate_ready = act.did(AC.activation(gate24[:, rt, :], bank[4][:, rt * 24:(rt + 1) * 24], ACT.Sigmoid,
                                               scale=scale_col[:, rt:rt + 1]))
        pending, gate_slots = [], iter(range(12))

        def gate_slot():
            n = next(gate_slots)
            read_gate_slot()
            pe.wait(free[n % 2])
            pending.append((n, slot_T(dense[n % 2], xn_hi, xn_lo)))

        def read_gate_slot():
            if pending:
                n, got = pending.pop()
                free[n % 2] = out_T(gates[:, 2 * n:2 * n + 2, :], n % 2, got)

        CL, CE = slice(384, 384 + N_CMP), slice(384 + N_CMP, 384 + N_CMP + N_CMP0)
        scored, transposed, valued, ysplit, pTs = {}, {}, {}, {}, {}
        for e in (pe, act, dve):
            e.wait(pe.now(), act.now(), dve.now())

        def nsa_scores(h):
            g, t = h // 4, h % 4
            pr = slice(g * HD, (g + 1) * HD)
            q = proj[pr, t // 2, t % 2, :]
            pe.wait(scored.get(h - 1))
            for b in range(2):
                k, out = proj[pr, 2, b, :], bank[2 + b]
                T.matmul(out[:, 0:S], q[:, P:S], k, start=True, stop=True)
                mm = T.matmul(out[:, S:S + P], q[:, 0:P], k[:, 0:P], start=True, stop=True)
                if b == 0:
                    T.matmul(out[:, CL], q[:, P:S], kc[pr, :], start=True, stop=True)
                    mm = T.matmul(out[:, CE], q[:, 0:P], kc[pr, 0:N_CMP0], start=True, stop=True)
            return pe.did(mm)

        spans = [(0, slice(0, S), slice(0, S)), (1, slice(0, S), slice(0, S)), (0, CL, slice(31, S, 16)),
                 (0, slice(S, S + P), slice(P, S)), (1, slice(S, S + P), slice(P, S)), (0, CE, slice(P + 31, S, 16))]

        def nsa_exps(h, ready):
            lg = logit[h % 2]
            s6 = stat[:, 0:4, 8 * (h % 2):8 * (h % 2) + 6]
            dve.wait(ready, transposed.get(h - 2))
            dve.settle()
            for n, (b, cols, tc) in enumerate(spans):
                m = dve.did(V.tensor_tensor_reduce(lg[:, b, cols], bank[2 + b][:, cols], table[:, h, tc], 1.0, LOWEST,
                                                   ALU.add, ALU.max, s6[:, 0, n:n + 1]))
            scored[h] = m
            dve.wait(m)
            m = dve.did(V.tensor_scalar(s6[:, 1, :], s6[:, 0, :], -0.125, None, ALU.mult))
            act.wait(m)
            for n, (b, cols, tc) in enumerate(spans):
                m = act.did(AC.activation(lg[:, b, cols], lg[:, b, cols], ACT.Exp, bias=s6[:, 1, n:n + 1], scale=0.125,
                                          accum_out=s6[:, 2, n:n + 1]))
            return m

        def nsa_weights(h, ready):
            lg = logit[h % 2]
            s6 = stat[:, 0:4, 8 * (h % 2):8 * (h % 2) + 6]
            dve.wait(ready, gate_ready)
            m = dve.did(V.reciprocal(s6[:, 3, :], s6[:, 2, :]))
            dve.wait(m)
            for rt, at in ((1, 0), (0, 3)):
                dve.did(V.tensor_tensor(s6[:, 3, at:at + 2], s6[:, 3, at:at + 2], gate24[:, rt, 8 + h:24:8], ALU.mult))
                m = dve.did(V.tensor_tensor(s6[:, 3, at + 2:at + 3], s6[:, 3, at + 2:at + 3], gate24[:, rt, h:h + 1], ALU.mult))
            dve.wait(m)
            m = dve.did(V.tensor_tensor(s6[:, 3, 5:6], s6[:, 3, 5:6], c("late"), ALU.mult))
            dve.wait(m)
            for n, (b, cols, tc) in enumerate(spans):
                m = dve.did(V.tensor_scalar(lg[:, b, cols], lg[:, b, cols], s6[:, 3, n:n + 1], None, ALU.mult))
            return m

        def nsa_transpose(h, ready):
            lg = logit[h % 2]
            pe.wait(ready, pTs.get(h - 1))
            for b in range(2):
                for to, frm in ((0, S), (1, 0), (2, P)):
                    mm = T.transpose(bank[4 + b][:, to * P:(to + 1) * P], lg[:, b, frm:frm + P], c("ident"))
            T.transpose(bank[6][0:N_CMP0, 0:P], lg[:, 0, CE], c("ident"))
            mm = T.transpose(bank[6][0:N_CMP, P:S], lg[:, 0, CL], c("ident"))
            transposed[h] = pe.did(mm)
            act.wait(transposed[h], valued.get(h - 2))
            dve.wait(transposed[h], valued.get(h - 2))
            cp = sq[0:N_CMP, h % 2, :]
            act.did(AC.activation(cp[0:N_CMP0, 0:P], bank[6][0:N_CMP0, 0:P], ACT.Copy))
            act.did(AC.activation(cp[:, P:S], bank[6][0:N_CMP, P:S], ACT.Copy))
            a = act.did(AC.activation(probT[h % 2][:, 0, 0:384], bank[4][:, 0:384], ACT.Copy))
            d = dve.did(V.tensor_copy(probT[h % 2][:, 1, 0:384], bank[5][:, 0:384]))
            pTs[h] = [a, d]

        def nsa_values(h):
            g, t = h // 4, h % 4
            pr = slice(g * HD, (g + 1) * HD)
            o = bank[7][pr, 0:S]
            cp = sq[0:N_CMP, h % 2, :]
            pe.wait(pTs[h], ysplit.get(h - 1))
            for b in range(2):
                v = lambda kt: proj[:, 8, kt, b * P + g * HD:b * P + (g + 1) * HD]
                causal_values(o, v, probT[h % 2][:, b, :], b == 0, False)
            T.matmul(o[:, 0:P], vc[0:N_CMP0, pr], cp[0:N_CMP0, 0:P], start=False, stop=False, skip_group_check=True)
            valued[h] = pe.did(T.matmul(o[:, P:S], vc[:, pr], cp[:, P:S], start=False, stop=True, skip_group_check=True))
            ysplit[h] = split_out(y_hi[pr, t, :], y_lo[pr, t, :], o, valued[h])

        for n in range(8 + 2):
            if 1 <= n < 9:
                w = nsa_weights(n - 1, e)
            if n < 8:
                if n == 0:
                    dve.wait(table_in)
                e = nsa_exps(n, nsa_scores(n))
            if n not in (0, 6, 9):
                gate_slot()
            if 1 <= n < 9:
                nsa_transpose(n - 1, w)
            if n >= 2:
                nsa_values(n - 2)
        nsa_end = [pe.now(), act.now(), dve.now()]

        scored, transposed, valued, ysplit, pTs, read = {}, {}, {}, {}, {}, {}
        for e in (pe, act, dve):
            e.wait(nsa_end)

        def swa_scores(h):
            g, t = h // 2, h % 2
            pr = slice(g * HD, (g + 1) * HD)
            q, k, out = proj[pr, 6, t, :], proj[pr, 7, 0, :], bank[2]
            pe.wait(scored.get(h - 1))
            T.matmul(out[:, 0:S], q[:, P:S], k, start=True, stop=True)
            return pe.did(T.matmul(out[:, S:S + P], q[:, 0:P], k[:, 0:P], start=True, stop=True))

        def swa_exps(h, ready):
            out, lg, s4 = bank[2], logit[0][:, h % 2, :], stat[:, 0:4, 16 + 4 * (h % 2):18 + 4 * (h % 2)]
            e2 = stat[:, 0, 18 + 4 * (h % 2):20 + 4 * (h % 2)]
            sink = sm("sinks")[:, h:h + 1]
            dve.wait(ready, transposed.get(h - 2))
            dve.settle()
            dve.did(V.tensor_tensor_reduce(lg[:, 0:S], out[:, 0:S], table[:, 8 + h, :], 1.0, LOWEST,
                                           ALU.add, ALU.max, s4[:, 0, 0:1]))
            m = dve.did(V.tensor_tensor_reduce(lg[:, S:S + P], out[:, S:S + P], table[:, 8 + h, P:S], 1.0, LOWEST,
                                               ALU.add, ALU.max, s4[:, 0, 1:2]))
            scored[h] = m
            dve.wait(m)
            m = dve.did(V.tensor_scalar(s4[:, 0, :], s4[:, 0, :], 0.125, sink, ALU.mult, ALU.max))
            dve.wait(m)
            m = dve.did(V.tensor_scalar(s4[:, 1, :], s4[:, 0, :], -1.0, None, ALU.mult))
            act.wait(m)
            act.did(AC.activation(e2, s4[:, 1, :], ACT.Exp, bias=sink))
            act.did(AC.activation(lg[:, 0:S], lg[:, 0:S], ACT.Exp, bias=s4[:, 1, 0:1], scale=0.125,
                                  accum_out=s4[:, 2, 0:1]))
            return act.did(AC.activation(lg[:, S:S + P], lg[:, S:S + P], ACT.Exp, bias=s4[:, 1, 1:2], scale=0.125,
                                         accum_out=s4[:, 2, 1:2]))

        def swa_weights(h, ready):
            lg, s4 = logit[0][:, h % 2, :], stat[:, 0:4, 16 + 4 * (h % 2):18 + 4 * (h % 2)]
            e2 = stat[:, 0, 18 + 4 * (h % 2):20 + 4 * (h % 2)]
            dve.wait(ready)
            m = dve.did(V.tensor_tensor(s4[:, 3, :], s4[:, 2, :], e2, ALU.add))
            dve.wait(m)
            m = dve.did(V.reciprocal(s4[:, 3, :], s4[:, 3, :]))
            dve.wait(m)
            dve.did(V.tensor_scalar(lg[:, 0:S], lg[:, 0:S], s4[:, 3, 0:1], None, ALU.mult))
            return dve.did(V.tensor_scalar(lg[:, S:S + P], lg[:, S:S + P], s4[:, 3, 1:2], None, ALU.mult))

        def swa_transpose(h, ready):
            pe.wait(ready, pTs.get(h - 1))
            for to, frm in ((0, S), (1, 0), (2, P)):
                m = T.transpose(bank[4][:, to * P:(to + 1) * P], logit[0][:, h % 2, frm:frm + P], c("ident"))
            transposed[h] = pe.did(m)
            act.wait(transposed[h], valued.get(h - 2))
            pTs[h] = act.did(AC.activation(probT[0][:, h % 2, 0:384], bank[4][:, 0:384], ACT.Copy))

        def swa_values(h):
            g, t = h // 2, h % 2
            pr = slice(g * HD, (g + 1) * HD)
            o = bank[6][pr, 0:S]
            pe.wait(pTs[h], ysplit.get(h - 1))
            v = lambda kt: proj[:, 7, 1, kt * P + g * HD:kt * P + (g + 1) * HD]
            valued[h] = pe.did(causal_values(o, v, probT[0][:, h % 2, :]))
            ysplit[h] = split_out(y_hi[pr, 6 + t, :], y_lo[pr, 6 + t, :], o, valued[h])

        zt, spt = logit[1][:, 0, 0:384], logit[1][:, 1, 0:384]
        diagonal = (slice(0, P), slice(S, S + P))

        def sb_scores(h):
            q, k, b = proj[head_rows(h), 4, h // 2, :], proj[head_rows(h), 5, h // 2, :], bank[3]
            pe.wait(read.get(("z", h - 1)))
            T.matmul(b[:, 0:S], k[:, 0:P], q, start=True, stop=True)
            return pe.did(T.matmul(b[:, S:S + P], k[:, P:S], q[:, P:S], start=True, stop=True))

        def sb_softplus(h, ready):
            b = bank[3]
            act.wait(ready, read.get(("w", h - 1)))
            zc = act.did(AC.activation(zt, b[:, 0:384], ACT.Copy, scale=0.125))
            a = act.did(AC.activation(spt, b[:, 0:384], ACT.Abs, scale=0.125))
            read[("z", h)] = a
            act.wait(a)
            a = act.did(AC.activation(spt, spt, ACT.Exp, scale=-1.0))
            act.wait(a)
            a = act.did(AC.activation(spt, spt, ACT.Ln, bias=one))
            dve.wait(zc, a)
            m = dve.did(V.scalar_tensor_tensor(spt, zt, 0.0, spt, ALU.max, ALU.add))
            dve.wait(m)
            for cols in diagonal:
                m = dve.did(V.tensor_tensor(spt[:, cols], spt[:, cols], c("strict"), ALU.mult))
            return m

        def sb_sums(h, ready):
            ab = bank[5]
            pe.wait(ready, read.get(("a", h - 1)))
            T.matmul(ab[:, 0:S], c("tri"), spt[:, 0:S], start=True, stop=False, skip_group_check=True)
            T.matmul(ab[:, P:S], ones, spt[:, S:S + P], start=False, stop=True, skip_group_check=True)
            m = pe.did(T.matmul(ab[:, S:S + P], c("tri"), spt[:, S:S + P], start=True, stop=True, skip_group_check=True))
            dve.wait(m)
            m = dve.did(V.tensor_tensor(zt, zt, ab[:, 0:384], ALU.subtract))
            read[("a", h)] = m
            dve.wait(m)
            for cols in diagonal:
                m = dve.did(V.tensor_tensor(zt[:, cols], zt[:, cols], c("strict_add"), ALU.add))
            act.wait(m, read.get(("v", h - 2)))
            read[("w", h)] = act.did(AC.activation(probT[1][:, h % 2, 0:384], zt, ACT.Exp))

        def sb_values(h):
            o = bank[7]
            pe.wait(read[("w", h)], read.get(("y", h // 2 - 1)))
            v = lambda kt: proj[:, 9, kt, h * HD:(h + 1) * HD]
            read[("v", h)] = pe.did(causal_values(o[head_rows(h), 0:S], v, probT[1][:, h % 2, :]))
            if h % 2:
                read[("y", h // 2)] = split_out(y_hi[:, 4 + h // 2, :], y_lo[:, 4 + h // 2, :], o[:, 0:S], read[("v", h)])

        for n in range(4 + 2):
            if 1 <= n < 5:
                w = swa_weights(n - 1, e)
            if n < 4:
                zs = sb_scores(n)
                e = swa_exps(n, swa_scores(n))
                sp = sb_softplus(n, zs)
            if n < 5:
                gate_slot()
            if 1 <= n < 5:
                sb_values(n - 1)
                swa_transpose(n - 1, w)
            if n < 4:
                sb_sums(n, sp)
            if n >= 2:
                swa_values(n - 2)
        read_gate_slot()
        swa_scored = scored[3]
        sb_done = [ysplit[3], read[("y", 1)]]

        pe.wait(free[0], free[1], swa_scored, nsa_end)
        for e in (act, dve):
            e.wait(pe.now(), act.now(), dve.now())
        up_banks = [[dense[0], dense[1], acc[0]], acc[1:4]]
        with L.run(2) as loop:
            for half in range(2):
                b = loop.i * 4 + half * 2
                pe.wait(loop.last(f"up read{half}", dve.counter))
                for part, r in halves():
                    if part == 1:
                        pe.wait(sb_done)
                    for k in range(HK):
                        n = 0 if part == 0 else 1 + k // 2
                        for ct in range(2):
                            mm = products(up_banks[half][n][:, ct, :], tile(r, k, slice(ct * P, (ct + 1) * P)),
                                          [t[:, part * HK + k, :] for t in (y_hi, y_lo)],
                                          k == (0, 0, 2)[n] and ct == 0)
                    got = used.did(mm)
                act.wait(gates_read if half else loop.last("gates_read1", dve.counter))
                g3 = [act_t, root, rinv]
                for n in range(3):
                    sg = act.did(AC.activation(g3[n], gates[:, bass.ds(b + 8 * n, 2), :], ACT.Sigmoid))
                dve.wait(got, sg, low if half else loop.last("merged1", dve.counter))
                t3 = [sq[:, 2 * n:2 * n + 2, :] for n in range(3)]
                for n in range(3):
                    m = dve.did(V.tensor_tensor(t3[n], up_banks[half][n], g3[n], ALU.mult))
                gates_read = m
                dve.wait(m)
                m = dve.did(V.tensor_tensor(t3[0], t3[0], t3[1], ALU.add))
                dve.wait(m)
                m = dve.did(V.tensor_tensor(t3[0], t3[0], t3[2], ALU.add))
                act.wait(m)
                hh = act.did(AC.activation(xn_hi[:, bass.ds(b, 2), :], t3[0], ACT.Copy))
                dve.wait(hh)
                low = dve.did(V.tensor_tensor(xn_lo[:, bass.ds(b, 2), :], t3[0],
                                              xn_hi[:, bass.ds(b, 2), :].bitcast(F32), ALU.subtract))
                loop.keep(f"up read{half}", gates_read)
                loop.keep(f"merged{half}", low)
                if half:
                    loop.keep("gates_read1", gates_read)
        got = out_projection(xn_hi, xn_lo, loop.ended("merged0"), loop.ended("up read0"), loop.ended("merged1"))

        def add(b):
            dve.wait(got[b])
            return dve.did(V.tensor_tensor(x[:, pair_of(b), :], x[:, pair_of(b), :], acc[b], ALU.add))

        pool.wait(got)
        fetch_small(l + (DEPTH + 1))
        update = half_ffn(sm("ffn2"), add, True, got[3])
        for b in range(4):
            update(b)

    pool.wait(dve.now())
    stored = Counter(L, "stored", 16)
    out_done = stored.did(G.dma_start(A["out"], x))
    pool.wait(out_done)
    return L


def constants():
    out = np.zeros((P, CON_W), np.float32)
    i, j = np.arange(P)[:, None], np.arange(P)[None, :]
    out[:, CON["ident"]] = i == j
    out[:, CON["blk"]] = (i // HD == j // HD) / HD
    out[:, CON["tri"]] = i >= j
    rot = np.zeros((P, P), np.float32)
    for p in range(P):
        if p % HD < HD // 2:
            rot[p + HD // 2, p] = -1
        else:
            rot[p - HD // 2, p] = 1
    out[:, CON["rot"]] = rot
    out[:, CON["causal"]] = np.where(P + i - np.arange(S)[None, :] >= 0, 0, BIG)
    out[:, CON["strict"]] = i < j
    out[:, CON["strict_add"]] = np.where(i < j, 0, BIG)
    gamma = 1 - 2.0 ** (-5.0 - np.arange(4))
    diff = j - i
    for h in range(4):
        diag = np.where(diff >= 0, gamma[h] ** np.maximum(diff, 0), 0)
        out[:, CON["decay"]][:, h * S:(h + 1) * S] = np.concatenate([diag, gamma[h] ** (P + diff)], 1) * HD ** -0.5
    half = HD // 2
    out[:, CON["inv_freq"]] = (np.float32(10000.0) ** (-(np.arange(P) % half).astype(np.float32) / half))[:, None]
    out[:, CON["late"]] = (np.arange(P) >= 31)[:, None]
    early = np.zeros((34, EARLY_W), np.float32)
    for h in range(8):
        early[h, EARLY["nsel"].start + h * P:EARLY["nsel"].start + (h + 1) * P] = -1
    dist = S - 1 - np.arange(VEC)
    big = 16 + (np.log(np.maximum(dist, 1).astype(np.float32) / 16) / np.float32(np.log(8)) * 16).astype(np.int32)
    bucket = np.where(np.maximum(dist, 0) < 16, np.maximum(dist, 0), np.minimum(big, 31))
    onehot = early[:, EARLY["onehot"]]
    onehot[bucket, np.arange(VEC)] = 1
    onehot[32] = dist < 0
    onehot[33] = dist >= P
    return out, early


def lay_out(a):
    def feature_major(t):
        return np.ascontiguousarray(t.reshape(S, KT, P).transpose(2, 1, 0)).reshape(P, KT * S)

    def cols(v):
        return v.reshape(-1, P).T

    def pair(w):
        return w.reshape(-1, P, w.shape[1]).transpose(1, 0, 2).reshape(P, -1)

    stream = np.zeros((2 * (N_SLOTS + 1), P, SLOT // 2), np.float32)
    at = [0]

    def put(block):
        for half in range(2):
            stream[at[0]] = block[:, half * SLOT // 2:(half + 1) * SLOT // 2]
            at[0] += 1

    def dense(w):
        for c in range(0, w.shape[1], COLS):
            put(pair(w[:, c:c + COLS]))

    def ffn(gate, up, down):
        for c in range(0, FF, COLS):
            put(pair(gate[:, c:c + COLS]))
            put(pair(up[:, c:c + COLS]))
        for j in range(FT // 2):
            put(pair(down[2 * j * P:2 * (j + 1) * P]))

    small = np.zeros((2 * DEPTH + 1, P, SM_W), np.float32)
    for l in range(DEPTH):
        w = a["w_in"][l]
        lx, ly, fq, fk, fv, ff, rq, rk, rv, rg = np.split(w, np.cumsum(
            [256, 256, 512, 512, 512, 8, 256, 256, 256, 256])[:-1], axis=1)
        for part in (fq, fk, rq, rk, rg, lx, ly):
            dense(part)
        f = np.zeros((D, COLS), np.float32)
        f[:, 0:8] = ff
        put(pair(f))
        dense(fv)
        dense(rv)
        for name in ("w_ck", "w_cv", "w_out", "w_cq", "w_co"):
            dense(a[name][l])
        ffn(a["w_gate"][l], a["w_up"][l], a["w_down"][l])
        s = small[l]
        for name in ("pre_mix", "post_mix", "pre_cross", "post_cross", "pre_ffn", "post_ffn"):
            s[:, SM1[name]] = cols(a[name + "_g"][l])
        s[:, SM1["conv_w"]] = np.concatenate([cols(a["conv_w"][l, n]) for n in range(4)], 1)
        for name, src in (("conv_b", "conv_b"), ("b_rg", "b_rg"), ("b_ig", "b_ig"), ("lam", "lru_lambda")):
            s[:, SM1[name]] = cols(a[src][l])
        s[0:8, SM1["fox_b"]] = a["fox_b_f"][l][:, None]
        for name in ("w_rg", "w_ig"):
            for n in range(4):
                r, o = (n % 2) * HD, SM1[name].start + n * HD
                s[r:r + HD, o:o + HD] = a[name][l, n]
    for l in range(DEPTH):
        ffn(a["ffn1_w_gate_2"][l], a["ffn1_w_up_2"][l], a["ffn1_w_down_2"][l])
        w = a["w_in_2"][l]
        (nq, nkc, nvc, nks, nvs, nkw, nvw, ngate, sq, sk, sv, wq, wk, wv, bgate) = np.split(w, np.cumsum(
            [512, 128, 128, 128, 128, 128, 128, 24, 256, 256, 256, 256, 128, 128, 3072])[:-1], axis=1)
        by_group8 = np.concatenate([np.arange(h * HD, (h + 1) * HD) for t in range(4) for h in (t, t + 4)])
        by_group4 = np.concatenate([np.arange(h * HD, (h + 1) * HD) for t in range(2) for h in (t, t + 2)])
        dense(nq[:, by_group8])
        dense(np.concatenate([nks, nkw], 1))
        dense(np.concatenate([nkc, nvc], 1))
        dense(sq)
        dense(sk)
        w1 = {(n, part): a["nsa_cmp_%s_w1_2" % n][l][part * D:(part + 1) * D] for n in "kv" for part in range(2)}
        dense(w1["k", 0])
        dense(wq[:, by_group4])
        dense(w1["k", 1])
        dense(np.concatenate([wk, wv], 1))
        dense(w1["v", 0])
        dense(np.concatenate([nvs, nvw], 1))
        dense(w1["v", 1])
        dense(sv)
        dense(bgate)
        up = np.concatenate([a["w_up_nsa_2"][l][by_group8], a["w_up_sb_2"][l], a["w_up_swa_2"][l][by_group4]], 0)
        dense(up)
        dense(a["w_out_2"][l])
        ffn(a["ffn2_w_gate_2"][l], a["ffn2_w_up_2"][l], a["ffn2_w_down_2"][l])
        s = small[DEPTH + l]
        for name, src in (("ffn1", "ffn1_norm_2"), ("mix", "mix_norm_2"), ("ffn2", "ffn2_norm_2")):
            s[:, SM2[name]] = cols(a[src][l])
        for name, src in (("nsa_q", "nsa_q_norm_2"), ("nsa_k", "nsa_k_norm_2"), ("swa_q", "swa_q_norm_2"),
                          ("swa_k", "swa_k_norm_2")):
            s[:, SM2[name]] = np.concatenate([a[src][l]] * 2)[:, None]
        s[:, SM2["sinks"]] = a["swa_sinks_2"][l][None, :]
        s[:, SM2["cmp_pos"]] = a["nsa_cmp_pos_2"][l].reshape(16, P).T
        for name, src in (("w2k", "nsa_cmp_k_w2_2"), ("w2v", "nsa_cmp_v_w2_2")):
            s[:, SM2[name]] = pair(a[src][l])
        s[:, SM2["w_gate"]] = pair(ngate)
    assert at[0] == 2 * N_SLOTS

    con, early = constants()
    con[:, CON["mem_g"]] = cols(a["mem_norm_g"])
    bias = np.zeros((34, 12), np.float32)
    bias[0:32] = a["rel_bias_2"]
    bias[32] = BIG / 8
    bias[33, 8:] = BIG / 8
    return {
        "stream": stream, "x": feature_major(a["x"]), "mem": feature_major(a["mem"]),
        "positions": np.ascontiguousarray(np.broadcast_to(a["positions"].reshape(1, S), (P, S))),
        "rel_bias": bias, "con": con, "early": early, "small": small,
    }


def program(nc, arrays, known, final):
    A = {n: nc.dram_tensor("in_" + n, a.shape, mybir.dt.from_np(a.dtype), kind="ExternalInput").ap()
         for n, a in arrays.items()}
    for n in ("x", "mem"):
        A[n] = A[n].rearrange("p (k s) -> p k s", k=KT)
    A["out"] = nc.dram_tensor("out", (P, KT, S), F32, kind="ExternalOutput").ap()
    A["skew"] = nc.dram_tensor("skew", (P * 12 * VEC,), F32, kind="Internal").ap()
    build(nc, A, known, final)


def kernel(**inputs):
    import concourse.bacc as bacc
    from concourse.bass_utils import run_bass_kernel_spmd

    arrays = lay_out({n: np.asarray(v) for n, v in inputs.items()})
    known = {}
    for final in (False, True):
        nc = bacc.Bacc("TRN2", target_bir_lowering=False, num_devices=1)
        program(nc, arrays, known, final)
    r = run_bass_kernel_spmd(nc, [{"in_" + n: v for n, v in arrays.items()}], core_ids=[0])
    out = r.results[0]["out"].reshape(P, KT, S)
    return np.ascontiguousarray(out.transpose(2, 1, 0)).reshape(1, S, D)
```
